# Optimizing a Trainium2 kernel written in Bass

```python
import math
import jax, jax.numpy as jnp
from jax import lax
import numpy as np

D_MODEL = 1024
BATCH = 1
SEQ = 256
DEPTH = 2

CHUNK = 64
Q_BLOCK = 128
LN_EPS = 1e-5
SB_HEADS = 8
SB_HEAD_DIM = 64
SB_WIDTH = SB_HEADS * SB_HEAD_DIM
RET_HEADS = 4
RET_HEAD_DIM = 128
RET_WIDTH = RET_HEADS * RET_HEAD_DIM
EVEN_IN = 3 * SB_WIDTH + 4 * RET_WIDTH
EVEN_MIX = SB_WIDTH + RET_WIDTH
DIFF_HEADS = 8
DIFF_HEAD_DIM = 64
DIFF_V_DIM = 2 * DIFF_HEAD_DIM
DIFF_QK = DIFF_HEADS * 2 * DIFF_HEAD_DIM
DIFF_VW = DIFF_HEADS * DIFF_V_DIM
ODD_IN = 2 * DIFF_QK + DIFF_VW
N_GROUPS = 4
EXPERTS_PER_GROUP = 8
N_EXPERTS = N_GROUPS * EXPERTS_PER_GROUP
TOP_K = 2
EXPERT_FF = 512
MOE_BLOCK = 128
N_EVEN = (DEPTH + 1) // 2
N_ODD = DEPTH // 2


def layer_norm(x, g, b):
    xf = x.astype(jnp.float32)
    mu = jnp.mean(xf, axis=-1, keepdims=True)
    var = jnp.mean(jnp.square(xf - mu), axis=-1, keepdims=True)
    y = (xf - mu) * lax.rsqrt(var + LN_EPS) * g.astype(jnp.float32) + b.astype(jnp.float32)
    return y.astype(x.dtype)

def split_cols(a, sizes):
    out = []
    o = 0
    for s in sizes:
        out.append(a[..., o:o + s])
        o += s
    return out

def stick_breaking_attention(q, k, v):
    B, S, H, dh = q.shape
    nb = S // Q_BLOCK
    kh = k.transpose(0, 2, 1, 3)
    vh = v.transpose(0, 2, 1, 3)
    q_blocks = jnp.moveaxis(q.transpose(0, 2, 1, 3).reshape(B, H, nb, Q_BLOCK, dh), 2, 0)
    key_pos = jnp.arange(S)
    scale = dh ** -0.5

    def block(args):
        qb, start = args
        z = jnp.einsum('bhqd,bhkd->bhqk', qb, kh, preferred_element_type=jnp.float32) * scale
        q_pos = start + jnp.arange(Q_BLOCK)
        mask = key_pos[None, :] < q_pos[:, None]
        log_1m_beta = jnp.where(mask, jax.nn.log_sigmoid(-z), 0.0)
        between = lax.cumsum(log_1m_beta, axis=3, reverse=True) - log_1m_beta
        w = jnp.where(mask, jnp.exp(jax.nn.log_sigmoid(z) + between), 0.0)
        return jnp.einsum('bhqk,bhkd->bhqd', w.astype(vh.dtype), vh)

    out = lax.map(block, (q_blocks, jnp.arange(nb) * Q_BLOCK))
    return jnp.moveaxis(out, 0, 2).reshape(B, H, S, dh).transpose(0, 2, 1, 3).reshape(B, S, H * dh)

def retention(q, k, v, g, gn_gain):
    B, S, H, d = q.shape
    nc = S // CHUNK
    f32 = jnp.float32

    def chunked(t):
        return t.astype(f32).transpose(0, 2, 1, 3).reshape(B, H, nc, CHUNK, d)

    qc = chunked(q)
    kc = chunked(k) * (d ** -0.5)
    vc = chunked(v)
    log_gamma = jnp.log1p(-jnp.exp2(-5.0 - jnp.arange(H, dtype=f32)))
    pos = jnp.arange(CHUNK, dtype=f32)
    intra_decay = jnp.exp(log_gamma[:, None, None] * jnp.abs(pos[:, None] - pos[None, :]))
    scores = jnp.einsum('bhncd,bhnsd->bhncs', qc, kc) * intra_decay[None, :, None]
    intra = jnp.einsum('bhncs,bhnse->bhnce', scores, vc)
    k_decay = jnp.exp(log_gamma[:, None] * (CHUNK - 1 - pos)[None, :])
    q_decay = jnp.exp(log_gamma[:, None] * (pos + 1.0)[None, :])
    chunk_kv = jnp.einsum('bhnsd,bhnse->nbhde', kc * k_decay[None, :, None, :, None], vc)
    chunk_decay = jnp.exp(log_gamma * CHUNK)[None, :, None, None]

    def step(state, kv):
        return chunk_decay * state + kv, state

    _, prev_state = lax.scan(step, jnp.zeros((B, H, d, d), f32), chunk_kv)
    inter = jnp.einsum('bhncd,nbhde->bhnce', qc * q_decay[None, :, None, :, None], prev_state)
    o = (intra + inter).reshape(B, H, S, d)
    mu = jnp.mean(o, axis=-1, keepdims=True)
    var = jnp.mean(jnp.square(o - mu), axis=-1, keepdims=True)
    o = ((o - mu) * lax.rsqrt(var + LN_EPS)).transpose(0, 2, 1, 3).reshape(B, S, H * d)
    o = o * gn_gain.astype(f32) * jax.nn.silu(g.astype(f32).reshape(B, S, H * d))
    return o.astype(q.dtype)

def differential_attention(q, k, v, lam, lambda_init, subln_gain):
    B, S, H, _, dh = q.shape
    dv = v.shape[-1]
    nb = S // Q_BLOCK
    f32 = jnp.float32
    kh = k.transpose(0, 2, 3, 1, 4)
    vh = v.transpose(0, 2, 1, 3)
    q_blocks = jnp.moveaxis(q.transpose(0, 2, 3, 1, 4).reshape(B, H, 2, nb, Q_BLOCK, dh), 3, 0)
    slopes = jnp.exp2(-8.0 / H * (jnp.arange(H, dtype=f32) + 1.0))
    key_pos = jnp.arange(S)
    key_chunk = key_pos // CHUNK
    scale = dh ** -0.5

    def block(args):
        qb, start = args
        z = jnp.einsum('bhmqd,bhmkd->bhmqk', qb, kh, preferred_element_type=f32) * scale
        q_pos = start + jnp.arange(Q_BLOCK)
        dist = jnp.abs(q_pos[:, None] - key_pos[None, :]).astype(f32)
        z = z - slopes[:, None, None, None] * dist
        mask = key_chunk[None, :] <= (q_pos // CHUNK)[:, None]
        p = jax.nn.softmax(jnp.where(mask, z, -jnp.inf), axis=-1)
        a = p[:, :, 0] - lam * p[:, :, 1]
        return jnp.einsum('bhqk,bhkd->bhqd', a.astype(vh.dtype), vh)

    out = lax.map(block, (q_blocks, jnp.arange(nb) * Q_BLOCK))
    o = jnp.moveaxis(out, 0, 2).reshape(B, H, S, dv).astype(f32)
    o = o * lax.rsqrt(jnp.mean(jnp.square(o), axis=-1, keepdims=True) + LN_EPS)
    o = o * subln_gain.astype(f32) * (1.0 - lambda_init)
    return o.transpose(0, 2, 1, 3).reshape(B, S, H * dv).astype(v.dtype)

def hierarchical_moe(h, w_group, b_group, w_router, b_router, w1, w3, w2):
    B, S, D = h.shape
    T = B * S
    f32 = jnp.float32
    xt = h.reshape(T, D)
    group_logits = (xt @ w_group).astype(f32) + b_group.astype(f32)
    grp = jnp.argmax(group_logits, axis=-1)
    p_grp = jnp.take_along_axis(jax.nn.softmax(group_logits, axis=-1), grp[:, None], axis=1)[:, 0]
    expert_logits = ((xt @ w_router).astype(f32) + b_router.astype(f32)).reshape(T, N_GROUPS, EXPERTS_PER_GROUP)
    in_group = jnp.take_along_axis(expert_logits, grp[:, None, None], axis=1)[:, 0]
    top_vals, top_idx = lax.top_k(in_group, TOP_K)
    gates = jax.nn.softmax(top_vals, axis=-1) * p_grp[:, None]
    expert_id = (grp[:, None] * EXPERTS_PER_GROUP + top_idx).astype(jnp.int32)
    M = T * TOP_K
    flat_e = expert_id.reshape(M)
    flat_tok = jnp.arange(M, dtype=jnp.int32) // TOP_K
    order = jnp.argsort(flat_e)
    e_sorted = flat_e[order]
    tok_sorted = flat_tok[order]
    gate_sorted = gates.reshape(M)[order]
    counts = jnp.zeros((N_EXPERTS,), jnp.int32).at[flat_e].add(1)
    padded = (counts + MOE_BLOCK - 1) // MOE_BLOCK * MOE_BLOCK
    pad_end = jnp.cumsum(padded)
    pad_start = pad_end - padded
    start = jnp.cumsum(counts) - counts
    dest = pad_start[e_sorted] + jnp.arange(M, dtype=jnp.int32) - start[e_sorted]
    P = M + N_EXPERTS * MOE_BLOCK
    n_blk = P // MOE_BLOCK
    slot_tok = jnp.full((P,), T, jnp.int32).at[dest].set(tok_sorted)
    x_pad = jnp.concatenate([xt, jnp.zeros((1, D), xt.dtype)], axis=0)
    x_slots = x_pad[slot_tok].reshape(n_blk, MOE_BLOCK, D)
    blk_expert = jnp.minimum(
        jnp.searchsorted(pad_end, jnp.arange(n_blk, dtype=jnp.int32) * MOE_BLOCK, side='right'),
        N_EXPERTS - 1)

    def expert_block(args):
        xb, e = args
        return (jax.nn.silu(xb @ w1[e]) * (xb @ w3[e])) @ w2[e]

    y_slots = lax.map(expert_block, (x_slots, blk_expert)).reshape(P, D)
    y = y_slots[dest] * gate_sorted[:, None].astype(y_slots.dtype)
    return jax.ops.segment_sum(y, tok_sorted, num_segments=T).reshape(B, S, D)

def first_inputs(seed: int = 0) -> dict:
    key = jax.random.key(seed)
    ks = jax.random.split(key, 26)
    D = D_MODEL
    beta = (8.0 * DEPTH) ** -0.25
    nrm = lambda k, shape, s: jax.random.normal(k, shape, jnp.float32) * s
    return {
        'x': nrm(ks[0], (BATCH, SEQ, D), 1.0),
        'c': nrm(ks[1], (BATCH, D), 1.0),
        'ln1_g': 1.0 + nrm(ks[2], (DEPTH, D), 0.02),
        'ln1_b': nrm(ks[3], (DEPTH, D), 0.02),
        'ln2_g': 1.0 + nrm(ks[4], (DEPTH, D), 0.02),
        'ln2_b': nrm(ks[5], (DEPTH, D), 0.02),
        'w_ada': nrm(ks[6], (DEPTH, D, 6 * D), 0.1 * D ** -0.5),
        'b_ada': nrm(ks[7], (DEPTH, 6 * D), 0.01),
        'even_w_in': nrm(ks[8], (N_EVEN, D, EVEN_IN), D ** -0.5),
        'even_w_out': nrm(ks[9], (N_EVEN, EVEN_MIX, D), beta * EVEN_MIX ** -0.5),
        'ret_gn_g': 1.0 + nrm(ks[10], (N_EVEN, RET_WIDTH), 0.02),
        'odd_w_in': nrm(ks[11], (N_ODD, D, ODD_IN), D ** -0.5),
        'odd_w_out': nrm(ks[12], (N_ODD, DIFF_VW, D), beta * DIFF_VW ** -0.5),
        'lambda_q1': nrm(ks[13], (N_ODD, DIFF_HEAD_DIM), 0.1),
        'lambda_k1': nrm(ks[14], (N_ODD, DIFF_HEAD_DIM), 0.1),
        'lambda_q2': nrm(ks[15], (N_ODD, DIFF_HEAD_DIM), 0.1),
        'lambda_k2': nrm(ks[16], (N_ODD, DIFF_HEAD_DIM), 0.1),
        'diff_subln_g': 1.0 + nrm(ks[17], (N_ODD, DIFF_V_DIM), 0.02),
        'moe_w_group': nrm(ks[18], (DEPTH, D, N_GROUPS), D ** -0.5),
        'moe_b_group': nrm(ks[19], (DEPTH, N_GROUPS), 0.01),
        'moe_w_router': nrm(ks[20], (DEPTH, D, N_EXPERTS), D ** -0.5),
        'moe_b_router': nrm(ks[21], (DEPTH, N_EXPERTS), 0.01),
        'moe_w1': nrm(ks[22], (DEPTH, N_EXPERTS, D, EXPERT_FF), D ** -0.5),
        'moe_w3': nrm(ks[23], (DEPTH, N_EXPERTS, D, EXPERT_FF), D ** -0.5),
        'moe_w2': nrm(ks[24], (DEPTH, N_EXPERTS, EXPERT_FF, D), beta * EXPERT_FF ** -0.5),
    }

def first_block(x, c, ln1_g, ln1_b, ln2_g, ln2_b, w_ada, b_ada,
              even_w_in, even_w_out, ret_gn_g,
              odd_w_in, odd_w_out, lambda_q1, lambda_k1, lambda_q2, lambda_k2, diff_subln_g,
              moe_w_group, moe_b_group, moe_w_router, moe_b_router, moe_w1, moe_w3, moe_w2):
    B, S, D = x.shape
    alpha = (2.0 * DEPTH) ** 0.25
    cond = jax.nn.silu(c)
    for l in range(DEPTH):
        mod = (cond @ w_ada[l] + b_ada[l])[:, None, :]
        sh1, sc1, g1, sh2, sc2, g2 = jnp.split(mod, 6, axis=-1)
        u = x * (1.0 + sc1) + sh1
        i = l // 2
        if l % 2 == 0:
            proj = u @ even_w_in[i]
            sq, sk, sv, rq, rk, rv, rg = split_cols(proj, [SB_WIDTH] * 3 + [RET_WIDTH] * 4)
            sb_shape = (B, S, SB_HEADS, SB_HEAD_DIM)
            ret_shape = (B, S, RET_HEADS, RET_HEAD_DIM)
            a_out = stick_breaking_attention(sq.reshape(sb_shape), sk.reshape(sb_shape), sv.reshape(sb_shape))
            b_out = retention(rq.reshape(ret_shape), rk.reshape(ret_shape), rv.reshape(ret_shape),
                              rg.reshape(ret_shape), ret_gn_g[i])
            mix = jnp.concatenate([a_out, b_out], axis=-1) @ even_w_out[i]
        else:
            proj = u @ odd_w_in[i]
            dq, dk, dv = split_cols(proj, [DIFF_QK, DIFF_QK, DIFF_VW])
            lambda_init = 0.8 - 0.6 * math.exp(-0.3 * l)
            lam = (jnp.exp(jnp.sum(lambda_q1[i].astype(jnp.float32) * lambda_k1[i].astype(jnp.float32)))
                   - jnp.exp(jnp.sum(lambda_q2[i].astype(jnp.float32) * lambda_k2[i].astype(jnp.float32)))
                   + lambda_init)
            c_out = differential_attention(dq.reshape(B, S, DIFF_HEADS, 2, DIFF_HEAD_DIM),
                                           dk.reshape(B, S, DIFF_HEADS, 2, DIFF_HEAD_DIM),
                                           dv.reshape(B, S, DIFF_HEADS, DIFF_V_DIM),
                                           lam, lambda_init, diff_subln_g[i])
            mix = c_out @ odd_w_out[i]
        x = layer_norm(alpha * x + (1.0 + g1) * mix, ln1_g[l], ln1_b[l])
        u = x * (1.0 + sc2) + sh2
        f = hierarchical_moe(u, moe_w_group[l], moe_b_group[l], moe_w_router[l], moe_b_router[l],
                             moe_w1[l], moe_w3[l], moe_w2[l])
        x = layer_norm(alpha * x + (1.0 + g2) * f, ln2_g[l], ln2_b[l])
    return x


GRID_W = 64
CTX_LEN = 256
N_MIXERS = 4
EPS = 1e-6
ROPE_THETA = 10000.0
NEG_INF = -1e30
HEAD_DIM = 64
D_FF = -(-(8 * D_MODEL) // (3 * 256)) * 256
SWA_HEADS = D_MODEL // HEAD_DIM
SWA_KV_HEADS = 4
SWA_WINDOW = 128
NA_HEADS = D_MODEL // HEAD_DIM
NA_KH = 8
NA_KW = 16
NA_QCB = 16
NA_SLAB = 2 * NA_KW
POOL_WINDOWS = (2, 4, 8, 16)
POOL_GROUPS = len(POOL_WINDOWS)
POOL_DG = D_MODEL // POOL_GROUPS
MLA_HEADS = 16
MLA_NOPE = 64
MLA_ROPE = 32
MLA_V = 64
MLA_Q_RANK = 256
MLA_KV_RANK = 128


def n_layers_of(m):
    return len(range(m, DEPTH, N_MIXERS))

def rms_norm(x, g):
    xf = x.astype(jnp.float32)
    y = xf * lax.rsqrt(jnp.mean(xf * xf, axis=-1, keepdims=True) + EPS)
    return (y * g.astype(jnp.float32)).astype(x.dtype)

def modulate(x, g, shift, scale):
    return rms_norm(x, g) * (1 + scale) + shift

def rope_1d(x, pos):
    half = x.shape[-1] // 2
    freqs = ROPE_THETA ** (-jnp.arange(half, dtype=jnp.float32) / half)
    ang = pos.astype(jnp.float32)[:, None] * freqs[None, :]
    cos = jnp.cos(ang)[:, None, :]
    sin = jnp.sin(ang)[:, None, :]
    xf = x.astype(jnp.float32)
    x1, x2 = xf[..., :half], xf[..., half:]
    return jnp.concatenate([x1 * cos - x2 * sin, x1 * sin + x2 * cos], -1).astype(x.dtype)

def rope_2d_axial(x, length):
    t = jnp.arange(length)
    d = x.shape[-1] // 2
    return jnp.concatenate([rope_1d(x[..., :d], t // GRID_W), rope_1d(x[..., d:], t % GRID_W)], -1)

def softmax_f32(s, sink=None):
    if sink is None:
        return jax.nn.softmax(s, axis=-1)
    sink = jnp.broadcast_to(sink, s.shape[:-1] + (1,))
    return jax.nn.softmax(jnp.concatenate([s, sink], -1), axis=-1)[..., :-1]

def swiglu(h, w_gu, w_down):
    gu = h @ w_gu
    return (jax.nn.silu(gu[..., :D_FF]) * gu[..., D_FF:]) @ w_down

def swa_mixer(a_lat, a_ctx, w_qkv, g_q, g_k, sink, w_o, need_ctx):
    B, L, _ = a_lat.shape
    Lc = a_ctx.shape[1]
    Hq, Hk, dh = SWA_HEADS, SWA_KV_HEADS, HEAD_DIM
    G = Hq // Hk
    nq, nk = Hq * dh, Hk * dh
    scale = dh ** -0.5
    qkv = a_lat @ w_qkv
    q = rope_2d_axial(rms_norm(qkv[..., :nq].reshape(B, L, Hq, dh), g_q), L)
    k = rope_2d_axial(rms_norm(qkv[..., nq:nq + nk].reshape(B, L, Hk, dh), g_k), L)
    v = qkv[..., nq + nk:].reshape(B, L, Hk, dh)
    kv_c = a_ctx @ w_qkv[:, nq:]
    k_c = rms_norm(kv_c[..., :nk].reshape(B, Lc, Hk, dh), g_k)
    v_c = kv_c[..., nk:].reshape(B, Lc, Hk, dh)
    sink_g = sink.astype(jnp.float32).reshape(Hk, G)[None, :, :, None, None]
    nb = L // Q_BLOCK
    span = Q_BLOCK + 2 * SWA_WINDOW
    pad = ((0, 0), (SWA_WINDOW, SWA_WINDOW), (0, 0), (0, 0))
    k_p = jnp.pad(k, pad)
    v_p = jnp.pad(v, pad)
    q_blocks = jnp.moveaxis(q.reshape(B, nb, Q_BLOCK, Hk, G, dh), 1, 0)
    ctx_valid = jnp.ones((Q_BLOCK, Lc), bool)

    def block(args):
        b, q_b = args
        start = b * Q_BLOCK
        k_b = jnp.concatenate([lax.dynamic_slice_in_dim(k_p, start, span, 1), k_c], 1)
        v_b = jnp.concatenate([lax.dynamic_slice_in_dim(v_p, start, span, 1), v_c], 1)
        q_pos = start + jnp.arange(Q_BLOCK)
        k_pos = start - SWA_WINDOW + jnp.arange(span)
        valid = (jnp.abs(q_pos[:, None] - k_pos[None, :]) <= SWA_WINDOW) & (k_pos >= 0) & (k_pos < L)
        valid = jnp.concatenate([valid, ctx_valid], 1)
        s = jnp.einsum('bqhgd,bkhd->bhgqk', q_b, k_b, preferred_element_type=jnp.float32) * scale
        p = softmax_f32(jnp.where(valid, s, NEG_INF), sink_g).astype(v_b.dtype)
        return jnp.einsum('bhgqk,bkhd->bqhgd', p, v_b)

    o = lax.map(block, (jnp.arange(nb), q_blocks))
    y_lat = jnp.moveaxis(o, 0, 1).reshape(B, L, nq) @ w_o
    y_ctx = None
    if need_ctx:
        q_c = rms_norm((a_ctx @ w_qkv[:, :nq]).reshape(B, Lc, Hk, G, dh), g_q)
        s = jnp.einsum('bqhgd,bkhd->bhgqk', q_c, k_c, preferred_element_type=jnp.float32) * scale
        p = softmax_f32(s, sink_g).astype(v_c.dtype)
        y_ctx = jnp.einsum('bhgqk,bkhd->bqhgd', p, v_c).reshape(B, Lc, nq) @ w_o
    return y_lat, y_ctx

def na_mixer(a_lat, a_ctx, w_qkv, g_q, g_k, rpb, w_o, need_ctx):
    B, L, _ = a_lat.shape
    Lc = a_ctx.shape[1]
    H, dh = NA_HEADS, HEAD_DIM
    n = H * dh
    scale = dh ** -0.5
    rows = L // GRID_W
    kh = min(NA_KH, rows)
    qkv = a_lat @ w_qkv
    q = rms_norm(qkv[..., :n].reshape(B, rows, GRID_W, H, dh), g_q)
    k = rms_norm(qkv[..., n:2 * n].reshape(B, rows, GRID_W, H, dh), g_k)
    v = qkv[..., 2 * n:].reshape(B, rows, GRID_W, H, dh)
    kv_c = a_ctx @ w_qkv[:, n:]
    k_c = rms_norm(kv_c[..., :n].reshape(B, Lc, H, dh), g_k)
    v_c = kv_c[..., n:].reshape(B, Lc, H, dh)
    ncb = GRID_W // NA_QCB
    q_col = np.arange(GRID_W).reshape(ncb, NA_QCB)
    slab0 = [int(s) for s in np.clip(np.arange(ncb) * NA_QCB - NA_KW // 2, 0, GRID_W - NA_SLAB)]
    col_start = np.clip(q_col - NA_KW // 2, 0, GRID_W - NA_KW)
    key_col = np.asarray(slab0)[:, None] + np.arange(NA_SLAB)
    kc3 = key_col[:, None, :]
    col_valid = (kc3 >= col_start[..., None]) & (kc3 < col_start[..., None] + NA_KW)
    dc_idx = (np.clip(kc3 - q_col[..., None], -(NA_KW - 1), NA_KW - 1) + NA_KW - 1)[:, :, None, :]
    nkey = kh * NA_SLAB
    valid_lat = np.broadcast_to(col_valid[:, :, None, :], (ncb, NA_QCB, kh, NA_SLAB)).reshape(ncb, NA_QCB, nkey)
    valid = jnp.asarray(np.concatenate([valid_lat, np.ones((ncb, NA_QCB, Lc), bool)], -1))
    rpb_f = rpb.astype(jnp.float32)

    def slabs(t):
        return jnp.stack([t[:, :, s:s + NA_SLAB] for s in slab0], 1).reshape(B, ncb, nkey, H, dh)

    def row_step(args):
        r, q_r = args
        r0 = jnp.clip(r - kh // 2, 0, rows - kh)
        k_s = slabs(lax.dynamic_slice_in_dim(k, r0, kh, 1))
        v_s = slabs(lax.dynamic_slice_in_dim(v, r0, kh, 1))
        dr_idx = (r0 + jnp.arange(kh) - r + NA_KH - 1)[None, None, :, None]
        bias = rpb_f[:, dr_idx, dc_idx].reshape(H, ncb, NA_QCB, nkey)
        q_b = q_r.reshape(B, ncb, NA_QCB, H, dh)
        s_lat = jnp.einsum('bjqhd,bjkhd->bhjqk', q_b, k_s, preferred_element_type=jnp.float32) * scale + bias
        s_ctx = jnp.einsum('bjqhd,bkhd->bhjqk', q_b, k_c, preferred_element_type=jnp.float32) * scale
        p = softmax_f32(jnp.where(valid, jnp.concatenate([s_lat, s_ctx], -1), NEG_INF)).astype(v.dtype)
        o = (jnp.einsum('bhjqk,bjkhd->bjqhd', p[..., :nkey], v_s)
             + jnp.einsum('bhjqk,bkhd->bjqhd', p[..., nkey:], v_c))
        return o.reshape(B, GRID_W, H, dh)

    o = lax.map(row_step, (jnp.arange(rows), jnp.moveaxis(q, 1, 0)))
    y_lat = jnp.moveaxis(o, 0, 1).reshape(B, L, n) @ w_o
    y_ctx = None
    if need_ctx:
        q_c = rms_norm((a_ctx @ w_qkv[:, :n]).reshape(B, Lc, H, dh), g_q)
        s = jnp.einsum('bqhd,bkhd->bhqk', q_c, k_c, preferred_element_type=jnp.float32) * scale
        p = softmax_f32(s).astype(v_c.dtype)
        y_ctx = jnp.einsum('bhqk,bkhd->bqhd', p, v_c).reshape(B, Lc, n) @ w_o
    return y_lat, y_ctx

def multi_pool(h):
    B, L, _ = h.shape
    hf = h.astype(jnp.float32)
    cs = jnp.pad(lax.cumsum(hf, axis=1), ((0, 0), (1, 0), (0, 0)))
    t = jnp.arange(L)
    outs = []
    for g, w in enumerate(POOL_WINDOWS):
        lo = jnp.clip(t - w // 2, 0, L)
        hi = jnp.clip(t - w // 2 + w, 0, L)
        cg = cs[..., g * POOL_DG:(g + 1) * POOL_DG]
        outs.append((cg[:, hi] - cg[:, lo]) / (hi - lo).astype(jnp.float32)[None, :, None])
    return (jnp.concatenate(outs, -1) - hf).astype(h.dtype)

def pool_mixer(a_lat, a_ctx, w, b, scale, need_ctx):
    def mix(h):
        B, L, _ = h.shape
        p = multi_pool(h).reshape(B, L, POOL_GROUPS, POOL_DG)
        y = jnp.einsum('blgc,gcd->blgd', p, w) + b
        return y.reshape(B, L, D_MODEL) * scale
    return mix(a_lat), (mix(a_ctx) if need_ctx else None)

def mla_mixer(a_lat, a_ctx, w_a, g_cq, g_ckv, w_uq, w_ukv, g_q, g_k, w_o, need_ctx):
    H, dn, dr, dv = MLA_HEADS, MLA_NOPE, MLA_ROPE, MLA_V
    dqk = dn + dr
    qr = MLA_Q_RANK
    scale = dqk ** -0.5

    def queries(cq_raw):
        B_, L_, _ = cq_raw.shape
        c_q = rms_norm(cq_raw, g_cq)
        return rms_norm((c_q @ w_uq).reshape(B_, L_, H, dqk), g_q)

    def keys_values(kv_raw):
        B_, L_, _ = kv_raw.shape
        c_kv = rms_norm(kv_raw[..., :MLA_KV_RANK], g_ckv)
        k_r = jnp.broadcast_to(kv_raw[..., MLA_KV_RANK:][:, :, None, :], (B_, L_, H, dr))
        kv = (c_kv @ w_ukv).reshape(B_, L_, H, dn + dv)
        k = rms_norm(jnp.concatenate([kv[..., :dn], k_r], -1), g_k)
        return k, kv[..., dn:]

    def rope_part(t):
        return jnp.concatenate([t[..., :dn], rope_2d_axial(t[..., dn:], t.shape[1])], -1)

    B, L, _ = a_lat.shape
    Lc = a_ctx.shape[1]
    proj = a_lat @ w_a
    q = rope_part(queries(proj[..., :qr]))
    k, v = keys_values(proj[..., qr:])
    k = rope_part(k)
    if need_ctx:
        proj_c = a_ctx @ w_a
        q_c = queries(proj_c[..., :qr])
        kv_raw_c = proj_c[..., qr:]
    else:
        kv_raw_c = a_ctx @ w_a[:, qr:]
    k_c, v_c = keys_values(kv_raw_c)
    k_all = jnp.concatenate([k, k_c], 1)
    v_all = jnp.concatenate([v, v_c], 1)
    nb = L // Q_BLOCK
    q_blocks = jnp.moveaxis(q.reshape(B, nb, Q_BLOCK, H, dqk), 1, 0)

    def block(q_b):
        s = jnp.einsum('bqhd,bkhd->bhqk', q_b, k_all, preferred_element_type=jnp.float32) * scale
        p = softmax_f32(s).astype(v_all.dtype)
        return jnp.einsum('bhqk,bkhd->bqhd', p, v_all)

    o = lax.map(block, q_blocks)
    y_lat = jnp.moveaxis(o, 0, 1).reshape(B, L, H * dv) @ w_o
    y_ctx = None
    if need_ctx:
        s = jnp.einsum('bqhd,bkhd->bhqk', q_c, k_c, preferred_element_type=jnp.float32) * scale
        p = softmax_f32(s).astype(v_c.dtype)
        y_ctx = jnp.einsum('bhqk,bkhd->bqhd', p, v_c).reshape(B, Lc, H * dv) @ w_o
    return y_lat, y_ctx

def second_inputs(seed: int = 0) -> dict:
    key = jax.random.key(seed)
    ks = iter(jax.random.split(key, 48))
    f32 = jnp.float32

    def nrm(shape, fan_in, gain=1.0):
        return jax.random.normal(next(ks), shape, f32) * (gain * fan_in ** -0.5)

    def gains(shape):
        return 1.0 + 0.05 * jax.random.normal(next(ks), shape, f32)

    def small(shape, s=0.01):
        return s * jax.random.normal(next(ks), shape, f32)

    D = D_MODEL
    nA, nB, nC, nD = (n_layers_of(m) for m in range(N_MIXERS))
    dqk = MLA_NOPE + MLA_ROPE
    return {
        'x': jax.random.normal(next(ks), (BATCH, SEQ, D), f32),
        'c': jax.random.normal(next(ks), (BATCH, D), f32),
        'ctx': jax.random.normal(next(ks), (BATCH, CTX_LEN, D), f32),
        'c_ctx': jax.random.normal(next(ks), (D,), f32),
        'w_ada': nrm((DEPTH, D, 6 * D), D, 0.5),
        'b_ada': small((DEPTH, 6 * D)),
        'g_mix': gains((DEPTH, D)),
        'g_ffn': gains((DEPTH, D)),
        'w_gate_up': nrm((DEPTH, D, 2 * D_FF), D),
        'w_down': nrm((DEPTH, D_FF, D), D_FF),
        'swa_w_qkv': nrm((nA, D, (SWA_HEADS + 2 * SWA_KV_HEADS) * HEAD_DIM), D),
        'swa_g_q': gains((nA, HEAD_DIM)),
        'swa_g_k': gains((nA, HEAD_DIM)),
        'swa_sink': small((nA, SWA_HEADS), 0.5),
        'swa_w_o': nrm((nA, SWA_HEADS * HEAD_DIM, D), SWA_HEADS * HEAD_DIM),
        'na_w_qkv': nrm((nB, D, 3 * NA_HEADS * HEAD_DIM), D),
        'na_g_q': gains((nB, HEAD_DIM)),
        'na_g_k': gains((nB, HEAD_DIM)),
        'na_rpb': small((nB, NA_HEADS, 2 * NA_KH - 1, 2 * NA_KW - 1), 0.1),
        'na_w_o': nrm((nB, NA_HEADS * HEAD_DIM, D), NA_HEADS * HEAD_DIM),
        'pool_w': nrm((nC, POOL_GROUPS, POOL_DG, POOL_DG), POOL_DG),
        'pool_b': small((nC, POOL_GROUPS, POOL_DG)),
        'pool_scale': gains((nC, D)),
        'mla_w_a': nrm((nD, D, MLA_Q_RANK + MLA_KV_RANK + MLA_ROPE), D),
        'mla_g_cq': gains((nD, MLA_Q_RANK)),
        'mla_g_ckv': gains((nD, MLA_KV_RANK)),
        'mla_w_uq': nrm((nD, MLA_Q_RANK, MLA_HEADS * dqk), MLA_Q_RANK),
        'mla_w_ukv': nrm((nD, MLA_KV_RANK, MLA_HEADS * (MLA_NOPE + MLA_V)), MLA_KV_RANK),
        'mla_g_q': gains((nD, dqk)),
        'mla_g_k': gains((nD, dqk)),
        'mla_w_o': nrm((nD, MLA_HEADS * MLA_V, D), MLA_HEADS * MLA_V),
    }

def second_block(x, c, ctx, c_ctx, w_ada, b_ada, g_mix, g_ffn, w_gate_up, w_down,
              swa_w_qkv, swa_g_q, swa_g_k, swa_sink, swa_w_o,
              na_w_qkv, na_g_q, na_g_k, na_rpb, na_w_o,
              pool_w, pool_b, pool_scale,
              mla_w_a, mla_g_cq, mla_g_ckv, mla_w_uq, mla_w_ukv, mla_g_q, mla_g_k, mla_w_o):
    cond = jax.nn.silu(c)
    cond_c = jax.nn.silu(c_ctx)
    h, hc = x, ctx
    for i in range(DEPTH):
        m, j = i % N_MIXERS, i // N_MIXERS
        need_ctx = i < DEPTH - 1
        mod = (cond @ w_ada[i] + b_ada[i])[:, None, :]
        mod_c = cond_c @ w_ada[i] + b_ada[i]
        sh1, sc1, gt1, sh2, sc2, gt2 = jnp.split(mod, 6, axis=-1)
        sh1c, sc1c, gt1c, sh2c, sc2c, gt2c = jnp.split(mod_c, 6, axis=-1)
        a = modulate(h, g_mix[i], sh1, sc1)
        ac = modulate(hc, g_mix[i], sh1c, sc1c)
        if m == 0:
            y, yc = swa_mixer(a, ac, swa_w_qkv[j], swa_g_q[j], swa_g_k[j], swa_sink[j], swa_w_o[j], need_ctx)
        elif m == 1:
            y, yc = na_mixer(a, ac, na_w_qkv[j], na_g_q[j], na_g_k[j], na_rpb[j], na_w_o[j], need_ctx)
        elif m == 2:
            y, yc = pool_mixer(a, ac, pool_w[j], pool_b[j], pool_scale[j], need_ctx)
        else:
            y, yc = mla_mixer(a, ac, mla_w_a[j], mla_g_cq[j], mla_g_ckv[j], mla_w_uq[j], mla_w_ukv[j],
                              mla_g_q[j], mla_g_k[j], mla_w_o[j], need_ctx)
        h = h + gt1 * y
        h = h + gt2 * swiglu(modulate(h, g_ffn[i], sh2, sc2), w_gate_up[i], w_down[i])
        if need_ctx:
            hc = hc + gt1c * yc
            hc = hc + gt2c * swiglu(modulate(hc, g_ffn[i], sh2c, sc2c), w_gate_up[i], w_down[i])
    return h


def setup_inputs(seed=0):
    out = dict(first_inputs(seed))
    for name, value in second_inputs(seed + 1).items():
        if name != "x":
            out[name + "_2"] = value
    return out


def reference(
    x, c, ln1_g, ln1_b, ln2_g, ln2_b, w_ada, b_ada, even_w_in, even_w_out, ret_gn_g, odd_w_in,
    odd_w_out, lambda_q1, lambda_k1, lambda_q2, lambda_k2, diff_subln_g, moe_w_group,
    moe_b_group, moe_w_router, moe_b_router, moe_w1, moe_w3, moe_w2, c_2, ctx_2, c_ctx_2,
    w_ada_2, b_ada_2, g_mix_2, g_ffn_2, w_gate_up_2, w_down_2, swa_w_qkv_2, swa_g_q_2,
    swa_g_k_2, swa_sink_2, swa_w_o_2, na_w_qkv_2, na_g_q_2, na_g_k_2, na_rpb_2, na_w_o_2,
    pool_w_2, pool_b_2, pool_scale_2, mla_w_a_2, mla_g_cq_2, mla_g_ckv_2, mla_w_uq_2,
    mla_w_ukv_2, mla_g_q_2, mla_g_k_2, mla_w_o_2,
):
    x = first_block(
        x, c, ln1_g, ln1_b, ln2_g, ln2_b, w_ada, b_ada, even_w_in, even_w_out, ret_gn_g,
        odd_w_in, odd_w_out, lambda_q1, lambda_k1, lambda_q2, lambda_k2, diff_subln_g,
        moe_w_group, moe_b_group, moe_w_router, moe_b_router, moe_w1, moe_w3, moe_w2,
    )
    return second_block(
        x, c_2, ctx_2, c_ctx_2, w_ada_2, b_ada_2, g_mix_2, g_ffn_2, w_gate_up_2, w_down_2,
        swa_w_qkv_2, swa_g_q_2, swa_g_k_2, swa_sink_2, swa_w_o_2, na_w_qkv_2, na_g_q_2,
        na_g_k_2, na_rpb_2, na_w_o_2, pool_w_2, pool_b_2, pool_scale_2, mla_w_a_2, mla_g_cq_2,
        mla_g_ckv_2, mla_w_uq_2, mla_w_ukv_2, mla_g_q_2, mla_g_k_2, mla_w_o_2,
    )


_drawn_inputs = setup_inputs


def setup_inputs(seed=0):
    import zlib

    import numpy as np

    out = dict(_drawn_inputs(seed))
    spreads = {}
    factors = {'b_ada': 2.813,
     'ret_gn_g': 8.0,
     'lambda_q1': 3.441,
     'lambda_k1': 5.108,
     'lambda_q2': 3.379,
     'lambda_k2': 4.735,
     'diff_subln_g': 8.0,
     'moe_b_group': 8.0,
     'moe_b_router': 5.877,
     'b_ada_2': 4.385,
     'g_mix_2': 8.0,
     'g_ffn_2': 2.67,
     'swa_g_q_2': 8.0,
     'swa_g_k_2': 8.0,
     'swa_sink_2': 8.0,
     'na_g_q_2': 8.0,
     'na_g_k_2': 8.0,
     'na_rpb_2': 8.0}
    for name, (base, spread) in spreads.items():
        noise = np.random.default_rng([zlib.crc32(name.encode()), seed]).standard_normal(out[name].shape)
        drawn = base * np.exp(spread * noise) if base else spread * noise
        out[name] = __import__('jax').numpy.asarray(drawn.astype(out[name].dtype))
    for name, factor in factors.items():
        out[name] = (out[name] * factor).astype(out[name].dtype)
    return out
```

```python
from contextlib import ExitStack

import numpy as np

import concourse.bass as bass
from concourse import mybir

F32 = mybir.dt.float32
I32 = mybir.dt.int32
ALU = mybir.AluOpType
ACT = mybir.ActivationFunctionType
AX_X = mybir.AxisListType.X

P = 128
D = 1024
KT = D // P
S = 256
DEPTH = 2
ALPHA = (2.0 * DEPTH) ** 0.25
EPS_LN, EPS_RMS = 1e-5, 1e-6
SB_HEADS, RET_HEADS, DIFF_HEADS = 8, 4, 8
N_GROUPS, PER_GROUP = 4, 8
N_EXPERTS = N_GROUPS * PER_GROUP
FF = 512
D_FF = 2816
FFT = D_FF // P
HQ, HKV = 16, 4
WINDOW = 128
CHUNK = 64
NEG = -1e30
LAMBDA_INIT = 0.8 - 0.6 * float(np.exp(-0.3))
GRID_W, NA_KH, NA_KW, NA_ROWS = 64, 8, 16, S // 64

RING = 12
SLOT = 2048

BLK = 32
GRP = 4
MAX_BLOCKS = 2 * S // BLK + N_EXPERTS + GRP
MAX_GROUPS = MAX_BLOCKS // GRP
INFO = 1 + MAX_BLOCKS

CONST = {}
_at = 0
for _name, _w in (("ident", P), ("ones", P), ("blk64", P), ("rot", P), ("before", P),
                  ("quad", 224), ("halves", 320), ("iota", P), ("sbmask", 384), ("namask", 64),
                  ("thresh", 8), ("gthresh", MAX_GROUPS), ("lead", N_EXPERTS), ("halfcol", 2), ("one", 1), ("eps_ln", 1),
                  ("eps_rms", 1), ("pid", 1)):
    CONST[_name] = (_at, _at + _w)
    _at += _w
CONST_W = _at
FIRST = {"decay": (0, 4 * 384), "dist": (1536, 1920), "after": (1920, 2048)}
ROPE = {"cos": (0, 256), "sin": (256, 512), "window": (512, 1024)}

COLS = {}
_at = 0
for _name, _w in (("c", KT), ("c2", KT), ("cc", KT), ("ln1_g", 2 * KT), ("ln1_b", 2 * KT), ("ln2_g", 2 * KT),
                  ("ln2_b", 2 * KT), ("b_ada", 4 * 48), ("ret_g", RET_HEADS), ("subln", 1), ("g_mix", 2 * KT),
                  ("g_ffn", 2 * KT), ("swa_gq", 1), ("swa_gk", 1), ("na_gq", 1), ("na_gk", 1), ("sink", HQ),
                  ("lam", 4), ("b_route", 2 * 36)):
    COLS[_name] = (_at, _at + _w)
    _at += _w
COLS_W = _at


def shape_constants():
    p = np.arange(P)
    q = np.arange(P)
    c = np.zeros((P, CONST_W), np.float32)

    def put(name, value):
        a, b = CONST[name]
        c[:, a:b] = value

    put("ident", np.eye(P))
    put("ones", 1.0)
    put("blk64", (p[:, None] // 64 == p[None, :] // 64))
    rot = np.zeros((P, P))
    for m in range(P):
        if m % 32 < 16:
            rot[m + 16, m] = -1.0
        else:
            rot[m - 16, m] = 1.0
    put("rot", rot)
    put("before", (p[:, None] < p[None, :]))
    quad = np.zeros((P, 224))
    quad[p, 96 + p % 32] = 1.0
    put("quad", quad)
    halves = np.zeros((P, 320))
    halves[:, 64:128] = np.eye(P)[:, 0:64]
    halves[:, 192:256] = np.eye(P)[:, 64:128]
    put("halves", halves)
    put("iota", np.arange(P)[None, :])
    diag = np.where(p[:, None] < q[None, :], 0.0, NEG)
    put("sbmask", np.concatenate([diag, np.zeros((P, P)), diag], 1))
    qc = p % GRID_W
    kc = np.arange(GRID_W)
    start = np.clip(qc - NA_KW // 2, 0, GRID_W - NA_KW)
    put("namask", np.where((kc[None] >= start[:, None]) & (kc[None] < start[:, None] + NA_KW), 0.0, NEG))
    put("thresh", BLK * np.arange(8)[None, :])
    put("lead", (np.arange(N_EXPERTS) < GRP)[None, :])
    put("gthresh", GRP * np.arange(1, 1 + MAX_GROUPS)[None, :])
    put("halfcol", np.stack([p < 64, p >= 64], 1) * 0.125)
    put("one", 1.0)
    put("eps_ln", EPS_LN)
    put("eps_rms", EPS_RMS)
    put("pid", p[:, None])

    f = np.zeros((P, 2048), np.float32)
    log_gamma = np.log1p(-np.exp2(-5.0 - np.arange(RET_HEADS)))
    kpos, qpos = np.arange(P)[:, None], np.arange(S)[None, :]
    for h in range(RET_HEADS):
        decay = np.exp(log_gamma[h] * np.abs(qpos - kpos)) * (kpos // CHUNK <= qpos // CHUNK)
        f[:, h * 384:h * 384 + 256] = decay
        f[:, h * 384 + 256:h * 384 + 384] = decay[:, 0:P]
    near = np.where(q[None, :] // CHUNK <= p[:, None] // CHUNK, np.abs(p[:, None] - q[None, :]), -NEG * 1e4)
    f[:, 1536:1920] = np.concatenate([near, P + p[:, None] - q[None, :], near], 1)
    f[:, 1920:2048] = (p[:, None] >= p[None, :])

    r = np.zeros((P, 1024), np.float32)
    t = np.arange(S)
    half = 16
    freqs = 10000.0 ** (-np.arange(half) / half)
    for m in range(P):
        d = m % 64
        pos = t // GRID_W if d < 32 else t % GRID_W
        ang = pos * freqs[d % 16]
        r[m, 0:256], r[m, 256:512] = np.cos(ang), np.sin(ang)
    for qb in range(2):
        valid = np.abs(p[:, None] + P * qb - t[None, :]) <= WINDOW
        r[:, 512 + 256 * qb:768 + 256 * qb] = np.where(valid, 0.0, NEG)
    return c, f, r


def build(nc, a, out, last_stage=99):
    ctx = ExitStack()
    with ctx:
        def sb(name, shape, dt=F32):
            return ctx.enter_context(nc.sbuf_tensor(name, shape, dt))

        def sem(name):
            return ctx.enter_context(nc.semaphore(name))

        ring = sb("ring", [P, RING, SLOT])
        res = sb("res", [P, 2, KT, S])
        u = sb("u", [P, 2, KT, S])
        work = sb("work", [P, 12288])
        scratch = sb("scratch", [P, 4096])
        const = sb("const", [P, CONST_W])
        cols = sb("cols", [P, COLS_W])
        mod = sb("mod", [P, 4, 48, 2])
        cond = sb("cond", [P, 24])
        condrep = sb("condrep", [P, KT, 32])
        adaT = sb("adaT", [P, 512])
        adac = sb("adac", [P, 4, 48, 2])
        tiny = sb("tiny", [P, 96])
        info = sb("info", [P, 64], I32)
        wroute = sb("wroute", [P, KT * 36])
        zmore = sb("zmore", [P, 3, 512])

        bank = [ctx.enter_context(nc.psum_tensor(f"bank{i}", [P, 512], F32)) for i in range(8)]

        def K(name):
            lo, hi = CONST[name]
            return const[:, lo:hi]

        def C(name, i=0, n=None):
            lo, hi = COLS[name]
            return cols[:, lo + i:hi if n is None else lo + i + n]

        first = res[:, 1].rearrange("p k s -> p (k s)")
        decay = first[:, 0:1536].rearrange("p (h w) -> p h w", w=384)
        dist = first[:, 1536:1920]
        after = first[:, 1920:2048]
        ident, ones = K("ident"), K("ones")
        x = res[:, 0]
        o1 = u[:, 1]
        both = lambda t, k: t[:, :, k, :]

        def W(lo, *dims):
            n = int(np.prod(dims))
            v = work[:, lo:lo + n]
            if len(dims) == 1:
                return v
            names = "abcd"[:len(dims)]
            return v.rearrange(f"p ({' '.join(names)}) -> p {' '.join(names)}", **dict(zip(names, dims)))

        def X(lo, *dims):
            n = int(np.prod(dims))
            v = scratch[:, lo:lo + n]
            if len(dims) == 1:
                return v
            names = "abcd"[:len(dims)]
            return v.rearrange(f"p ({' '.join(names)}) -> p {' '.join(names)}", **dict(zip(names, dims)))

        sq_pad = W(0, SB_HEADS, S)
        sk = W(2048, 4, S)
        sv = W(3072, 2, 512)
        rq = W(4096, 4, S)
        rk = W(5120, 4, S)
        rv = W(6144, 2, 512)
        rg = W(7168, 4, S)
        sb_t = W(8192, 4, 384)
        sb_l = W(9728, 4, 384)
        sb_z = X(0, 4, 384)
        ret_p = X(1536, 4, 384)
        ret_o = W(8192, 4, S)
        ret_s = W(9216, 4, S)
        dq_pad = W(0, 16, S)
        dk = W(4096, 8, S)
        dv = W(6144, 2, D)
        dz3 = [W(8192, 2, 384), W(8960, 2, 384), W(11264, 2, 384)]
        da = W(9728, 2, 384)
        daT = W(10496, 2, 384)
        dsq = X(0, 8, S)
        dr = X(2048, 8, S)
        xnat = W(0, 2, D)
        acc = W(2048, KT, S)
        xg = W(4096, KT, P)
        sil = W(5120, 512)
        hid = W(5632, 512)
        hidT = W(6144, 4, P)
        ysb = W(6656, D)
        sel = W(7680, 2, P)
        selT = W(7936, S)
        selT2 = W(8192, S)
        drow = W(8448, 4, S)
        route = W(9472, 2048)
        R_CH, R_BC, R_EXP, R_DEST, R_SMALL = 0, 64, 1088, 1098, 1103
        dest = route[:, R_DEST:R_DEST + 4].rearrange("p (c b) -> p c b", c=2)
        slotcol = route[:, R_DEST + 4:R_DEST + 5]
        wq = W(0, 8, 2, S)
        kpad = W(4096, 8, 512)
        wv = W(8192, 4, S)
        kraw = W(9216, 2, 2, S)
        rope = work[:, 10240:11264]
        nq_pad = W(0, HQ, S)
        nk = W(4096, 8, 2, S)
        nv = W(8192, 4, D)
        hidden = W(0, FFT, 2, S)
        pT = X(0, 4, 4, S)
        nz = first[:, 0:1536].rearrange("p (b w) -> p b w", w=512)
        wz = W(9216, 3, 512)
        zbuf = {2: [wz[:, i] for i in range(3)], 3: [nz[:, i] for i in range(3)]}
        for v in zbuf.values():
            v += [zmore[:, i] for i in range(3)]
        btab = u[:, 1].rearrange("p k s -> p (k s)")[:, 0:1536].rearrange("p (b j w) -> p b j w", b=4, w=GRID_W)

        lead0 = []
        tile0, slot0 = {}, {}
        loads = []
        state = {"t": 0, "epoch": 0, "n": 0}
        per_pos = [0] * RING

        def job(name, tiles, sources=(), release=None):
            tile0[name] = state["t"]
            slot0[name] = len(loads)
            state["t"] += tiles
            for i, src in enumerate(sources):
                r = state["n"] % RING
                per_pos[r] += 1
                by_tile = release is None or i == len(sources) - 1
                rel = ("tile", state["t"] - 1) if by_tile else ("down", release + i + 1)
                loads.append((state["epoch"], r, per_pos[r], src, rel))
                state["n"] += 1

        def panel(w, g):
            v = w[:, 512 * g:512 * g + 512].rearrange("(k p) n -> p k n", p=P)
            return [v[:, 0:4], v[:, 4:8]]

        def ada_jobs(L, g0, g1):
            w = a["w_ada"][L] if L < 2 else a["w_ada_2"][L - 2]
            for g in range(g0, g1):
                job(f"ada{L}.{g}", 1, panel(w, g))

        def lead_jobs(l):
            lead0.append(state["n"] % RING)
            for ph in range(3):
                for j in range(GRP):
                    w = a["moe_w1"] if ph < 2 else a["moe_w3"]
                    half = ph % 2
                    src = w[l, j, 512 * half:512 * half + 512, :].rearrange("(k p) n -> p k n", p=P)
                    loads.append((state["epoch"], state["n"] % RING, 0, src, None))
                    state["n"] += 1

        def down_jobs(L):
            v = a["w_down_2"][L - 2].rearrange("(k p) n -> p k n", p=P)
            job(f"down{L}", 8, [v[:, 2 * i:2 * i + 2] for i in range(FFT // 2)], release=(L - 2) * (FFT // 2 - 1))

        ada_jobs(0, 0, 4)
        job("adafin0a", 1)
        for g in range(7):
            job(f"even.{g}", 2 if g in (2, 5) else 4, panel(a["even_w_in"][0], g))
            ada_jobs(0, 4 + g, 5 + g)
        ada_jobs(0, 11, 12)
        job("adafin0b", 1)
        for b in range(2):
            job(f"sbS{b}", 4)
            ada_jobs(1, 4 * b, 4 * b + 3)
            job(f"sbR{b}", 4)
            ada_jobs(1, 4 * b + 3, 4 * b + 4)
            job(f"sbO{b}", 2)
        job("retS", 4)
        ada_jobs(1, 8, 9)
        job("retO", 4)
        job("retM", 2)
        ada_jobs(1, 9, 10)
        job("retV", 2)
        ada_jobs(1, 10, 12)
        for g in range(2):
            job(f"out0.{g}", 4, panel(a["even_w_out"][0], g))
        job("adafin1a", 1)
        job("adafin1b", 1)
        job("ln0a", 2)
        job("route0", 1 + 4 + 1 + 2)
        lead_jobs(0)
        state.update(epoch=1)
        job("ln0b", 2)
        for g in range(6):
            job(f"odd.{g}", 2 if g >= 4 else 4, panel(a["odd_w_in"][0], g))
        job("lam", 1)
        for n in range(DIFF_HEADS + 3):
            if n < DIFF_HEADS:
                job(f"dS{n}", 2)
            if n < 10:
                ada_jobs(2, n, n + 1)
            if 2 <= n < DIFF_HEADS + 2:
                job(f"dT{n - 2}", 1)
            if n >= 3:
                job(f"dO{n - 3}", 1)
        job("dV", 4)
        ada_jobs(2, 10, 12)
        for g in range(2):
            job(f"out1.{g}", 4, panel(a["odd_w_out"][0], g))
        job("adafin2a", 1)
        job("adafin2b", 1)
        job("ln1a", 2)
        job("route1", 1 + 4 + 1 + 2)
        lead_jobs(1)
        state.update(epoch=2)
        job("ln1b", 2)
        for L in (2, 3):
            w_in = a["swa_w_qkv_2"][0] if L == 2 else a["na_w_qkv_2"][0]
            w_o = a["swa_w_o_2"][0] if L == 2 else a["na_w_o_2"][0]
            job(f"rms{L}a", 1)
            if L == 2:
                for g in range(2):
                    job(f"in2.{g}", 4, panel(w_in, g))
                job("in2.2", 6, panel(w_in, 2))
                job("nrm2", 20)
                job("kpad", 8)
            else:
                for g in range(6):
                    job(f"in3.{g}", 4, panel(w_in, g))
                job("nrm3", 16)
            units = [(s, h) for s in range(2 if L == 2 else 1) for h in range(HQ)]
            for n in range(len(units) + 3):
                if n < len(units):
                    job(f"aS{L}.{n}", 2 if units[n][0] == 0 else 1)
                if L == 2 and n < 24 and n % 2 == 0:
                    ada_jobs(3, n // 2, n // 2 + 1)
                if 2 <= n < len(units) + 2:
                    job(f"aT{L}.{n - 2}", 2 if units[n - 2][0] == 0 else 1)
                if n >= 4 and n % 2 == 0:
                    job(f"aO{L}.{(n - 4) // 2}", 1)
            for g in range(2):
                job(f"out{L}.{g}", 4, panel(w_o, g))
            if L == 2:
                job("adafin3a", 1)
                job("adafin3b", 1)
            job(f"rms{L}b", 1)
            for g in range(11):
                job(f"gu{L}.{g}", 4, panel(a["w_gate_up_2"][L - 2], g))
            down_jobs(L)

        SEQ = {}
        for L in (2, 3):
            SEQ[L] = []
            for v, (s, h) in enumerate((s, h) for s in range(2 if L == 2 else 1) for h in range(HQ)):
                for qb in range(2 if s == 0 else 1):
                    SEQ[L].append((v, s, h, qb, tile0[f"aS{L}.{v}"] + qb, tile0[f"aT{L}.{v}"] + qb))
        SB0 = {2: DIFF_HEADS, 3: DIFF_HEADS + len(SEQ[2])}
        NB = {2: 0, 3: 10}
        RMS_N = {2: (5, 6), 3: (7, 8)}
        U_N = {2: (24, 32), 3: (40, 44)}

        def NT(L, i):
            return tile0[f"nrm{L}"] + (i if L == 3 else max(2 * i - 1, 0))

        def RT(i):
            return tile0["nrm2"] + min(2 * i + 2, 19)

        def nsq(i, width):
            return X(1024 + 512 * (i % 2), width)

        UNITS = {L: [(s, h) for s in range(2 if L == 2 else 1) for h in range(HQ)] for L in (2, 3)}

        filled = [sem(f"bank{i}_filled") for i in range(8)]
        moved = [sem(f"bank{i}_moved") for i in range(8)]
        loaded = [sem(f"slot{i}_loaded") for i in range(RING)]
        mloaded = [[sem(f"moe{l}_slot{i}_loaded") for i in range(RING)] for l in range(2)]
        down_used = sem("down_slot_used")
        const_in = sem("constants_loaded")
        first_in = sem("first_stack_loaded")
        second_in = sem("context_loaded")
        rope_in = sem("rope_loaded")
        cond_done = sem("condition_ready")
        condrep_done = sem("condition_spread")
        mod_done = sem("modulation_ready")
        u_act, u_dve = sem("u_by_act"), sem("u_by_dve")
        x_act, x_dve = sem("residual_by_act"), sem("residual_by_dve")
        xs_done = sem("residual_scaled")
        sq_act, sq_dve = sem("squares_by_act"), sem("squares_by_dve")
        std_done = sem("deviation_ready")
        cent_done = sem("centred_by_dve")
        sb_d, sb_e, sb_sp, sb_a, sb_w = (sem(f"sb_{n}") for n in ("negabs", "log", "softplus", "exponent", "weights"))
        ret_done = sem("retention_ready")
        soft_z, soft_e, soft_p = sem("scores_shifted"), sem("exponentials_ready"), sem("probabilities_ready")
        lam_e = sem("lambda_exponentials")
        lam_p = sem("lambda_products")
        o_done = sem("attention_output_ready")
        nrm_std = sem("head_deviation_ready")
        nrm_q = sem("head_normed")
        nrm_done = sem("head_rotated")
        bias_in = [sem(f"bias{i}_loaded") for i in range(4)]
        bias_ok = sem("bias_masked")
        route_pe = sem("routing_counted")
        route_dve = sem("routing_ready")
        route_act = sem("routing_exponentials")
        info_done = sem("block_table_ready")
        acc_zero = sem("sum_cleared")
        moe = []
        for l in range(2):
            moe.append({n: sem(f"moe{l}_{n}") for n in (
                "selected", "gathered", "xg_by_act", "xg_by_dve", "phase", "silu", "hidden", "turned", "turned_out",
                "y_by_act", "y_by_dve", "spread_ready", "scattered", "summed", "step")})
        chain_v, chain_a = sem("dve_step"), sem("act_step")
        chain_adac = sem("modulation_sums_turned")
        res_ready = sem("residual_complete")
        nsq_done = sem("head_squares_ready")
        wroute_in = sem("router_weights_loaded")
        out_done = sem("output_stored")

        def is_filled(eng, t):
            eng.wait_ge(filled[t % 8], t // 8 + 1)

        def is_moved(eng, t):
            eng.wait_ge(moved[t % 8], t // 8 + 1)

        def T(name, i=0):
            return tile0[name] + i

        def B(t):
            return bank[t % 8]

        block = ctx.enter_context(nc.Block())

        @block.sync
        def _(sp):
            def epoch(e):
                for n, (ep, r, count, src, _) in enumerate(loads):
                    if ep != e:
                        continue
                    first_of_epoch = n == 0 or loads[n - 1][0] != e
                    if first_of_epoch:
                        sp_state["base"] = n
                    k = n - sp_state["base"]
                    if k >= RING:
                        kind, v = loads[n - RING][4]
                        if kind == "tile":
                            is_filled(sp, v)
                        else:
                            sp.wait_ge(down_used, v)
                    elif e > 0:
                        sp.wait_ge(moe[e - 1]["phase"], sp_state["more"] * 6 + (k // 4 + 4))
                    dst = ring[:, r, :].rearrange("p (k n) -> p k n", n=src.shape[2])
                    sp.dma_start(dst, src).then_inc(loaded[r] if count else mloaded[e][r], 16)

            sp_state = {}

            def experts(l):
                m = moe[l]
                sp.wait_ge(info_done, l + 1)
                more = sp.value_load(info[0:1, 0:1], min_val=0, max_val=MAX_GROUPS - 1)
                sp_state["more"] = more

                def group(i, phases):
                    for ph in phases:
                        if ph in (phases[0], 4):
                            e = [sp.value_load(info[0:1, bass.ds(1 + GRP * i + j, 1)], min_val=1, max_val=N_EXPERTS)
                                 for j in range(GRP)]
                        sp.wait_ge(m["phase"], 6 * i + (ph - 2))
                        for j in range(GRP):
                            r = (lead0[l] + 4 * ph + j) % RING
                            if ph < 4:
                                w = a["moe_w1"] if ph < 2 else a["moe_w3"]
                                half = ph % 2
                                src = w[l, bass.ds(e[j] - 1, 1), 512 * half:512 * half + 512, :]
                                src = src.rearrange("a (k p) n -> p (a k) n", p=P)
                                dst = ring[:, r, :].rearrange("p (k n) -> p k n", k=4)
                            else:
                                half = ph - 4
                                src = a["moe_w2"][l, bass.ds(e[j] - 1, 1), 256 * half:256 * half + 256, :]
                                src = src.rearrange("a (k p) n -> p (a k) n", p=P)
                                dst = ring[:, r, :].rearrange("p (k n) -> p k n", k=2)
                            sp.dma_start(dst, src).then_inc(mloaded[l][r], 16)

                with sp.Fori(0, more) as i:
                    group(i, (3, 4, 5))
                    group(i + 1, (0, 1, 2))
                group(more, (3, 4, 5))

            epoch(0)
            if last_stage >= 2:
                experts(0)
            if last_stage >= 3:
                epoch(1)
            if last_stage >= 4:
                experts(1)
            if last_stage >= 5:
                epoch(2)
            sp.wait_ge(x_act, 4 * min(last_stage, 4))
            sp.wait_ge(x_dve, 4 * min(last_stage, 4))
            if last_stage >= 5:
                for i in range(8):
                    is_moved(sp, T("down2" if last_stage < 7 else "down3", i))
            sp.dma_start(out, x).then_inc(out_done, 16)
            sp.wait_ge(out_done, 16)

        @block.tensor
        def _(pe):
            def open_tile(t):
                if t >= 8:
                    is_moved(pe, t - 8)
                return B(t)

            def mm(o, l, r, start=True, stop=True):
                return pe.matmul(o, l, r, start=start, stop=stop, skip_group_check=True)

            def slot(n):
                _, r, count, src, _ = loads[n]
                pe.wait_ge(loaded[r], 16 * count)
                return ring[:, r, :].rearrange("p (k n) -> p k n", n=src.shape[2])

            def panel_slots(name):
                n = slot0[name]
                s0, s1 = slot(n), slot(n + 1)
                return lambda k: (s0, s1)[k // 4][:, k % 4]

            def ada(L, g0, g1):
                pe.wait_ge(condrep_done, 1 if L < 2 else 2)
                for g in range(g0, g1):
                    t = T(f"ada{L}.{g}")
                    b = open_tile(t)
                    w = panel_slots(f"ada{L}.{g}")
                    for k in range(KT):
                        j = k % 4
                        r = mm(b[32 * j:32 * j + 32, :], condrep[:, k, :], w(k), start=k < 4, stop=k >= 4)
                    r.then_inc(filled[t % 8], 1)

            def ada_sums(L, part):
                t = T(f"adafin{L}{part}")
                b = open_tile(t)
                a0, a1 = (0, 16) if part == "a" else (16, 48)
                pe.wait_ge(chain_adac, 12 * L + a1 // 4)
                lo = CONST["quad"][0]
                for q in range(4):
                    r = mm(b[:, 0:2 * (a1 - a0)], const[:, lo + 96 - 32 * q:lo + 224 - 32 * q],
                           adac[:, q, a0:a1].rearrange("p a c -> p (a c)"), start=q == 0, stop=q == 3)
                r.then_inc(filled[t % 8], 1)

            def project(name, rhs, width, tiles=4, first_tile=0, w=None):
                w = w or panel_slots(name)
                for i in range(tiles):
                    t = T(name, first_tile + i)
                    b = open_tile(t)
                    for k in range(KT):
                        r = mm(b[:, 0:width], w(k)[:, P * i:P * i + P], rhs(k), start=k == 0, stop=k == KT - 1)
                    r.then_inc(filled[t % 8], 1)

            def project_tokens(name, streams, c0, c1, first_tile=0, w=None):
                w = w or panel_slots(name)
                i = 0
                for s in range(streams):
                    for tb in range(2):
                        t = T(name, first_tile + i)
                        i += 1
                        b = open_tile(t)
                        for k in range(KT):
                            r = mm(b[:, 0:c1 - c0], u[:, s, k, P * tb:P * tb + P], w(k)[:, c0:c1],
                                   start=k == 0, stop=k == KT - 1)
                        r.then_inc(filled[t % 8], 1)

            def one_tile(t, calls):
                b = open_tile(t)
                for args in calls(b):
                    r = mm(*args)
                r.then_inc(filled[t % 8], 1)

            def ln_sums(name, n_sq):
                pe.wait_ge(res_ready, n_sq)
                one_tile(T(name), lambda b: [(b[:, 0:S], ones, x[:, k], k == 0, k == KT - 1) for k in range(KT)])
                pe.wait_ge(sq_act, n_sq)
                pe.wait_ge(sq_dve, n_sq)
                sqv = X(0, KT, S)
                one_tile(T(name, 1), lambda b: [(b[:, 0:S], ones, sqv[:, k], k == 0, k == KT - 1)
                                                for k in range(KT)])

            def even():
                ada(0, 0, 4)
                ada_sums(0, "a")
                pe.wait_ge(u_act, 4)
                pe.wait_ge(u_dve, 4)
                rhs = lambda k: u[:, 0, k]
                for g in range(7):
                    if g in (2, 5):
                        project_tokens(f"even.{g}", 1, 0, 512)
                    else:
                        project(f"even.{g}", rhs, S)
                    ada(0, 4 + g, 5 + g)
                ada(0, 11, 12)
                ada_sums(0, "b")
                for b in range(2):
                    for i in range(4):
                        h = 4 * b + i
                        is_moved(pe, T("even.0", h // 2))
                        is_moved(pe, T("even.1", h // 2))
                        one_tile(T(f"sbS{b}", i), lambda o: [
                            (o[:, 0:256], sk[:, h // 2, 0:P], sq_pad[:, h]),
                            (o[:, 256:384], sk[:, h // 2, P:S], sq_pad[:, h, P:S])])
                    ada(1, 4 * b, 4 * b + 3)
                    pe.wait_ge(sb_sp, b + 1)
                    for i in range(4):
                        one_tile(T(f"sbR{b}", i), lambda o: [
                            (o[:, 0:256], after, sb_l[:, i, 0:256], True, False),
                            (o[:, 128:256], ones, sb_l[:, i, 256:384], False, True),
                            (o[:, 256:384], after, sb_l[:, i, 256:384])])
                    ada(1, 4 * b + 3, 4 * b + 4)
                    for i in range(2):
                        pe.wait_ge(sb_w, b + 1)
                        is_moved(pe, T("even.2", 1))
                        calls = []
                        t = T(f"sbO{b}", i)
                        o = B(t)
                        for tb, (lo, hi) in enumerate(((0, 256), (128, 256))):
                            for j in range(2):
                                h = 4 * b + 2 * i + j
                                src = sb_l[:, 2 * i + j, 0:256] if tb == 0 else sb_l[:, 2 * i + j, 256:384]
                                calls.append((o[64 * j:64 * j + 64, lo:hi], sv[:, tb, 64 * h:64 * h + 64], src,
                                              tb == 0, tb == 1))
                        one_tile(t, lambda o: calls)
                is_moved(pe, T("even.3", 3))
                is_moved(pe, T("even.4", 3))
                for h in range(4):
                    one_tile(T("retS", h), lambda o: [
                        (o[:, 0:256], rk[:, h, 0:P], rq[:, h]),
                        (o[:, 256:384], rk[:, h, P:S], rq[:, h, P:S])])
                is_moved(pe, T("even.5", 1))
                ada(1, 8, 9)
                for h in range(4):
                    is_moved(pe, T("retS", h))
                    one_tile(T("retO", h), lambda o: [
                        (o[:, 0:256], rv[:, 0, P * h:P * h + P], ret_p[:, h, 0:256], True, False),
                        (o[:, 128:256], rv[:, 1, P * h:P * h + P], ret_p[:, h, 256:384], False, True)])
                for h in range(2):
                    is_moved(pe, T("retO", 2 * h + 1))
                    is_moved(pe, T("retO", 2 * h))
                    one_tile(T("retM", h), lambda o: [(o[:, :], ones, ret_o[:, 2 * h:2 * h + 2])])
                ada(1, 9, 10)
                pe.wait_ge(ret_done, 1)
                for h in range(2):
                    one_tile(T("retV", h), lambda o: [(o[:, :], ones, ret_s[:, 2 * h:2 * h + 2])])
                ada(1, 10, 12)
                pe.wait_ge(o_done, 1)
                is_moved(pe, T("sbO1", 1))
                is_moved(pe, T("sbO0", 1))
                is_moved(pe, T("sbO0", 0))
                is_moved(pe, T("sbO1", 0))
                for g in range(2):
                    project(f"out0.{g}", lambda k: o1[:, k], S)
                ada_sums(1, "a")
                ada_sums(1, "b")
                ln_sums("ln0a", 1)

            def odd():
                pe.wait_ge(u_act, 12)
                pe.wait_ge(u_dve, 12)
                rhs = lambda k: u[:, 0, k]
                for g in range(6):
                    if g >= 4:
                        project_tokens(f"odd.{g}", 1, 0, 512)
                    else:
                        project(f"odd.{g}", rhs, S)
                pe.wait_ge(lam_p, 1)
                one_tile(T("lam"), lambda o: [(o[:, 0:2], ones, tiny[:, 0:2])])
                for i in range(4):
                    for g in range(4):
                        is_moved(pe, T(f"odd.{g}", i))
                for g in (4, 5):
                    for i in range(2):
                        is_moved(pe, T(f"odd.{g}", i))
                for n in range(DIFF_HEADS + 3):
                    if n < DIFF_HEADS:
                        for m in range(2):
                            q = dq_pad[:, 2 * n + m]
                            one_tile(T(f"dS{n}", m), lambda o: [
                                (o[:, 0:128], q[:, 0:P], dk[:, n, 0:P]),
                                (o[:, 128:384], q[:, P:S], dk[:, n, :])])
                    if n < 10:
                        ada(2, n, n + 1)
                    if 2 <= n < DIFF_HEADS + 2:
                        h = n - 2
                        pe.wait_ge(soft_p, h + 1)
                        t = T(f"dT{h}")
                        o = open_tile(t)
                        for c in range(3):
                            src = (0, 128, 256)[c]
                            r = pe.transpose(o[:, src:src + P], da[:, h % 2, src:src + P], ident)
                        r.then_inc(filled[t % 8], 1)
                    if n >= 3:
                        h = n - 3
                        is_moved(pe, T(f"dT{h}"))
                        one_tile(T(f"dO{h}"), lambda o: [
                            (o[:, 0:256], dv[:, 0, P * h:P * h + P], daT[:, h % 2, 0:256], True, False),
                            (o[:, 128:256], dv[:, 1, P * h:P * h + P], daT[:, h % 2, 256:384], False, True)])
                pe.wait_ge(ret_done, 2)
                for i in range(4):
                    one_tile(T("dV", i), lambda o: [(o[:, :], ones, dsq[:, 2 * i:2 * i + 2])])
                ada(2, 10, 12)
                pe.wait_ge(o_done, 2)
                for g in range(2):
                    project(f"out1.{g}", lambda k: o1[:, k], S)
                ada_sums(2, "a")
                ada_sums(2, "b")
                ln_sums("ln1a", 3)

            def routing(l):
                m = moe[l]
                pe.wait_ge(u_act, 8 + 8 * l)
                pe.wait_ge(u_dve, 8 + 8 * l)
                pe.wait_ge(wroute_in, 32 * (l + 1))
                t = T(f"route{l}")
                b = open_tile(t)
                for tb in range(2):
                    for k in range(KT):
                        r = mm(b[:, 36 * tb:36 * tb + 36], u[:, 0, k, P * tb:P * tb + P],
                               wroute[:, 36 * k:36 * k + 36], k == 0, k == KT - 1)
                r.then_inc(filled[t % 8], 1)
                for i in range(4):
                    t = T(f"route{l}", 1 + i)
                    b = open_tile(t)
                    for j in range(4):
                        n = 4 * i + j
                        r = pe.transpose(b[:, P * j:P * j + P], x[:, n % KT, P * (n // KT):P * (n // KT) + P], ident)
                    r.then_inc(filled[t % 8], 1)
                pe.wait_ge(route_dve, 3 * l + 1)
                t = T(f"route{l}", 5)
                ch = route[:, R_CH:R_CH + 64]
                one_tile(t, lambda o: [
                    (o[:, 0:32], K("before"), ch[:, 0:32]),
                    (o[:, 32:64], K("before"), ch[:, 32:64], True, False),
                    (o[:, 32:64], ones, ch[:, 0:32], False, True),
                    (o[:, 64:96], ones, ch[:, 0:32], True, False),
                    (o[:, 64:96], ones, ch[:, 32:64], False, True)])
                pe.wait_ge(route_dve, 3 * l + 3)
                for i in range(2):
                    t = T(f"route{l}", 6 + i)
                    b = open_tile(t)
                    for j in range(4):
                        v, tb = 2 * i + j // 2, j % 2
                        at = R_BC + P * (4 * i + j)
                        r = mm(b[:, P * j:P * j + P], route[:, at:at + P], ident)
                    r.then_inc(filled[t % 8], 1)

            def experts(l):
                m = moe[l]
                last = T(f"route{l}", 7)
                for t in range(last - 7, last + 1):
                    is_moved(pe, t)
                pe.wait_ge(info_done, l + 1)
                n = pe.value_load(info[0:1, 0:1], min_val=0, max_val=MAX_GROUPS - 1) + 1
                with pe.Fori(0, n) as i:
                    pe.wait_ge(m["selected"], i + 1)
                    pe.wait_ge(m["summed"], 4 * i + 1)
                    for k in range(KT):
                        o = bank[k // 4][:, P * (k % 4):P * (k % 4) + P]
                        mm(o, xnat[:, 0, P * k:P * k + P], sel[:, 0], True, False)
                        r = mm(o, xnat[:, 1, P * k:P * k + P], sel[:, 1], False, True)
                        if k % 4 == 3:
                            r.then_inc(m["gathered"], 1)
                    pe.wait_ge(m["xg_by_act"], 4 * i + 4)
                    pe.wait_ge(m["xg_by_dve"], 4 * i + 4)
                    for ph in range(4):
                        o = bank[2 + ph // 2]
                        for j in range(GRP):
                            r_ = (lead0[l] + 4 * ph + j) % RING
                            pe.wait_ge(mloaded[l][r_], 16 * (2 * i + (1 if ph < 3 else 2)))
                        for k in range(4):
                            for j in range(GRP):
                                w = ring[:, (lead0[l] + 4 * ph + j) % RING, :].rearrange("p (k n) -> p k n", k=4)
                                r = mm(o[32 * j:32 * j + 32, :], xg[:, 4 * (ph % 2) + k, 32 * j:32 * j + 32], w[:, k],
                                       ph % 2 == 0 and k == 0, ph % 2 == 1 and k == 3)
                        r.then_inc(m["phase"], 1)
                    pe.wait_ge(m["hidden"], i + 1)
                    for f in range(4):
                        r = pe.transpose(bank[4][:, P * f:P * f + P], hid[:, P * f:P * f + P], ident)
                    r.then_inc(m["turned"], 1)
                    pe.wait_ge(m["turned_out"], i + 1)
                    for ph in (4, 5):
                        for j in range(GRP):
                            r_ = (lead0[l] + 4 * ph + j) % RING
                            pe.wait_ge(mloaded[l][r_], 16 * (2 * i + 2))
                        for k in range(2):
                            f = 2 * (ph - 4) + k
                            for c in range(2):
                                for j in range(GRP):
                                    w = ring[:, (lead0[l] + 4 * ph + j) % RING, :].rearrange("p (k n) -> p k n", k=2)
                                    r = mm(bank[5 + c][32 * j:32 * j + 32, :], hidT[:, f, 32 * j:32 * j + 32],
                                           w[:, k, 512 * c:512 * c + 512], f == 0, f == 3)
                        r.then_inc(m["phase"], 1)
                    pe.wait_ge(m["y_by_act"], i + 1)
                    pe.wait_ge(m["y_by_dve"], i + 1)
                    pe.wait_ge(m["spread_ready"], i + 1)
                    for c, b in enumerate((7, 4, 0, 1)):
                        for k in range(2):
                            n_ = 2 * c + k
                            r = mm(bank[b][:, S * k:S * k + S], ysb[:, P * n_:P * n_ + P], selT)
                        r.then_inc(m["scattered"], 1)
                pe.wait_ge(m["summed"], 4 * n + 1)

            def rms_sums(name, n_sq, streams):
                pe.wait_ge(sq_act, n_sq)
                pe.wait_ge(sq_dve, n_sq)
                sqv = W(0, 2, KT, S)
                one_tile(T(name), lambda b: [
                    (b[:, 0:S * streams], ones, sqv[:, 0:streams, k], k == 0, k == KT - 1) for k in range(KT)])

            def head_norms(L):
                n = 10 if L == 2 else 16

                def rotate(i):
                    pe.wait_ge(nrm_q, i + 1)
                    src = wq[:, i, 0] if i < 8 else kraw[:, i - 8, 0]
                    one_tile(RT(i), lambda o: [(o[:, 0:S], K("rot"), src)])

                for i in range(n):
                    width = 512 if L == 2 or i >= 8 else S
                    pe.wait_ge(nsq_done, NB[L] + i + 1)
                    one_tile(NT(L, i), lambda o: [(o[:, 0:width], K("blk64"), nsq(i, width))])
                    if L == 2 and i >= 1:
                        rotate(i - 1)
                if L == 2:
                    rotate(n - 1)

            def attention(L):
                units = UNITS[L]
                for n in range(len(units) + 3):
                    if n < len(units):
                        s, h = units[n]
                        for qb in range(2 if s == 0 else 1):
                            t = T(f"aS{L}.{n}", qb)
                            if L == 2:
                                kp = kpad[:, 2 * (h // 4) + h % 2]
                                if s == 0:
                                    one_tile(t, lambda o: [(o[:, :], wq[:, h // 2, 0, P * qb:P * qb + P], kp)])
                                else:
                                    one_tile(t, lambda o: [(o[:, S * b:S * b + S], wq[:, h // 2, 1, P * b:P * b + P],
                                                            kp[:, S:2 * S]) for b in range(2)])
                            else:
                                one_tile(t, lambda o: [(o[:, :], nq_pad[:, h, P * qb:P * qb + P],
                                                        nk[:, h // 2])])
                    if L == 2 and n < 24 and n % 2 == 0:
                        ada(3, n // 2, n // 2 + 1)
                    if 2 <= n < len(units) + 2:
                        v = n - 2
                        s, h = units[v]
                        for qb in range(2 if s == 0 else 1):
                            t = T(f"aT{L}.{v}", qb)
                            q = next(n_ for n_, e in enumerate(SEQ[L]) if e[0] == v and e[3] == qb)
                            z = zbuf[L][q % 6]
                            pe.wait_ge(soft_p, SB0[L] + q + 1)
                            o = open_tile(t)
                            for kb in range(4):
                                r = pe.transpose(o[:, P * kb:P * kb + P], z[:, P * kb:P * kb + P], ident)
                            r.then_inc(filled[t % 8], 1)
                    if n >= 4 and n % 2 == 0:
                        pair = (n - 4) // 2
                        s = units[2 * pair][0]
                        t = T(f"aO{L}.{pair}")
                        for v in (2 * pair, 2 * pair + 1):
                            is_moved(pe, T(f"aT{L}.{v}"))
                            if s == 0:
                                is_moved(pe, T(f"aT{L}.{v}", 1))
                        calls = []
                        o = B(t)
                        nkb = 4 if s == 0 else 2
                        for kb in range(nkb):
                            for j in range(2):
                                v = 2 * pair + j
                                h = units[v][1]
                                if L == 2:
                                    val = wv[:, kb + (0 if s == 0 else 2), 64 * (h // 4):64 * (h // 4) + 64]
                                else:
                                    val = nv[:, kb, 64 * h:64 * h + 64]
                                calls.append((o[64 * j:64 * j + 64, 0:S], val, pT[:, v % 4, kb], kb == 0, kb == nkb - 1))
                        one_tile(t, lambda o: calls)
                for pair in range(len(units) // 2):
                    is_moved(pe, T(f"aO{L}.{pair}"))

            def ffn(L):
                streams = 2 if L == 2 else 1
                rhs = (lambda k: both(u, k)) if L == 2 else (lambda k: u[:, 0, k])
                width = S * streams
                for g in range(11):
                    project(f"gu{L}.{g}", rhs, width)
                for i in range(8):
                    open_tile(T(f"down{L}", i))
                for g in (9, 10):
                    for i in range(4):
                        is_moved(pe, T(f"gu{L}.{g}", i))
                for i in range(FFT // 2):
                    w = slot(slot0[f"down{L}"] + i)
                    for k in range(2):
                        f = 2 * i + k
                        for c in range(8):
                            t = T(f"down{L}", c)
                            r = mm(B(t)[:, 0:width], w[:, k, P * c:P * c + P], hidden[:, f, 0:streams],
                                   f == 0, f == FFT - 1)
                            if f == FFT - 1:
                                r.then_inc(filled[t % 8], 1)
                            elif k == 1 and c == 7:
                                r.then_inc(down_used, 1)

            def second(L):
                streams = 2 if L == 2 else 1
                rms_sums(f"rms{L}a", RMS_N[L][0], 2)
                pe.wait_ge(u_act, U_N[L][0])
                pe.wait_ge(u_dve, U_N[L][0])
                ru = lambda k: both(u, k)
                if L == 2:
                    for g in range(2):
                        project(f"in2.{g}", ru, 512)
                    w = panel_slots("in2.2")
                    project("in2.2", ru, 512, tiles=2, w=w)
                    project_tokens("in2.2", 2, 256, 512, first_tile=2, w=w)
                    head_norms(2)
                    pe.wait_ge(nrm_done, 10)
                    for kv in range(HKV):
                        for d in range(2):
                            lo = CONST["halves"][0] + 64 + 128 * (kv % 2) - 64 * d
                            one_tile(T("kpad", 2 * kv + d), lambda o: [
                                (o[:, :], const[:, lo:lo + P], kraw[:, kv // 2])])
                    for i in range(8):
                        is_moved(pe, T("kpad", i))
                    for i in range(4):
                        is_moved(pe, T("in2.2", 2 + i))
                else:
                    for g in range(2):
                        project(f"in3.{g}", lambda k: u[:, 0, k], S)
                    for g in (2, 3):
                        project(f"in3.{g}", ru, 512)
                    for g in (4, 5):
                        project_tokens(f"in3.{g}", 2, 0, 512)
                    head_norms(3)
                    pe.wait_ge(nrm_q, 26)
                    for g in (4, 5):
                        for i in range(4):
                            is_moved(pe, T(f"in3.{g}", i))
                attention(L)
                for g in range(2):
                    project(f"out{L}.{g}", (lambda k: both(u, k)) if L == 2 else (lambda k: u[:, 0, k]), S * streams)
                if L == 2:
                    ada_sums(3, "a")
                    ada_sums(3, "b")
                rms_sums(f"rms{L}b", RMS_N[L][1], streams)
                pe.wait_ge(u_act, U_N[L][1])
                pe.wait_ge(u_dve, U_N[L][1])
                ffn(L)

            pe.wait_ge(const_in, 32)
            pe.wait_ge(first_in, 32)
            even()
            if last_stage >= 2:
                routing(0)
                experts(0)
                ln_sums("ln0b", 2)
            if last_stage >= 3:
                odd()
            if last_stage >= 4:
                routing(1)
                experts(1)
                ln_sums("ln1b", 4)
            if last_stage >= 5:
                second(2)
            if last_stage >= 7:
                second(3)

        @block.scalar
        def _(act):
            def f(o, i, func, **kw):
                return act.activation(o, i, func, **kw)

            cnt = {"std": 0, "cent": 0, "x": 0, "u": 0}

            def deviation(tile, o, width, n, eps):
                is_filled(act, tile)
                f(o, B(tile)[:, 0:width], ACT.Sqrt, scale=1.0 / n, bias=K(eps)).then_inc(moved[tile % 8], 1)

            def layer_norm(name, which, L):
                cnt["cent"] += 1
                act.wait_ge(cent_done, cnt["cent"])
                f(X(0, 4, S), x[:, 0:4], ACT.Square).then_inc(sq_act, 1)
                deviation(T(name, 1), X(2048, S), S, D, "eps_ln")
                cnt["cent"] += 1
                act.wait_ge(cent_done, cnt["cent"])
                for k in range(4):
                    f(x[:, k], x[:, k], ACT.Identity, scale=C(f"ln{which}_g", KT * L + k, 1),
                      bias=C(f"ln{which}_b", KT * L + k, 1)).then_inc(x_act, 1)
                cnt["x"] += 4

            def modulate(L, half):
                act.wait_ge(mod_done, 2 * L + 1 + half)
                if L or half:
                    act.wait_ge(x_act, cnt["x"])
                for k in range(4):
                    f(u[:, 0, k], x[:, k], ACT.Identity, scale=mod[:, L, 24 * half + 8 + k, 0:1],
                      bias=mod[:, L, 24 * half + k, 0:1]).then_inc(u_act, 1)
                cnt["u"] += 4

            def scale_residual():
                act.wait_ge(u_dve, cnt["u"])
                f(x, x, ACT.Copy, scale=ALPHA).then_inc(xs_done, 1)

            def copy_tile(t, o, width, func=ACT.Copy, **kw):
                is_filled(act, t)
                f(o, B(t)[:, 0:width], func, **kw).then_inc(moved[t % 8], 1)

            def pad_heads(t, o0, o1_):
                is_filled(act, t)
                f(o0, B(t)[:, 0:S], ACT.Identity, scale=K("halfcol")[:, 0:1])
                f(o1_, B(t)[:, 0:S], ACT.Identity, scale=K("halfcol")[:, 1:2]).then_inc(moved[t % 8], 1)

            def even():
                modulate(0, 0)
                for i in range(4):
                    pad_heads(T("even.0", i), sq_pad[:, 2 * i], sq_pad[:, 2 * i + 1])
                scale_residual()
                for i in range(4):
                    copy_tile(T("even.4", i), rk[:, i], S, scale=128 ** -0.5)
                for i in range(2):
                    copy_tile(T("even.5", i), rv[:, i], 512)
                for i in range(4):
                    copy_tile(T("even.6", i), rg[:, i], S, ACT.Silu)
                for b in range(2):
                    act.wait_ge(sb_d, b + 1)
                    f(sb_l, sb_l, ACT.Exp).then_inc(chain_a, 1)
                    act.wait_ge(chain_a, b + 1)
                    f(sb_l, sb_l, ACT.Ln, bias=K("one")).then_inc(sb_e, 1)
                    act.wait_ge(sb_a, b + 1)
                    f(sb_l, sb_z, ACT.Exp).then_inc(sb_w, 1)
                    for i in range(2):
                        copy_tile(T(f"sbO{b}", i), o1[:, 2 * b + i], S)
                for h in range(2):
                    deviation(T("retV", h), X(512 * h, 512), 512, P, "eps_ln")
                layer_norm("ln0a", 1, 0)

            def odd():
                modulate(1, 0)
                for g in range(2):
                    for i in range(4):
                        t = 4 * g + i
                        pad_heads(T(f"odd.{g}", i), dq_pad[:, 2 * t], dq_pad[:, 2 * t + 1])
                scale_residual()
                for i in range(2):
                    copy_tile(T("odd.4", i), dv[:, i, 0:512], 512)
                copy_tile(T("lam"), tiny[:, 2:4], 2, ACT.Exp)
                for n in range(DIFF_HEADS + 4):
                    if n < DIFF_HEADS:
                        act.wait_ge(soft_z, n + 1)
                        sm = tiny[:, 16 + 16 * (n % 2):32 + 16 * (n % 2)]
                        for m in range(2):
                            for qb, (lo, hi) in enumerate(((0, 128), (128, 384))):
                                c = 2 * m + qb
                                z = dz3[n % 3][:, m, lo:hi]
                                r = f(z, z, ACT.Exp, bias=sm[:, 4 + c:5 + c], accum_out=sm[:, 8 + c:9 + c])
                        r.then_inc(soft_e, 1)
                    if 2 <= n < DIFF_HEADS + 2:
                        h = n - 2
                        if h >= 2:
                            is_filled(act, T(f"dO{h - 2}"))
                        copy_tile(T(f"dT{h}"), daT[:, h % 2], 384)
                    if n >= 4:
                        copy_tile(T(f"dO{n - 4}"), o1[:, n - 4], S)
                for i in range(4):
                    deviation(T("dV", i), dr[:, 2 * i:2 * i + 2], 512, P, "eps_ln")
                layer_norm("ln1a", 1, 1)

            def experts(l):
                m = moe[l]
                modulate(l, 1)
                act.wait_ge(route_dve, 3 * l + 2)
                f(route[:, R_EXP:R_EXP + 10], route[:, R_EXP:R_EXP + 10], ACT.Exp).then_inc(route_act, 1)
                for i in range(2):
                    copy_tile(T(f"route{l}", 1 + i), xnat[:, 0, 512 * i:512 * i + 512], 512)
                is_filled(act, T(f"route{l}", 4))
                scale_residual()
                for i in range(2):
                    copy_tile(T(f"route{l}", 6 + i), drow[:, 2 * i:2 * i + 2], 512)
                act.wait_ge(info_done, l + 1)
                n = act.value_load(info[0:1, 0:1], min_val=0, max_val=MAX_GROUPS - 1) + 1
                with act.Fori(0, n) as i:
                    act.wait_ge(m["gathered"], 2 * i + 1)
                    for k in range(4):
                        f(xg[:, k], bank[0][:, P * k:P * k + P], ACT.Identity, scale=mod[:, l, 32 + k, 0:1],
                          bias=mod[:, l, 24 + k, 0:1]).then_inc(m["xg_by_act"], 1)
                    act.wait_ge(m["phase"], 6 * i + 2)
                    f(sil, bank[2][:, :], ACT.Silu).then_inc(m["silu"], 1)
                    act.wait_ge(m["turned"], i + 1)
                    f(hidT.rearrange("p a b -> p (a b)"), bank[4][:, :], ACT.Copy).then_inc(m["turned_out"], 1)
                    act.wait_ge(m["phase"], 6 * i + 6)
                    f(ysb[:, 0:512], bank[5][:, :], ACT.Copy).then_inc(m["y_by_act"], 1)
                layer_norm(f"ln{l}b", 2, l)

            def rms(L, half, streams, name):
                if half == 1:
                    for g in range(2):
                        for i in range(4):
                            is_moved(act, T(f"out{L}.{g}", i))
                elif L == 2:
                    act.wait_ge(second_in, 16)
                    act.wait_ge(x_act, 16)
                    act.wait_ge(x_dve, 16)
                else:
                    for i in range(8):
                        is_moved(act, T("down2", i))
                sqv = W(0, 2, KT, S)
                if streams == 2:
                    f(sqv[:, 0], res[:, 0], ACT.Square).then_inc(sq_act, 1)
                else:
                    f(sqv[:, 0, 0:4], res[:, 0, 0:4], ACT.Square).then_inc(sq_act, 1)
                deviation(T(name), X(0, S * streams), S * streams, D, "eps_rms")
                cnt["cent"] += 1
                act.wait_ge(cent_done, cnt["cent"])
                act.wait_ge(mod_done, 2 * L + 1 + half)
                for k in range(KT if streams == 2 else 4):
                    f(u[:, 0, k], u[:, 0, k], ACT.Identity, scale=mod[:, L, 24 * half + 8 + k, 0:1],
                      bias=mod[:, L, 24 * half + k, 0:1]).then_inc(u_act, 1)

            def head_norms(L):
                n = 10 if L == 2 else 16

                def square(i):
                    if L == 3 and i < 8:
                        src, width = nq_pad[:, 2 * i], S
                        is_moved(act, T(f"in3.{i // 4}", i % 4))
                    elif L == 3:
                        src, width = nk[:, i - 8], 512
                        is_moved(act, T(f"in3.{i // 4}", i % 4))
                    else:
                        src, width = (wq[:, i] if i < 8 else kraw[:, i - 8]), 512
                        is_moved(act, T(f"in2.{i // 4}", i % 4))
                    if i >= 2:
                        is_filled(act, NT(L, i - 2))
                    f(nsq(i, width), src, ACT.Square).then_inc(nsq_done, 1)

                square(0)
                for i in range(n):
                    if i + 1 < n:
                        square(i + 1)
                    width = S if L == 3 and i < 8 else 512
                    if i >= 2:
                        act.wait_ge(nrm_q, NB[L] + i - 1)
                    deviation(NT(L, i), X(2048 + 512 * (i % 2), width), width, 64, "eps_rms")

            def attention(L):
                seqs = SEQ[L]

                def exps(q):
                    v, s, h, qb, tS, tT = seqs[q]
                    act.wait_ge(soft_z, SB0[L] + q + 1)
                    sm = tiny[:, 16 + 16 * (q % 4):32 + 16 * (q % 4)]
                    z = zbuf[L][q % 6]
                    if s == 0:
                        f(z[:, S:2 * S], B(tS)[:, S:2 * S], ACT.Exp, bias=sm[:, 4:5],
                          accum_out=sm[:, 6:7]).then_inc(moved[tS % 8], 1)
                        if L == 2:
                            f(sm[:, 8:9], C("sink", h, 1), ACT.Exp, bias=sm[:, 4:5])
                        f(z[:, 0:S], z[:, 0:S], ACT.Exp, bias=sm[:, 4:5], accum_out=sm[:, 7:8]).then_inc(soft_e, 1)
                    else:
                        for b in range(2):
                            r = f(z[:, S * b:S * b + S], B(tS)[:, S * b:S * b + S], ACT.Exp, bias=sm[:, 4 + b:5 + b],
                                  accum_out=sm[:, 6 + b:7 + b])
                        r.then_inc(moved[tS % 8], 1)
                        f(sm[:, 8:10], sm[:, 4:6], ACT.Exp, bias=C("sink", h, 1)).then_inc(soft_e, 1)

                def turned(q):
                    v, s, h, qb, tS, tT = seqs[q]
                    if v >= 4:
                        is_filled(act, T(f"aO{L}.{(v - 4) // 2}"))
                    if s == 0:
                        copy_tile(tT, pT[:, v % 4, :, P * qb:P * qb + P], 512)
                    else:
                        for b in range(2):
                            is_filled(act, tT)
                            r = f(pT[:, v % 4, 0:2, P * b:P * b + P], B(tT)[:, S * b:S * b + S], ACT.Copy)
                        r.then_inc(moved[tT % 8], 1)

                for n in range(len(UNITS[L]) + 2):
                    for q, e in enumerate(seqs):
                        if e[0] == n:
                            exps(q)
                    for q, e in enumerate(seqs):
                        if e[0] == n - 2:
                            turned(q)

            def second(L):
                rms(L, 0, 2, f"rms{L}a")
                if L == 2:
                    for i in range(8):
                        copy_tile(T(f"in2.{i // 4}", i % 4), wq[:, i], 512)
                    for i in range(2):
                        copy_tile(T("in2.2", i), kraw[:, i], 512)
                    head_norms(2)
                    for i in range(0, 8, 2):
                        copy_tile(T("kpad", i), kpad[:, i], 512)
                else:
                    for i in range(8):
                        copy_tile(T(f"in3.{i // 4}", i % 4), nq_pad[:, 2 * i], S)
                    for i in range(4):
                        copy_tile(T("in3.4", i), nv[:, i, 0:512], 512)
                    head_norms(3)
                attention(L)
                streams = 2 if L == 2 else 1
                rms(L, 1, streams, f"rms{L}b")
                for n in range(FFT):
                    copy_tile(T(f"gu{L}.{n // 4}", n % 4), hidden[:, n, 0:streams], S * streams, ACT.Silu)

            act.dma_start(cols[:, :], a["cols"]).then_inc(const_in, 16)
            act.dma_start(const[:, :], a["const"]).then_inc(const_in, 16)
            act.dma_start(x, a["x"]).then_inc(first_in, 16)
            act.dma_start(first, a["first"]).then_inc(first_in, 16)
            act.wait_ge(const_in, 32)
            f(cond[:, :], cols[:, 0:24], ACT.Silu).then_inc(cond_done, 1)
            act.wait_ge(first_in, 32)
            even()
            if last_stage >= 2:
                experts(0)
            if last_stage >= 3:
                odd()
            if last_stage >= 4:
                experts(1)
            if last_stage >= 5:
                second(2)
            if last_stage >= 7:
                second(3)

        @block.vector
        def _(dve):
            cnt = {"chain": 0, "cent": 0, "x": 0, "u": 0, "xs": 0}

            def step(ins):
                cnt["chain"] += 1
                ins.then_inc(chain_v, 1)
                dve.wait_ge(chain_v, cnt["chain"])

            tt, ts, stt = dve.tensor_tensor, dve.tensor_scalar, dve.scalar_tensor_tensor

            def ada(L, g0, g1):
                for g in range(g0, g1):
                    t = T(f"ada{L}.{g}")
                    if L or g:
                        dve.wait_ge(chain_adac, 12 * L + g)
                    is_filled(dve, t)
                    dve.transpose(adaT[:, :], B(t)[:, :]).then_inc(moved[t % 8], 1)
                    is_moved(dve, t)
                    v = adaT[:, :].rearrange("p (a q c r) -> p q a c r", a=4, q=4, c=2)
                    for c in range(2):
                        r = dve.tensor_copy(adac[:, :, 4 * g:4 * g + 4, c], v[:, :, :, c, 0])
                    r.then_inc(chain_adac, 1)

            def ada_sums(L, part):
                t = T(f"adafin{L}{part}")
                a0, a1 = (0, 16) if part == "a" else (16, 48)
                is_filled(dve, t)
                bias = C("b_ada", 48 * L + a0, a1 - a0).unsqueeze(2).broadcast_to([P, a1 - a0, 2])
                tt(mod[:, L, a0:a1], B(t)[:, 0:2 * (a1 - a0)].rearrange("p (a c) -> p a c", c=2), bias,
                   ALU.add).then_inc(moved[t % 8], 1)
                is_moved(dve, t)
                if L < 2 and part == "b":
                    ts(mod[:, L, 16:24], mod[:, L, 16:24], 1.0, None, ALU.add)
                at, name = (8, "g_mix") if part == "a" else (32, "g_ffn")
                if L < 2:
                    n = 8 if part == "a" else 16
                    r = ts(mod[:, L, at:at + n], mod[:, L, at:at + n], 1.0, None, ALU.add)
                else:
                    g = C(name, KT * (L - 2), KT).unsqueeze(2).broadcast_to([P, KT, 2])
                    r = stt(mod[:, L, at:at + 8], mod[:, L, at:at + 8], 1.0, g, ALU.add, ALU.mult)
                r.then_inc(mod_done, 1)
                dve.wait_ge(mod_done, 2 * L + (1 if part == "a" else 2))

            def modulate(L, half):
                if L or half:
                    dve.wait_ge(x_dve, cnt["x"])
                for k in range(4, 8):
                    ts(u[:, 0, k], x[:, k], mod[:, L, 24 * half + 8 + k, 0:1], mod[:, L, 24 * half + k, 0:1],
                       ALU.mult, ALU.add).then_inc(u_dve, 1)
                cnt["u"] += 4

            def copy_tile(t, o, width):
                is_filled(dve, t)
                dve.tensor_copy(o, B(t)[:, 0:width]).then_inc(moved[t % 8], 1)

            def layer_norm(name, which, L):
                t = T(name)
                dve.wait_ge(res_ready, res_n["dve"])
                is_filled(dve, t)
                mean = B(t)[:, 0:S].unsqueeze(1).broadcast_to([P, KT, S])
                stt(x, mean, -1.0 / D, x, ALU.mult, ALU.add).then_inc(cent_done, 1)
                cnt["cent"] += 1
                dve.wait_ge(cent_done, cnt["cent"])
                tt(X(1024, 4, S), x[:, 4:8], x[:, 4:8], ALU.mult).then_inc(sq_dve, 1)
                is_moved(dve, T(name, 1))
                dve.tensor_copy(tiny[:, 90:91], tiny[:, 91:92]).then_inc(moved[t % 8], 1)
                step(dve.reciprocal(X(2304, S), X(2048, S)))
                tt(x, x, X(2304, S).unsqueeze(1).broadcast_to([P, KT, S]), ALU.mult).then_inc(cent_done, 1)
                cnt["cent"] += 1
                dve.wait_ge(cent_done, cnt["cent"])
                for k in range(4, 8):
                    ts(x[:, k], x[:, k], C(f"ln{which}_g", KT * L + k, 1), C(f"ln{which}_b", KT * L + k, 1),
                       ALU.mult, ALU.add).then_inc(x_dve, 1)
                cnt["x"] += 4

            res_n = {"dve": 0}

            def add_mixer(L):
                cnt["xs"] += 1
                dve.wait_ge(xs_done, cnt["xs"])
                for g in range(2):
                    for i in range(4):
                        t, k = T(f"out{L}.{g}", i), 4 * g + i
                        is_filled(dve, t)
                        stt(x[:, k], B(t)[:, 0:S], mod[:, L, 16 + k, 0:1], x[:, k], ALU.mult,
                            ALU.add).then_inc(moved[t % 8], 1)
                for i in range(4):
                    is_moved(dve, T(f"out{L}.1", i))
                    is_moved(dve, T(f"out{L}.0", i))
                dve.tensor_copy(tiny[:, 90:91], tiny[:, 91:92]).then_inc(res_ready, 1)
                res_n["dve"] += 1

            def even():
                dve.memset(tiny[:, :], 0.0).then_inc(chain_v, 1)
                cnt["chain"] += 1
                dve.wait_ge(chain_v, cnt["chain"])
                dve.wait_ge(cond_done, 1)
                dve.tensor_copy(condrep[:, :, :], cond[:, 0:8].unsqueeze(2).broadcast_to([P, KT, 32]))\
                   .then_inc(condrep_done, 1)
                dve.wait_ge(const_in, 32)
                dve.wait_ge(first_in, 32)
                ada(0, 0, 4)
                ada_sums(0, "a")
                modulate(0, 0)
                ada(0, 4, 5)
                for i in range(4):
                    copy_tile(T("even.1", i), sk[:, i], S)
                ada(0, 5, 6)
                for i in range(2):
                    copy_tile(T("even.2", i), sv[:, i], 512)
                ada(0, 6, 7)
                for i in range(4):
                    copy_tile(T("even.3", i), rq[:, i], S)
                ada(0, 7, 12)
                ada_sums(0, "b")
                for b in range(2):
                    if b:
                        is_filled(dve, T("sbO0", 1))
                    for i in range(4):
                        t = T(f"sbS{b}", i)
                        is_filled(dve, t)
                        tt(sb_z[:, i], B(t)[:, 0:384], K("sbmask"), ALU.add).then_inc(moved[t % 8], 1)
                    for i in range(4):
                        is_moved(dve, T(f"sbS{b}", i))
                    step(ts(sb_t, sb_z, 0.0, None, ALU.max))
                    stt(sb_l, sb_t, -2.0, sb_z, ALU.mult, ALU.add).then_inc(sb_d, 1)
                    ada(1, 4 * b, 4 * b + 3)
                    dve.wait_ge(sb_e, b + 1)
                    tt(sb_l, sb_l, sb_t, ALU.add).then_inc(sb_sp, 1)
                    for i in range(4):
                        t = T(f"sbR{b}", i)
                        is_filled(dve, t)
                        tt(sb_z[:, i], sb_z[:, i], B(t)[:, 0:384], ALU.subtract).then_inc(moved[t % 8], 1)
                    for i in range(4):
                        is_moved(dve, T(f"sbR{b}", i))
                    dve.tensor_copy(tiny[:, 90:91], tiny[:, 91:92]).then_inc(sb_a, 1)
                    ada(1, 4 * b + 3, 4 * b + 4)
                for h in range(4):
                    t = T("retS", h)
                    is_filled(dve, t)
                    tt(ret_p[:, h], B(t)[:, 0:384], decay[:, h], ALU.mult).then_inc(moved[t % 8], 1)
                is_filled(dve, T("sbO1", 1))
                ada(1, 8, 9)
                for h in range(4):
                    copy_tile(T("retO", h), ret_o[:, h], S)
                for h in range(2):
                    t = T("retM", h)
                    is_filled(dve, t)
                    v = ret_o[:, 2 * h:2 * h + 2]
                    stt(v, B(t)[:, :].rearrange("p (a s) -> p a s", a=2), -1.0 / P, v, ALU.mult,
                        ALU.add).then_inc(moved[t % 8], 1)
                    is_moved(dve, t)
                    r = tt(ret_s[:, 2 * h:2 * h + 2], v, v, ALU.mult)
                r.then_inc(ret_done, 1)
                ada(1, 9, 10)
                for h in range(2):
                    is_moved(dve, T("retV", h))
                step(dve.reciprocal(X(0, 1024), X(0, 1024)))
                step(tt(ret_o, ret_o, X(0, 4, S), ALU.mult))
                for h in range(4):
                    is_moved(dve, T("even.6", h))
                    r = stt(o1[:, 4 + h], ret_o[:, h], C("ret_g", h, 1), rg[:, h], ALU.mult, ALU.mult)
                r.then_inc(o_done, 1)
                ada(1, 10, 12)
                add_mixer(0)
                ada_sums(1, "a")
                ada_sums(1, "b")
                layer_norm("ln0a", 1, 0)

            def odd():
                dve.tensor_copy(condrep[:, :, 0:16], cond[:, 8:16].unsqueeze(2).broadcast_to([P, KT, 16]))
                dve.tensor_copy(condrep[:, :, 16:32], cond[:, 16:24].unsqueeze(2).broadcast_to([P, KT, 16]))\
                   .then_inc(condrep_done, 1)
                modulate(1, 0)
                tt(tiny[:, 0:2], C("lam", 0, 2), C("lam", 2, 2), ALU.mult).then_inc(lam_p, 1)
                ts(tiny[:, 6:7], C("subln"), 1.0 - LAMBDA_INIT, None, ALU.mult)
                for g in (2, 3):
                    for i in range(4):
                        copy_tile(T(f"odd.{g}", i), dk[:, 4 * (g - 2) + i], S)
                for i in range(2):
                    copy_tile(T("odd.5", i), dv[:, i, 512:1024], 512)
                is_moved(dve, T("lam"))
                step(tt(tiny[:, 4:5], tiny[:, 3:4], tiny[:, 2:3], ALU.subtract))
                step(ts(tiny[:, 5:6], tiny[:, 4:5], -LAMBDA_INIT, None, ALU.add))
                for n in range(DIFF_HEADS + 2):
                    if n < DIFF_HEADS:
                        sm = tiny[:, 16 + 16 * (n % 2):32 + 16 * (n % 2)]
                        for m in range(2):
                            t = T(f"dS{n}", m)
                            is_filled(dve, t)
                            stt(dz3[n % 3][:, m], dist, -(2.0 ** -(n + 1)), B(t)[:, 0:384], ALU.mult,
                                ALU.add).then_inc(moved[t % 8], 1)
                        is_moved(dve, T(f"dS{n}", 0))
                        is_moved(dve, T(f"dS{n}", 1))
                        mx = sm[:, 0:4].rearrange("p (m q) -> p m q", m=2)
                        dve.tensor_reduce(mx[:, :, 0], dz3[n % 3][:, :, 0:128], AX_X, ALU.max)
                        step(dve.tensor_reduce(mx[:, :, 1], dz3[n % 3][:, :, 128:384], AX_X, ALU.max))
                        ts(sm[:, 4:8], sm[:, 0:4], -1.0, None, ALU.mult).then_inc(soft_z, 1)
                    if 1 <= n <= DIFF_HEADS:
                        h = n - 1
                        sm = tiny[:, 16 + 16 * (h % 2):32 + 16 * (h % 2)]
                        dve.wait_ge(soft_e, n)
                        step(dve.reciprocal(sm[:, 12:16], sm[:, 8:12]))
                        step(ts(sm[:, 14:16], sm[:, 14:16], tiny[:, 5:6], None, ALU.mult))
                        for qb, (lo, hi) in enumerate(((0, 128), (128, 384))):
                            r = ts(dz3[h % 3][:, 1, lo:hi], dz3[h % 3][:, 1, lo:hi], sm[:, 14 + qb:15 + qb], None, ALU.mult)
                        step(r)
                        if h >= 2:
                            is_filled(dve, T(f"dT{h - 2}"))
                        for qb, (lo, hi) in enumerate(((0, 128), (128, 384))):
                            r = stt(da[:, h % 2, lo:hi], dz3[h % 3][:, 0, lo:hi], sm[:, 12 + qb:13 + qb],
                                    dz3[h % 3][:, 1, lo:hi], ALU.mult, ALU.add)
                        r.then_inc(soft_p, 1)
                    ada(2, n, n + 1)
                for h in range(DIFF_HEADS):
                    is_moved(dve, T(f"dO{h}"))
                tt(dsq, o1, o1, ALU.mult).then_inc(ret_done, 1)
                for i in range(4):
                    is_moved(dve, T("dV", i))
                step(dve.reciprocal(dr, dr))
                stt(o1, o1, tiny[:, 6:7], dr, ALU.mult, ALU.mult).then_inc(o_done, 1)
                ada(2, 10, 12)
                add_mixer(1)
                ada_sums(2, "a")
                ada_sums(2, "b")
                layer_norm("ln1a", 1, 1)

            def routing(l):
                at = {"n": R_SMALL}

                def new(*dims):
                    n = int(np.prod(dims))
                    v = route[:, at["n"]:at["n"] + n]
                    at["n"] += n
                    assert at["n"] <= 2048
                    if len(dims) == 1:
                        return v
                    names = "abcd"[:len(dims)]
                    return v.rearrange(f"p ({' '.join(names)}) -> p {' '.join(names)}", **dict(zip(names, dims)))

                def wide(v, n):
                    return v.unsqueeze(2).broadcast_to([P, 2, n])

                def first_of(v, top, n, out_index, eq):
                    step(tt(eq, v, wide(top, n), ALU.is_equal))
                    step(stt(eq, eq, -1000.0, iota_of(n), ALU.mult, ALU.add))
                    step(dve.tensor_reduce(out_index, eq, AX_X, ALU.min))
                    step(ts(out_index, out_index, 1000.0, None, ALU.add))

                def iota_of(n):
                    return K("iota")[:, 0:n].unsqueeze(1).broadcast_to([P, 2, n])

                t = T(f"route{l}")
                is_filled(dve, t)
                lg = new(2, 36)
                step_sem = B(t)[:, 0:72].rearrange("p (a b) -> p a b", a=2)
                bias = C("b_route", 36 * l, 36).unsqueeze(1).broadcast_to([P, 2, 36])
                tt(lg, step_sem, bias, ALU.add).then_inc(moved[t % 8], 1)
                is_moved(dve, t)
                gl = lg[:, :, 0:4]
                gmax, grp, eq4, g1h = new(2), new(2), new(2, 4), new(2, 4)
                step(dve.tensor_reduce(gmax, gl, AX_X, ALU.max))
                ex = route[:, R_EXP:R_EXP + 10].rearrange("p (a b) -> p a b", a=2)
                tt(ex[:, :, 0:4], gl, wide(gmax, 4), ALU.subtract)
                first_of(gl, gmax, 4, grp, eq4)
                step(tt(g1h, iota_of(4), wide(grp, 4), ALU.is_equal))
                pick, ing, eq8 = new(2, 4, 8), new(2, 8), new(2, 8)
                for tb in range(2):
                    r = tt(pick[:, tb], lg[:, tb, 4:36].rearrange("p (g e) -> p g e", g=4),
                           g1h[:, tb].unsqueeze(2).broadcast_to([P, 4, 8]), ALU.mult)
                step(r)
                for tb in range(2):
                    r = dve.tensor_reduce(ing[:, tb], pick[:, tb].rearrange("p g e -> p e g"), AX_X, ALU.add)
                step(r)
                top, idx, rest = new(2, 2), new(2, 2), new(2, 8)
                step(dve.tensor_reduce(top[:, 0], ing, AX_X, ALU.max))
                first_of(ing, top[:, 0], 8, idx[:, 0], eq8)
                step(tt(eq8, iota_of(8), wide(idx[:, 0], 8), ALU.is_equal))
                step(stt(rest, eq8, NEG, ing, ALU.mult, ALU.add))
                step(dve.tensor_reduce(top[:, 1], rest, AX_X, ALU.max))
                first_of(rest, top[:, 1], 8, idx[:, 1], eq8)
                tt(ex[:, :, 4], top[:, 1], top[:, 0], ALU.subtract)
                eid, hot, ch = new(2, 2), new(2, 2, 32), route[:, R_CH:R_CH + 64].rearrange("p (a b) -> p a b", a=2)
                for c in range(2):
                    r = stt(eid[:, c], grp, float(PER_GROUP), idx[:, c], ALU.mult, ALU.add)
                step(r)
                for c in range(2):
                    r = tt(hot[:, c], iota_of(32), wide(eid[:, c], 32), ALU.is_equal)
                step(r)
                tt(ch, hot[:, 0], hot[:, 1], ALU.add).then_inc(route_dve, 1)
                t = T(f"route{l}", 5)
                is_filled(dve, t)
                rank = new(96)
                dve.tensor_copy(rank, B(t)[:, 0:96]).then_inc(moved[t % 8], 1)
                is_moved(dve, t)
                over, nblk, end, zero32 = W(5120, 32, 8), new(32), new(32), new(32)
                dve.memset(zero32, 0.0)
                step(tt(over, rank[:, 64:96].unsqueeze(2).broadcast_to([P, 32, 8]),
                        K("thresh").unsqueeze(1).broadcast_to([P, 32, 8]), ALU.is_gt))
                step(dve.tensor_reduce(nblk, over, AX_X, ALU.add))
                step(tt(nblk, nblk, K("lead"), ALU.subtract))
                step(ts(nblk, nblk, 0.0, None, ALU.max))
                step(dve.tensor_tensor_scan(end, nblk, zero32, 0.0, ALU.add, ALU.add))
                start = new(32)
                step(tt(start, end, nblk, ALU.subtract))
                step(ts(end, end, float(GRP), None, ALU.add))
                base, lower = new(32), new(32)
                step(tt(base, start, K("lead"), ALU.subtract))
                step(ts(base, base, float(GRP), float(BLK), ALU.add, ALU.mult))
                step(stt(lower, K("iota")[:, 0:32], float(BLK), base, ALU.mult, ALU.subtract))
                step(tt(lower, lower, K("lead"), ALU.mult))
                slots, in_lead, hs = new(2, 32), W(6144, 2, 32), W(5632, 2, 2, 32)
                rank2 = rank[:, 0:64].rearrange("p (a b) -> p a b", a=2)
                step(ts(in_lead, rank2, float(BLK), None, ALU.is_lt))
                step(tt(in_lead, in_lead, lower.unsqueeze(1).broadcast_to([P, 2, 32]), ALU.mult))
                step(tt(slots, rank2, base.unsqueeze(1).broadcast_to([P, 2, 32]), ALU.add))
                step(tt(slots, slots, in_lead, ALU.add))
                for c in range(2):
                    r = tt(hs[:, c], hot[:, c], slots, ALU.mult)
                step(r)
                step(dve.tensor_reduce(dest, hs, AX_X, ALU.add))
                tb_ = W(5120, MAX_BLOCKS, 32)
                fl = W(9472 + R_BC, 64)
                step(tt(tb_[0:1], end[0:1].unsqueeze(1).broadcast_to([1, MAX_BLOCKS, 32]),
                        K("iota")[0:1, 0:MAX_BLOCKS].unsqueeze(2).broadcast_to([1, MAX_BLOCKS, 32]), ALU.is_le))
                step(dve.tensor_reduce(fl[0:1, 1:1 + MAX_BLOCKS], tb_[0:1], AX_X, ALU.add))
                step(ts(fl[0:1, 1:1 + MAX_BLOCKS], fl[0:1, 1:1 + MAX_BLOCKS], float(N_EXPERTS - 1), 1.0, ALU.min, ALU.add))
                step(dve.tensor_copy(fl[0:1, 1:1 + GRP], K("iota")[0:1, 1:1 + GRP]))
                step(tt(tb_[0:1, 0, 0:MAX_GROUPS], end[0:1, 31:32].broadcast_to([1, MAX_GROUPS]), K("gthresh")[0:1],
                        ALU.is_gt))
                step(dve.tensor_reduce(fl[0:1, 0:1], tb_[0:1, 0, 0:MAX_GROUPS], AX_X, ALU.add))
                dve.tensor_copy(info[0:1, 0:INFO], fl[0:1, 0:INFO]).then_inc(info_done, 1)
                dve.tensor_copy(tiny[:, 90:91], tiny[:, 91:92]).then_inc(route_dve, 1)
                dve.wait_ge(route_act, l + 1)
                den, gate = new(2, 2), new(2, 2)
                step(dve.tensor_reduce(den[:, 0], ex[:, :, 0:4], AX_X, ALU.add))
                step(ts(den[:, 1], ex[:, :, 4], 1.0, None, ALU.add))
                step(tt(den[:, 0], den[:, 0], den[:, 1], ALU.mult))
                step(dve.reciprocal(gate[:, 0], den[:, 0]))
                step(tt(gate[:, 1], gate[:, 0], ex[:, :, 4], ALU.mult))
                bc = route[:, R_BC:R_BC + 1024].rearrange("p (a b) -> p a b", b=P)
                dve.wait_ge(info_done, l + 1)
                for c in range(2):
                    for tb in range(2):
                        ts(bc[:, 2 * c + tb], ones, dest[:, c, tb:tb + 1], None, ALU.mult)
                        r = ts(bc[:, 4 + 2 * c + tb], ones, gate[:, c, tb:tb + 1], None, ALU.mult)
                r.then_inc(route_dve, 1)

            def experts(l):
                m = moe[l]
                modulate(l, 1)
                routing(l)
                for i in range(2):
                    copy_tile(T(f"route{l}", 3 + i), xnat[:, 1, 512 * i:512 * i + 512], 512)
                dve.memset(acc, 0.0).then_inc(m["summed"], 1)
                step(dve.tensor_copy(slotcol, K("pid")))
                for i in range(2):
                    is_moved(dve, T(f"route{l}", 6 + i))

                def select(first):
                    for tb in range(2):
                        r = ts(sel[:, tb], K("iota"), dest[:, 0, tb:tb + 1], None, ALU.is_equal)
                    r.then_inc(m["step"], 1)

                def select2():
                    for tb in range(2):
                        r = stt(sel[:, tb], K("iota"), dest[:, 1, tb:tb + 1], sel[:, tb], ALU.is_equal, ALU.add)
                    r.then_inc(m["selected"], 1)

                select(True)
                dve.wait_ge(m["step"], 1)
                select2()
                n = dve.value_load(info[0:1, 0:1], min_val=0, max_val=MAX_GROUPS - 1) + 1
                STEPS = 3
                with dve.Fori(0, n) as i:
                    stt(selT, drow[:, 0], slotcol, drow[:, 2], ALU.is_equal, ALU.mult)
                    stt(selT2, drow[:, 1], slotcol, drow[:, 3], ALU.is_equal, ALU.mult).then_inc(m["step"], 1)
                    dve.wait_ge(m["step"], STEPS * i + 2)
                    tt(selT, selT, selT2, ALU.add).then_inc(m["spread_ready"], 1)
                    dve.wait_ge(m["gathered"], 2 * i + 2)
                    for k in range(4, 8):
                        ts(xg[:, k], bank[1][:, P * (k - 4):P * (k - 4) + P], mod[:, l, 32 + k, 0:1],
                           mod[:, l, 24 + k, 0:1], ALU.mult, ALU.add).then_inc(m["xg_by_dve"], 1)
                    ts(slotcol, slotcol, float(P), None, ALU.add)
                    ts(dest, dest, -float(P), None, ALU.add).then_inc(m["step"], 1)
                    dve.wait_ge(m["step"], STEPS * i + 3)
                    select(False)
                    dve.wait_ge(m["step"], STEPS * i + 4)
                    select2()
                    dve.wait_ge(m["silu"], i + 1)
                    dve.wait_ge(m["phase"], 6 * i + 4)
                    tt(hid, sil, bank[3][:, :], ALU.mult).then_inc(m["hidden"], 1)
                    dve.wait_ge(m["phase"], 6 * i + 6)
                    dve.tensor_copy(ysb[:, 512:1024], bank[6][:, :]).then_inc(m["y_by_dve"], 1)
                    for c, b in enumerate((7, 4, 0, 1)):
                        dve.wait_ge(m["scattered"], 4 * i + c + 1)
                        v = acc[:, 2 * c:2 * c + 2]
                        tt(v, v, bank[b][:, :].rearrange("p (a s) -> p a s", a=2), ALU.add).then_inc(m["summed"], 1)
                cnt["xs"] += 1
                dve.wait_ge(m["summed"], 4 * n + 1)
                dve.wait_ge(xs_done, cnt["xs"])
                for k in range(KT):
                    r = stt(x[:, k], acc[:, k], mod[:, l, 40 + k, 0:1], x[:, k], ALU.mult, ALU.add)
                r.then_inc(res_ready, 1)
                res_n["dve"] += 1
                layer_norm(f"ln{l}b", 2, l)

            def rms(L, half, streams, name):
                if half == 1:
                    for g in range(2):
                        for i in range(4):
                            is_moved(dve, T(f"out{L}.{g}", i))
                elif L == 2:
                    dve.wait_ge(second_in, 16)
                    dve.wait_ge(x_act, 16)
                    dve.wait_ge(x_dve, 16)
                else:
                    for i in range(8):
                        is_moved(dve, T("down2", i))
                sqv = W(0, 2, KT, S)
                if streams == 2:
                    tt(sqv[:, 1], res[:, 1], res[:, 1], ALU.mult).then_inc(sq_dve, 1)
                else:
                    tt(sqv[:, 0, 4:8], res[:, 0, 4:8], res[:, 0, 4:8], ALU.mult).then_inc(sq_dve, 1)
                is_moved(dve, T(name))
                step(dve.reciprocal(X(512, S * streams), X(0, S * streams)))
                for s in range(streams):
                    r = tt(u[:, s], res[:, s], X(512 + S * s, S).unsqueeze(1).broadcast_to([P, KT, S]), ALU.mult)
                r.then_inc(cent_done, 1)
                cnt["cent"] += 1
                dve.wait_ge(cent_done, cnt["cent"])
                s = streams - 1
                for k in range(0 if streams == 2 else 4, KT):
                    ts(u[:, s, k], u[:, s, k], mod[:, L, 24 * half + 8 + k, s:s + 1], mod[:, L, 24 * half + k, s:s + 1],
                       ALU.mult, ALU.add).then_inc(u_dve, 1)

            def add_second(L, names, gate, streams):
                for k, t in enumerate(names):
                    is_filled(dve, t)
                    for s in range(streams):
                        r = stt(res[:, s, k], B(t)[:, S * s:S * s + S], mod[:, L, gate + k, s:s + 1], res[:, s, k],
                                ALU.mult, ALU.add)
                    r.then_inc(moved[t % 8], 1)

            def head_norms(L):
                n = 10 if L == 2 else 16

                def rotate(i):
                    t = RT(i)
                    is_filled(dve, t)
                    v = wq[:, i, 0] if i < 8 else kraw[:, i - 8, 0]
                    w = X(3072 + S * (i % 2), S)
                    tt(w, B(t)[:, 0:S], rope[:, 256:512], ALU.mult).then_inc(moved[t % 8], 1)
                    step(tt(v, v, rope[:, 0:256], ALU.mult))
                    tt(v, v, w, ALU.add).then_inc(nrm_done, 1)

                for i in range(n):
                    is_moved(dve, NT(L, i))
                    width = S if L == 3 and i < 8 else 512
                    r = X(2048 + 512 * (i % 2), width)
                    step(dve.reciprocal(r, r))
                    if L == 2:
                        v = wq[:, i] if i < 8 else kraw[:, i - 8]
                        v = v.rearrange("p s t -> p (s t)")
                        g = tiny[:, 8:9] if i < 8 else C("swa_gk")
                        stt(v, v, g, r, ALU.mult, ALU.mult).then_inc(nrm_q, 1)
                        if i == 0:
                            dve.wait_ge(rope_in, 16)
                        else:
                            rotate(i - 1)
                    elif i < 8:
                        v = nq_pad[:, 2 * i]
                        step(stt(v, v, C("na_gq"), r, ALU.mult, ALU.mult))
                        step(ts(nq_pad[:, 2 * i + 1], v, K("halfcol")[:, 1:2], None, ALU.mult))
                        ts(v, v, K("halfcol")[:, 0:1], None, ALU.mult).then_inc(nrm_q, 1)
                    else:
                        v = nk[:, i - 8].rearrange("p s t -> p (s t)")
                        stt(v, v, C("na_gk"), r, ALU.mult, ALU.mult).then_inc(nrm_q, 1)
                if L == 2:
                    rotate(n - 1)

            def attention(L):
                seqs = SEQ[L]

                def shift(q):
                    v, s, h, qb, tS, tT = seqs[q]
                    sm = tiny[:, 16 + 16 * (q % 4):32 + 16 * (q % 4)]
                    z = zbuf[L][q % 6]
                    if q >= 6:
                        is_filled(dve, seqs[q - 6][5])
                    is_filled(dve, tS)
                    if s == 0:
                        step(dve.tensor_reduce(sm[:, 0:1], B(tS)[:, S:2 * S], AX_X, ALU.max))
                        if L == 2:
                            step(tt(sm[:, 0:1], sm[:, 0:1], C("sink", h, 1), ALU.max))
                            bias = rope[:, 512 + S * qb:512 + S * qb + S]
                            src, dst = B(tS)[:, 0:S], z[:, 0:S]
                        else:
                            if qb == 0:
                                b = h % 4
                                dve.wait_ge(bias_in[b], 32 * (h // 4 + 1))
                                tb = btab[:, b]
                                step(tt(tb, tb, K("namask").unsqueeze(1).broadcast_to([P, 6, GRID_W]), ALU.add))
                            j = 2 - 2 * qb
                            bias = btab[:, h % 4, j:j + 4].rearrange("p j w -> p (j w)")
                            src, dst = B(tS)[:, 0:S], z[:, 0:S]
                        step(dve.tensor_tensor_reduce(out=dst, in0=src, in1=bias, scale=1.0, scalar=sm[:, 0:1],
                                                      op0=ALU.add, op1=ALU.max, accum_out=sm[:, 1:2]))
                        ts(sm[:, 4:5], sm[:, 1:2], -1.0, None, ALU.mult).then_inc(soft_z, 1)
                    else:
                        step(dve.tensor_reduce(sm[:, 0:2], B(tS)[:, :].rearrange("p (b k) -> p b k", b=2), AX_X, ALU.max))
                        ts(sm[:, 4:6], sm[:, 0:2], C("sink", h, 1), -1.0, ALU.max, ALU.mult).then_inc(soft_z, 1)

                def norm(q):
                    v, s, h, qb, tS, tT = seqs[q]
                    sm = tiny[:, 16 + 16 * (q % 4):32 + 16 * (q % 4)]
                    z = zbuf[L][q % 6]
                    dve.wait_ge(soft_e, SB0[L] + q + 1)
                    if s == 0:
                        n = 3 if L == 2 else 2
                        step(dve.tensor_reduce(sm[:, 10:11], sm[:, 6:6 + n], AX_X, ALU.add))
                        step(dve.reciprocal(sm[:, 11:12], sm[:, 10:11]))
                        ts(z, z, sm[:, 11:12], None, ALU.mult).then_inc(soft_p, 1)
                    else:
                        step(tt(sm[:, 10:12], sm[:, 6:8], sm[:, 8:10], ALU.add))
                        step(dve.reciprocal(sm[:, 12:14], sm[:, 10:12]))
                        for b in range(2):
                            r = ts(z[:, S * b:S * b + S], z[:, S * b:S * b + S], sm[:, 12 + b:13 + b], None, ALU.mult)
                        r.then_inc(soft_p, 1)

                for n in range(len(UNITS[L]) + 4):
                    for q, e in enumerate(seqs):
                        if e[0] == n:
                            shift(q)
                    for q, e in enumerate(seqs):
                        if e[0] == n - 1:
                            norm(q)
                    if L == 2 and n < 24 and n % 2 == 0:
                        ada(3, n // 2, n // 2 + 1)
                    if n >= 5 and n % 2 == 1:
                        pair = (n - 5) // 2
                        s, h = UNITS[L][2 * pair]
                        copy_tile(T(f"aO{L}.{pair}"), u[:, s, h // 2], S)

            def second(L):
                streams = 2 if L == 2 else 1
                if L == 2:
                    step(ts(tiny[:, 8:9], C("swa_gq"), 0.125, None, ALU.mult))
                rms(L, 0, 2, f"rms{L}a")
                if L == 2:
                    for i in range(4):
                        copy_tile(T("in2.2", 2 + i), wv[:, i], S)
                    head_norms(2)
                    for i in range(1, 8, 2):
                        copy_tile(T("kpad", i), kpad[:, i], 512)
                    for i in range(0, 8, 2):
                        is_filled(dve, T("kpad", i))
                else:
                    for i in range(8):
                        copy_tile(T(f"in3.{2 + i // 4}", i % 4), nk[:, i], 512)
                    for i in range(4):
                        copy_tile(T("in3.5", i), nv[:, i, 512:1024], 512)
                    head_norms(3)
                attention(L)
                add_second(L, [T(f"out{L}.{k // 4}", k % 4) for k in range(8)], 16, streams)
                if L == 2:
                    ada_sums(3, "a")
                    ada_sums(3, "b")
                rms(L, 1, streams, f"rms{L}b")
                for n in range(FFT):
                    t = T(f"gu{L}.{(n + FFT) // 4}", (n + FFT) % 4)
                    is_moved(dve, T(f"gu{L}.{n // 4}", n % 4))
                    is_filled(dve, t)
                    v = hidden[:, n, 0:streams]
                    tt(v, v, B(t)[:, 0:S * streams].rearrange("p (s t) -> p s t", s=streams), ALU.mult)\
                        .then_inc(moved[t % 8], 1)
                add_second(L, [T(f"down{L}", k) for k in range(8)], 40, streams)

            even()
            if last_stage >= 2:
                experts(0)
            if last_stage >= 3:
                odd()
            if last_stage >= 4:
                experts(1)
            if last_stage >= 5:
                second(2)
            if last_stage >= 7:
                second(3)

        @block.gpsimd
        def _(pool):
            def route_weights(l):
                if l:
                    is_filled(pool, T("route0"))
                v = wroute[:, :].rearrange("p (k n) -> p k n", n=36)
                pool.dma_start(v[:, :, 0:4], a["moe_w_group"][l].rearrange("(k p) n -> p k n", p=P)).then_inc(wroute_in, 16)
                pool.dma_start(v[:, :, 4:36], a["moe_w_router"][l].rearrange("(k p) n -> p k n", p=P))\
                    .then_inc(wroute_in, 16)

            route_weights(0)
            if last_stage >= 4:
                route_weights(1)
            if last_stage >= 5:
                pool.wait_ge(res_ready, 3)
                pool.dma_start(res[:, 1], a["ctx"]).then_inc(second_in, 16)
                pool.wait_ge(res_ready, 4)
                pool.dma_start(rope, a["rope"]).then_inc(rope_in, 16)
            if last_stage >= 7:
                is_filled(pool, T("in3.5", 3))
                rpb = a["na_rpb"]
                for h in range(HQ):
                    if h >= 4:
                        pool.wait_ge(soft_z, SB0[3] + 2 * (h - 4) + 2)
                    for b in range(2):
                        src = bass.AP(rpb.tensor, h * 465 + (5 - b) * 31 + 15, [[HQ * 465 - 1, 64], [31, 6], [1, 64]])
                        pool.dma_start(btab[64 * b:64 * b + 64, h % 4], src).then_inc(bias_in[h % 4], 16)


_INS = ["w_ada", "w_ada_2", "even_w_in", "even_w_out", "odd_w_in", "odd_w_out", "moe_w_group", "moe_w_router",
        "moe_w1", "moe_w3", "moe_w2", "w_gate_up_2", "w_down_2", "swa_w_qkv_2", "swa_w_o_2", "na_w_qkv_2", "na_w_o_2"]


def lay_out(inputs):
    g = {k: np.asarray(v) for k, v in inputs.items()}

    def col(v):
        v = v.reshape(-1, P)
        return np.ascontiguousarray(v.T)

    def rows(v):
        return np.broadcast_to(v.reshape(1, -1), (P, v.size))

    def tall(v):
        return np.concatenate([v.reshape(-1, 1), np.zeros((P - v.size, 1), v.dtype)])

    def twice(v):
        return np.concatenate([v.reshape(-1, 1)] * 2)

    parts = [col(g["c"]), col(g["c_2"]), col(g["c_ctx_2"]), col(g["ln1_g"]), col(g["ln1_b"]), col(g["ln2_g"]),
             col(g["ln2_b"]), col(g["b_ada"]), col(g["b_ada_2"]), col(g["ret_gn_g"]), col(g["diff_subln_g"]),
             col(g["g_mix_2"]), col(g["g_ffn_2"]), twice(g["swa_g_q_2"]), twice(g["swa_g_k_2"]),
             twice(g["na_g_q_2"]), twice(g["na_g_k_2"]), rows(g["swa_sink_2"]),
             tall(g["lambda_q1"]), tall(g["lambda_q2"]), tall(g["lambda_k1"]), tall(g["lambda_k2"])]
    for l in range(2):
        parts += [rows(g["moe_b_group"][l]), rows(g["moe_b_router"][l])]
    const, first, rope = shape_constants()
    arrays = {"cols": np.ascontiguousarray(np.concatenate(parts, 1)), "const": const, "first": first, "rope": rope}
    for name, key in (("x", "x"), ("ctx", "ctx_2")):
        arrays[name] = np.ascontiguousarray(g[key][0].T.reshape(KT, P, S).transpose(1, 0, 2))
    for name in _INS:
        arrays[name] = np.ascontiguousarray(g[name])
    arrays["na_rpb"] = np.ascontiguousarray(np.broadcast_to(g["na_rpb_2"].reshape(1, -1), (GRID_W, HQ * 465)))
    return arrays


def kernel(**inputs):
    import concourse.bacc as bacc
    from concourse.bass_utils import run_bass_kernel_spmd

    nc = bacc.Bacc("TRN2", target_bir_lowering=False, num_devices=1, dynamic_dma_scratch_size=8192)
    arrays = {f"in_{k}": v for k, v in lay_out(inputs).items()}
    aps = {k[3:]: nc.dram_tensor(k, v.shape, mybir.dt.from_np(v.dtype), kind="ExternalInput").ap()
           for k, v in arrays.items()}
    out = nc.dram_tensor("out_x", (P, KT, S), F32, kind="ExternalOutput").ap()
    build(nc, aps, out)
    r = run_bass_kernel_spmd(nc, [arrays], core_ids=[0])
    got = r.results[0]["out_x"]
    return np.ascontiguousarray(got.transpose(1, 0, 2).reshape(D, S).T)[None]
```

```python
from contextlib import ExitStack

import numpy as np

import concourse.bass as bass
from concourse import mybir

F32 = mybir.dt.float32
I32 = mybir.dt.int32
ALU = mybir.AluOpType
ACT = mybir.ActivationFunctionType
AX_X = mybir.AxisListType.X

P = 128
D = 1024
KT = D // P
S = 256
DEPTH = 2
ALPHA = (2.0 * DEPTH) ** 0.25
EPS_LN, EPS_RMS = 1e-5, 1e-6
SB_HEADS, RET_HEADS, DIFF_HEADS = 8, 4, 8
N_GROUPS, PER_GROUP = 4, 8
N_EXPERTS = N_GROUPS * PER_GROUP
FF = 512
D_FF = 2816
FFT = D_FF // P
HQ, HKV = 16, 4
WINDOW = 128
CHUNK = 64
NEG = -1e30
LAMBDA_INIT = 0.8 - 0.6 * float(np.exp(-0.3))
GRID_W, NA_KH, NA_KW, NA_ROWS = 64, 8, 16, S // 64

RING = 12
SLOT = 2048

BLK = 32
GRP = 4
MAX_BLOCKS = 2 * S // BLK + N_EXPERTS + GRP
MAX_GROUPS = MAX_BLOCKS // GRP
INFO = 1 + MAX_BLOCKS

CONST = {}
_at = 0
for _name, _w in (("ident", P), ("ones", P), ("blk64", P), ("rot", P), ("before", P),
                  ("quad", 224), ("halves", 320), ("iota", P), ("sbmask", 384), ("namask", 64),
                  ("thresh", 8), ("gthresh", MAX_GROUPS), ("lead", N_EXPERTS), ("halfcol", 2), ("one", 1), ("eps_ln", 1),
                  ("eps_rms", 1), ("pid", 1)):
    CONST[_name] = (_at, _at + _w)
    _at += _w
CONST_W = _at
FIRST = {"decay": (0, 4 * 384), "dist": (1536, 1920), "after": (1920, 2048)}
ROPE = {"cos": (0, 256), "sin": (256, 512), "window": (512, 1024)}

COLS = {}
_at = 0
for _name, _w in (("c", KT), ("c2", KT), ("cc", KT), ("ln1_g", 2 * KT), ("ln1_b", 2 * KT), ("ln2_g", 2 * KT),
                  ("ln2_b", 2 * KT), ("b_ada", 4 * 48), ("ret_g", RET_HEADS), ("subln", 1), ("g_mix", 2 * KT),
                  ("g_ffn", 2 * KT), ("swa_gq", 1), ("swa_gk", 1), ("na_gq", 1), ("na_gk", 1), ("sink", HQ),
                  ("lam", 4), ("b_route", 2 * 36)):
    COLS[_name] = (_at, _at + _w)
    _at += _w
COLS_W = _at


def shape_constants():
    p = np.arange(P)
    q = np.arange(P)
    c = np.zeros((P, CONST_W), np.float32)

    def put(name, value):
        a, b = CONST[name]
        c[:, a:b] = value

    put("ident", np.eye(P))
    put("ones", 1.0)
    put("blk64", (p[:, None] // 64 == p[None, :] // 64))
    rot = np.zeros((P, P))
    for m in range(P):
        if m % 32 < 16:
            rot[m + 16, m] = -1.0
        else:
            rot[m - 16, m] = 1.0
    put("rot", rot)
    put("before", (p[:, None] < p[None, :]))
    quad = np.zeros((P, 224))
    quad[p, 96 + p % 32] = 1.0
    put("quad", quad)
    halves = np.zeros((P, 320))
    halves[:, 64:128] = np.eye(P)[:, 0:64]
    halves[:, 192:256] = np.eye(P)[:, 64:128]
    put("halves", halves)
    put("iota", np.arange(P)[None, :])
    diag = np.where(p[:, None] < q[None, :], 0.0, NEG)
    put("sbmask", np.concatenate([diag, np.zeros((P, P)), diag], 1))
    qc = p % GRID_W
    kc = np.arange(GRID_W)
    start = np.clip(qc - NA_KW // 2, 0, GRID_W - NA_KW)
    put("namask", np.where((kc[None] >= start[:, None]) & (kc[None] < start[:, None] + NA_KW), 0.0, NEG))
    put("thresh", BLK * np.arange(8)[None, :])
    put("lead", (np.arange(N_EXPERTS) < GRP)[None, :])
    put("gthresh", GRP * np.arange(1, 1 + MAX_GROUPS)[None, :])
    put("halfcol", np.stack([p < 64, p >= 64], 1) * 0.125)
    put("one", 1.0)
    put("eps_ln", EPS_LN)
    put("eps_rms", EPS_RMS)
    put("pid", p[:, None])

    f = np.zeros((P, 2048), np.float32)
    log_gamma = np.log1p(-np.exp2(-5.0 - np.arange(RET_HEADS)))
    kpos, qpos = np.arange(P)[:, None], np.arange(S)[None, :]
    for h in range(RET_HEADS):
        decay = np.exp(log_gamma[h] * np.abs(qpos - kpos)) * (kpos // CHUNK <= qpos // CHUNK)
        f[:, h * 384:h * 384 + 256] = decay
        f[:, h * 384 + 256:h * 384 + 384] = decay[:, 0:P]
    near = np.where(q[None, :] // CHUNK <= p[:, None] // CHUNK, np.abs(p[:, None] - q[None, :]), -NEG * 1e4)
    f[:, 1536:1920] = np.concatenate([near, P + p[:, None] - q[None, :], near], 1)
    f[:, 1920:2048] = (p[:, None] >= p[None, :])

    r = np.zeros((P, 1024), np.float32)
    t = np.arange(S)
    half = 16
    freqs = 10000.0 ** (-np.arange(half) / half)
    for m in range(P):
        d = m % 64
        pos = t // GRID_W if d < 32 else t % GRID_W
        ang = pos * freqs[d % 16]
        r[m, 0:256], r[m, 256:512] = np.cos(ang), np.sin(ang)
    for qb in range(2):
        valid = np.abs(p[:, None] + P * qb - t[None, :]) <= WINDOW
        r[:, 512 + 256 * qb:768 + 256 * qb] = np.where(valid, 0.0, NEG)
    return c, f, r


def build(nc, a, out):
    ctx = ExitStack()
    with ctx:
        def sb(name, shape, dt=F32):
            return ctx.enter_context(nc.sbuf_tensor(name, shape, dt))

        def sem(name):
            return ctx.enter_context(nc.semaphore(name))

        ring = sb("ring", [P, RING, SLOT])
        res = sb("res", [P, 2, KT, S])
        u = sb("u", [P, 2, KT, S])
        work = sb("work", [P, 12288])
        scratch = sb("scratch", [P, 4096])
        const = sb("const", [P, CONST_W])
        cols = sb("cols", [P, COLS_W])
        mod = sb("mod", [P, 4, 48, 2])
        cond = sb("cond", [P, 24])
        condrep = sb("condrep", [P, KT, 32])
        adaT = sb("adaT", [P, 512])
        adac = sb("adac", [P, 4, 48, 2])
        tiny = sb("tiny", [P, 96])
        info = sb("info", [P, 64], I32)
        wroute = sb("wroute", [P, KT * 36])
        zmore = sb("zmore", [P, 3, 512])

        bank = [ctx.enter_context(nc.psum_tensor(f"bank{i}", [P, 512], F32)) for i in range(8)]

        def K(name):
            lo, hi = CONST[name]
            return const[:, lo:hi]

        def C(name, i=0, n=None):
            lo, hi = COLS[name]
            return cols[:, lo + i:hi if n is None else lo + i + n]

        first = res[:, 1].rearrange("p k s -> p (k s)")
        decay = first[:, 0:1536].rearrange("p (h w) -> p h w", w=384)
        dist = first[:, 1536:1920]
        after = first[:, 1920:2048]
        ident, ones = K("ident"), K("ones")
        x = res[:, 0]
        o1 = u[:, 1]
        both = lambda t, k: t[:, :, k, :]

        def W(lo, *dims):
            n = int(np.prod(dims))
            v = work[:, lo:lo + n]
            if len(dims) == 1:
                return v
            names = "abcd"[:len(dims)]
            return v.rearrange(f"p ({' '.join(names)}) -> p {' '.join(names)}", **dict(zip(names, dims)))

        def X(lo, *dims):
            n = int(np.prod(dims))
            v = scratch[:, lo:lo + n]
            if len(dims) == 1:
                return v
            names = "abcd"[:len(dims)]
            return v.rearrange(f"p ({' '.join(names)}) -> p {' '.join(names)}", **dict(zip(names, dims)))

        sq_pad = W(0, SB_HEADS, S)
        sk = W(2048, 4, S)
        sv = W(3072, 2, 512)
        rq = W(4096, 4, S)
        rk = W(5120, 4, S)
        rv = W(6144, 2, 512)
        rg = W(7168, 4, S)
        sb_t = W(8192, 4, 384)
        sb_l = W(9728, 4, 384)
        sb_z = X(0, 4, 384)
        ret_p = X(1536, 4, 384)
        ret_o = W(8192, 4, S)
        ret_s = W(9216, 4, S)
        dq_pad = W(0, 16, S)
        dk = W(4096, 8, S)
        dv = W(6144, 2, D)
        dz3 = [W(8192, 2, 384), W(8960, 2, 384), W(11264, 2, 384)]
        da = W(9728, 2, 384)
        daT = W(10496, 2, 384)
        dsq = X(0, 8, S)
        dr = X(2048, 8, S)
        xnat = W(0, 2, D)
        acc = W(2048, KT, S)
        xg = W(4096, KT, P)
        sil = W(5120, 512)
        hid = W(5632, 512)
        hidT = W(6144, 4, P)
        ysb = W(6656, D)
        sel = W(7680, 2, P)
        selT = W(7936, S)
        selT2 = W(8192, S)
        drow = W(8448, 4, S)
        route = W(9472, 2048)
        R_CH, R_BC, R_EXP, R_DEST, R_SMALL = 0, 64, 1088, 1098, 1103
        dest = route[:, R_DEST:R_DEST + 4].rearrange("p (c b) -> p c b", c=2)
        slotcol = route[:, R_DEST + 4:R_DEST + 5]
        wq = W(0, 8, 2, S)
        kpad = W(4096, 8, 512)
        wv = W(8192, 4, S)
        kraw = W(9216, 2, 2, S)
        rope = work[:, 10240:11264]
        nq_pad = W(0, HQ, S)
        nk = W(4096, 8, 2, S)
        nv = W(8192, 4, D)
        hidden = W(0, FFT, 2, S)
        pT = X(0, 4, 4, S)
        nz = first[:, 0:1536].rearrange("p (b w) -> p b w", w=512)
        wz = W(9216, 3, 512)
        zbuf = {2: [wz[:, i] for i in range(3)], 3: [nz[:, i] for i in range(3)]}
        for v in zbuf.values():
            v += [zmore[:, i] for i in range(3)]
        btab = u[:, 1].rearrange("p k s -> p (k s)")[:, 0:1536].rearrange("p (b j w) -> p b j w", b=4, w=GRID_W)

        lead0 = []
        tile0, slot0 = {}, {}
        loads = []
        state = {"t": 0, "epoch": 0, "n": 0}
        per_pos = [0] * RING

        def job(name, tiles, sources=(), release=None):
            tile0[name] = state["t"]
            slot0[name] = len(loads)
            state["t"] += tiles
            for i, src in enumerate(sources):
                r = state["n"] % RING
                per_pos[r] += 1
                by_tile = release is None or i == len(sources) - 1
                rel = ("tile", state["t"] - 1) if by_tile else ("down", release + i + 1)
                loads.append((state["epoch"], r, per_pos[r], src, rel))
                state["n"] += 1

        def panel(w, g):
            v = w[:, 512 * g:512 * g + 512].rearrange("(k p) n -> p k n", p=P)
            return [v[:, 0:4], v[:, 4:8]]

        def ada_jobs(L, g0, g1):
            w = a["w_ada"][L] if L < 2 else a["w_ada_2"][L - 2]
            for g in range(g0, g1):
                job(f"ada{L}.{g}", 1, panel(w, g))

        def lead_jobs(l):
            lead0.append(state["n"] % RING)
            for ph in range(3):
                for j in range(GRP):
                    w = a["moe_w1"] if ph < 2 else a["moe_w3"]
                    half = ph % 2
                    src = w[l, j, 512 * half:512 * half + 512, :].rearrange("(k p) n -> p k n", p=P)
                    loads.append((state["epoch"], state["n"] % RING, 0, src, None))
                    state["n"] += 1

        def down_jobs(L):
            v = a["w_down_2"][L - 2].rearrange("(k p) n -> p k n", p=P)
            job(f"down{L}", 8, [v[:, 2 * i:2 * i + 2] for i in range(FFT // 2)], release=(L - 2) * (FFT // 2 - 1))

        ada_jobs(0, 0, 4)
        job("adafin0a", 1)
        for g in range(7):
            job(f"even.{g}", 2 if g in (2, 5) else 4, panel(a["even_w_in"][0], g))
            ada_jobs(0, 4 + g, 5 + g)
        ada_jobs(0, 11, 12)
        job("adafin0b", 1)
        for b in range(2):
            job(f"sbS{b}", 4)
            ada_jobs(1, 4 * b, 4 * b + 3)
            job(f"sbR{b}", 4)
            ada_jobs(1, 4 * b + 3, 4 * b + 4)
            job(f"sbO{b}", 2)
        job("retS", 4)
        ada_jobs(1, 8, 9)
        job("retO", 4)
        job("retM", 2)
        ada_jobs(1, 9, 10)
        job("retV", 2)
        ada_jobs(1, 10, 12)
        for g in range(2):
            job(f"out0.{g}", 4, panel(a["even_w_out"][0], g))
        job("adafin1a", 1)
        job("adafin1b", 1)
        job("ln0a", 2)
        job("route0", 1 + 4 + 1 + 2)
        lead_jobs(0)
        state.update(epoch=1)
        job("ln0b", 2)
        for g in range(6):
            job(f"odd.{g}", 2 if g >= 4 else 4, panel(a["odd_w_in"][0], g))
        job("lam", 1)
        for n in range(DIFF_HEADS + 3):
            if n < DIFF_HEADS:
                job(f"dS{n}", 2)
            if n < 10:
                ada_jobs(2, n, n + 1)
            if 2 <= n < DIFF_HEADS + 2:
                job(f"dT{n - 2}", 1)
            if n >= 3:
                job(f"dO{n - 3}", 1)
        job("dV", 4)
        ada_jobs(2, 10, 12)
        for g in range(2):
            job(f"out1.{g}", 4, panel(a["odd_w_out"][0], g))
        job("adafin2a", 1)
        job("adafin2b", 1)
        job("ln1a", 2)
        job("route1", 1 + 4 + 1 + 2)
        lead_jobs(1)
        state.update(epoch=2)
        job("ln1b", 2)
        for L in (2, 3):
            w_in = a["swa_w_qkv_2"][0] if L == 2 else a["na_w_qkv_2"][0]
            w_o = a["swa_w_o_2"][0] if L == 2 else a["na_w_o_2"][0]
            job(f"rms{L}a", 1)
            if L == 2:
                steps2 = []
                for i in range(10):
                    steps2 += [("in", i)] + [("nrm", i - 1)] * (i >= 1) + [("rot", i - 2)] * (i >= 2)
                steps2 += [("v", 0), ("nrm", 9), ("rot", 8), ("v", 1), ("rot", 9), ("v", 2), ("v", 3)]
                cuts = [0, steps2.index(("in", 4)), steps2.index(("in", 8)), len(steps2)]
                panels2 = [steps2[cuts[g]:cuts[g + 1]] for g in range(3)]
                for g in range(3):
                    job(f"in2.{g}", len(panels2[g]), panel(w_in, g))
                tile2 = {e: tile0["in2.0"] + n for n, e in enumerate(steps2)}
                job("kpad", 8)
            else:
                for g in range(6):
                    job(f"in3.{g}", 4 if g < 2 else 8, panel(w_in, g))
            units = [(s, h) for s in range(2 if L == 2 else 1) for h in range(HQ)]
            for n in range(len(units) + 3):
                if n < len(units):
                    job(f"aS{L}.{n}", 2 if units[n][0] == 0 else 1)
                if L == 2 and n < 24 and n % 2 == 0:
                    ada_jobs(3, n // 2, n // 2 + 1)
                if 2 <= n < len(units) + 2:
                    job(f"aT{L}.{n - 2}", 2 if units[n - 2][0] == 0 else 1)
                if n >= 4 and n % 2 == 0:
                    job(f"aO{L}.{(n - 4) // 2}", 1)
            for g in range(2):
                job(f"out{L}.{g}", 4, panel(w_o, g))
            if L == 2:
                job("adafin3a", 1)
                job("adafin3b", 1)
            job(f"rms{L}b", 1)
            for g in range(11):
                job(f"gu{L}.{g}", 4, panel(a["w_gate_up_2"][L - 2], g))
            down_jobs(L)

        SEQ = {}
        for L in (2, 3):
            SEQ[L] = []
            for v, (s, h) in enumerate((s, h) for s in range(2 if L == 2 else 1) for h in range(HQ)):
                for qb in range(2 if s == 0 else 1):
                    SEQ[L].append((v, s, h, qb, tile0[f"aS{L}.{v}"] + qb, tile0[f"aT{L}.{v}"] + qb))
        SB0 = {2: DIFF_HEADS, 3: DIFF_HEADS + len(SEQ[2])}
        NB = {2: 0, 3: 10}
        RMS_N = {2: (5, 6), 3: (7, 8)}
        U_N = {2: (16, 24), 3: (32, 40)}

        def NT(L, i):
            if L == 3:
                return tile0[f"in3.{2 + i // 4}"] + 2 * (i % 4) + 1
            return tile2["nrm", i]

        def IT(g, i):
            return tile0[f"in3.{g}"] + (i if g < 2 else 2 * i)

        def RT(i):
            return tile2["rot", i]

        def nsq(i, width):
            return X(1024 + 512 * (i % 2), width)

        UNITS = {L: [(s, h) for s in range(2 if L == 2 else 1) for h in range(HQ)] for L in (2, 3)}

        filled = [sem(f"bank{i}_filled") for i in range(8)]
        moved = [sem(f"bank{i}_moved") for i in range(8)]
        loaded = [sem(f"slot{i}_loaded") for i in range(RING)]
        mloaded = [[sem(f"moe{l}_slot{i}_loaded") for i in range(RING)] for l in range(2)]
        down_used = sem("down_slot_used")
        cols_in = sem("parameters_loaded")
        const_in = sem("constants_loaded")
        first_in = sem("first_stack_loaded")
        second_in = sem("context_loaded")
        rope_in = sem("rope_loaded")
        cond_done = sem("condition_ready")
        condrep_done = sem("condition_spread")
        mod_done = sem("modulation_ready")
        u_act, u_dve = sem("u_by_act"), sem("u_by_dve")
        x_act = sem("residual_by_act")
        xs_done = sem("residual_scaled")
        sq_act = sem("squares_by_act")
        cent_done = sem("centred_by_dve")
        sb_d, sb_e, sb_sp, sb_a, sb_w = (sem(f"sb_{n}") for n in ("negabs", "log", "softplus", "exponent", "weights"))
        ret_done = sem("retention_ready")
        soft_z, soft_e, soft_p = sem("scores_shifted"), sem("exponentials_ready"), sem("probabilities_ready")
        lam_p = sem("lambda_products")
        o_done = sem("attention_output_ready")
        nrm_q = sem("head_normed")
        nrm_done = sem("head_rotated")
        bias_in = [sem(f"bias{i}_loaded") for i in range(4)]
        route_dve = sem("routing_ready")
        route_act = sem("routing_exponentials")
        info_done = sem("block_table_ready")
        moe = []
        for l in range(2):
            moe.append({n: sem(f"moe{l}_{n}") for n in (
                "selected", "gathered", "xg_by_act", "xg_by_dve", "phase", "silu", "hidden", "turned", "turned_out",
                "y_by_act", "y_by_dve", "spread_ready", "scattered", "summed", "step")})
        chain_v, chain_a = sem("dve_step"), sem("act_step")
        chain_adac = sem("modulation_sums_turned")
        res_ready = sem("residual_complete")
        nsq_done = sem("head_squares_ready")
        wroute_in = sem("router_weights_loaded")
        out_done = sem("output_stored")

        def is_filled(eng, t):
            eng.wait_ge(filled[t % 8], t // 8 + 1)

        def is_moved(eng, t):
            eng.wait_ge(moved[t % 8], t // 8 + 1)

        def T(name, i=0):
            return tile0[name] + i

        def B(t):
            return bank[t % 8]

        block = ctx.enter_context(nc.Block())

        @block.sync
        def _(sp):
            def epoch(e):
                for n, (ep, r, count, src, _) in enumerate(loads):
                    if ep != e:
                        continue
                    first_of_epoch = n == 0 or loads[n - 1][0] != e
                    if first_of_epoch:
                        sp_state["base"] = n
                    k = n - sp_state["base"]
                    if k >= RING:
                        kind, v = loads[n - RING][4]
                        if kind == "tile":
                            is_filled(sp, v)
                        else:
                            sp.wait_ge(down_used, v)
                    elif e > 0:
                        sp.wait_ge(moe[e - 1]["phase"], sp_state["more"] * 6 + (k // 4 + 4))
                    dst = ring[:, r, :].rearrange("p (k n) -> p k n", n=src.shape[2])
                    sp.dma_start(dst, src).then_inc(loaded[r] if count else mloaded[e][r], 16)

            sp_state = {}

            def experts(l):
                m = moe[l]
                sp.wait_ge(info_done, l + 1)
                more = sp.value_load(info[0:1, 0:1], min_val=0, max_val=MAX_GROUPS - 1)
                sp_state["more"] = more

                def group(i, phases):
                    for ph in phases:
                        if ph in (phases[0], 4):
                            e = [sp.value_load(info[0:1, bass.ds(1 + GRP * i + j, 1)], min_val=1, max_val=N_EXPERTS)
                                 for j in range(GRP)]
                        sp.wait_ge(m["phase"], 6 * i + (ph - 2))
                        for j in range(GRP):
                            r = (lead0[l] + 4 * ph + j) % RING
                            if ph < 4:
                                w = a["moe_w1"] if ph < 2 else a["moe_w3"]
                                half = ph % 2
                                src = w[l, bass.ds(e[j] - 1, 1), 512 * half:512 * half + 512, :]
                                src = src.rearrange("a (k p) n -> p (a k) n", p=P)
                                dst = ring[:, r, :].rearrange("p (k n) -> p k n", k=4)
                            else:
                                half = ph - 4
                                src = a["moe_w2"][l, bass.ds(e[j] - 1, 1), 256 * half:256 * half + 256, :]
                                src = src.rearrange("a (k p) n -> p (a k) n", p=P)
                                dst = ring[:, r, :].rearrange("p (k n) -> p k n", k=2)
                            sp.dma_start(dst, src).then_inc(mloaded[l][r], 16)

                with sp.Fori(0, more) as i:
                    group(i, (3, 4, 5))
                    group(i + 1, (0, 1, 2))
                group(more, (3, 4, 5))

            epoch(0)
            experts(0)
            epoch(1)
            experts(1)
            epoch(2)
            for i in range(8):
                is_moved(sp, T("down3", i))
            sp.dma_start(out, x).then_inc(out_done, 16)
            sp.wait_ge(out_done, 16)

        @block.tensor
        def _(pe):
            def open_tile(t):
                if t >= 8:
                    is_moved(pe, t - 8)
                return B(t)

            def mm(o, l, r, start=True, stop=True):
                return pe.matmul(o, l, r, start=start, stop=stop, skip_group_check=True)

            def slot(n):
                _, r, count, src, _ = loads[n]
                pe.wait_ge(loaded[r], 16 * count)
                return ring[:, r, :].rearrange("p (k n) -> p k n", n=src.shape[2])

            def panel_slots(name):
                n = slot0[name]
                s0, s1 = slot(n), slot(n + 1)
                return lambda k: (s0, s1)[k // 4][:, k % 4]

            def ada(L, g0, g1):
                pe.wait_ge(condrep_done, 1 if L < 2 else 2)
                for g in range(g0, g1):
                    t = T(f"ada{L}.{g}")
                    b = open_tile(t)
                    w = panel_slots(f"ada{L}.{g}")
                    for k in range(KT):
                        j = k % 4
                        r = mm(b[32 * j:32 * j + 32, :], condrep[:, k, :], w(k), start=k < 4, stop=k >= 4)
                    r.then_inc(filled[t % 8], 1)

            def ada_sums(L, part):
                t = T(f"adafin{L}{part}")
                b = open_tile(t)
                a0, a1 = (0, 16) if part == "a" else (16, 48)
                pe.wait_ge(chain_adac, 12 * L + a1 // 4)
                lo = CONST["quad"][0]
                for q in range(4):
                    r = mm(b[:, 0:2 * (a1 - a0)], const[:, lo + 96 - 32 * q:lo + 224 - 32 * q],
                           adac[:, q, a0:a1].rearrange("p a c -> p (a c)"), start=q == 0, stop=q == 3)
                r.then_inc(filled[t % 8], 1)

            def project(name, rhs, width, tiles=4, first_tile=0, w=None):
                w = w or panel_slots(name)
                for i in range(tiles):
                    t = T(name, first_tile + i)
                    b = open_tile(t)
                    for k in range(KT):
                        r = mm(b[:, 0:width], w(k)[:, P * i:P * i + P], rhs(k), start=k == 0, stop=k == KT - 1)
                    r.then_inc(filled[t % 8], 1)

            def project_tokens(name, streams, c0, c1, first_tile=0, w=None):
                w = w or panel_slots(name)
                i = 0
                for s in range(streams):
                    for tb in range(2):
                        t = T(name, first_tile + i)
                        i += 1
                        b = open_tile(t)
                        for k in range(KT):
                            r = mm(b[:, 0:c1 - c0], u[:, s, k, P * tb:P * tb + P], w(k)[:, c0:c1],
                                   start=k == 0, stop=k == KT - 1)
                        r.then_inc(filled[t % 8], 1)

            def one_tile(t, calls):
                b = open_tile(t)
                for args in calls(b):
                    r = mm(*args)
                r.then_inc(filled[t % 8], 1)

            def ln_sums(name, n_sq):
                pe.wait_ge(res_ready, n_sq)
                one_tile(T(name), lambda b: [(b[:, 0:S], ones, x[:, k], k == 0, k == KT - 1) for k in range(KT)])
                sqv = X(0, KT, S)
                square_sums(T(name, 1), n_sq, S, lambda k: sqv[:, k])

            def square_sums(t, n_sq, width, squares):
                b = open_tile(t)
                for k in range(KT):
                    pe.wait_ge(sq_act, KT * (n_sq - 1) + k + 1)
                    r = mm(b[:, 0:width], ones, squares(k), k == 0, k == KT - 1)
                r.then_inc(filled[t % 8], 1)

            def even():
                ada(0, 0, 4)
                pe.wait_ge(const_in, 16)
                ada_sums(0, "a")
                pe.wait_ge(first_in, 32)
                pe.wait_ge(u_act, 4)
                pe.wait_ge(u_dve, 4)
                rhs = lambda k: u[:, 0, k]
                for g in range(7):
                    if g in (2, 5):
                        project_tokens(f"even.{g}", 1, 0, 512)
                    else:
                        project(f"even.{g}", rhs, S)
                    ada(0, 4 + g, 5 + g)
                ada(0, 11, 12)
                ada_sums(0, "b")
                for b in range(2):
                    for i in range(4):
                        h = 4 * b + i
                        is_moved(pe, T("even.0", h // 2))
                        is_moved(pe, T("even.1", h // 2))
                        one_tile(T(f"sbS{b}", i), lambda o: [
                            (o[:, 0:256], sk[:, h // 2, 0:P], sq_pad[:, h]),
                            (o[:, 256:384], sk[:, h // 2, P:S], sq_pad[:, h, P:S])])
                    ada(1, 4 * b, 4 * b + 3)
                    pe.wait_ge(sb_sp, b + 1)
                    for i in range(4):
                        one_tile(T(f"sbR{b}", i), lambda o: [
                            (o[:, 0:256], after, sb_l[:, i, 0:256], True, False),
                            (o[:, 128:256], ones, sb_l[:, i, 256:384], False, True),
                            (o[:, 256:384], after, sb_l[:, i, 256:384])])
                    ada(1, 4 * b + 3, 4 * b + 4)
                    for i in range(2):
                        pe.wait_ge(sb_w, b + 1)
                        is_moved(pe, T("even.2", 1))
                        calls = []
                        t = T(f"sbO{b}", i)
                        o = B(t)
                        for tb, (lo, hi) in enumerate(((0, 256), (128, 256))):
                            for j in range(2):
                                h = 4 * b + 2 * i + j
                                src = sb_l[:, 2 * i + j, 0:256] if tb == 0 else sb_l[:, 2 * i + j, 256:384]
                                calls.append((o[64 * j:64 * j + 64, lo:hi], sv[:, tb, 64 * h:64 * h + 64], src,
                                              tb == 0, tb == 1))
                        one_tile(t, lambda o: calls)
                is_moved(pe, T("even.3", 3))
                is_moved(pe, T("even.4", 3))
                for h in range(4):
                    one_tile(T("retS", h), lambda o: [
                        (o[:, 0:256], rk[:, h, 0:P], rq[:, h]),
                        (o[:, 256:384], rk[:, h, P:S], rq[:, h, P:S])])
                is_moved(pe, T("even.5", 1))
                ada(1, 8, 9)
                for h in range(4):
                    is_moved(pe, T("retS", h))
                    one_tile(T("retO", h), lambda o: [
                        (o[:, 0:256], rv[:, 0, P * h:P * h + P], ret_p[:, h, 0:256], True, False),
                        (o[:, 128:256], rv[:, 1, P * h:P * h + P], ret_p[:, h, 256:384], False, True)])
                for h in range(2):
                    is_moved(pe, T("retO", 2 * h + 1))
                    is_moved(pe, T("retO", 2 * h))
                    one_tile(T("retM", h), lambda o: [(o[:, :], ones, ret_o[:, 2 * h:2 * h + 2])])
                ada(1, 9, 10)
                pe.wait_ge(ret_done, 1)
                for h in range(2):
                    one_tile(T("retV", h), lambda o: [(o[:, :], ones, ret_s[:, 2 * h:2 * h + 2])])
                ada(1, 10, 12)
                pe.wait_ge(o_done, 1)
                is_moved(pe, T("sbO1", 1))
                is_moved(pe, T("sbO0", 1))
                is_moved(pe, T("sbO0", 0))
                is_moved(pe, T("sbO1", 0))
                for g in range(2):
                    project(f"out0.{g}", lambda k: o1[:, k], S)
                ada_sums(1, "a")
                ada_sums(1, "b")
                ln_sums("ln0a", 1)

            def odd():
                pe.wait_ge(u_act, 12)
                pe.wait_ge(u_dve, 12)
                rhs = lambda k: u[:, 0, k]
                for g in range(6):
                    if g >= 4:
                        project_tokens(f"odd.{g}", 1, 0, 512)
                    else:
                        project(f"odd.{g}", rhs, S)
                pe.wait_ge(lam_p, 1)
                one_tile(T("lam"), lambda o: [(o[:, 0:2], ones, tiny[:, 0:2])])
                for i in range(4):
                    for g in range(4):
                        is_moved(pe, T(f"odd.{g}", i))
                for g in (4, 5):
                    for i in range(2):
                        is_moved(pe, T(f"odd.{g}", i))
                for n in range(DIFF_HEADS + 3):
                    if n < DIFF_HEADS:
                        for m in range(2):
                            q = dq_pad[:, 2 * n + m]
                            one_tile(T(f"dS{n}", m), lambda o: [
                                (o[:, 0:128], q[:, 0:P], dk[:, n, 0:P]),
                                (o[:, 128:384], q[:, P:S], dk[:, n, :])])
                    if n < 10:
                        ada(2, n, n + 1)
                    if 2 <= n < DIFF_HEADS + 2:
                        h = n - 2
                        pe.wait_ge(soft_p, h + 1)
                        t = T(f"dT{h}")
                        o = open_tile(t)
                        for c in range(3):
                            src = (0, 128, 256)[c]
                            r = pe.transpose(o[:, src:src + P], da[:, h % 2, src:src + P], ident)
                        r.then_inc(filled[t % 8], 1)
                    if n >= 3:
                        h = n - 3
                        is_moved(pe, T(f"dT{h}"))
                        one_tile(T(f"dO{h}"), lambda o: [
                            (o[:, 0:256], dv[:, 0, P * h:P * h + P], daT[:, h % 2, 0:256], True, False),
                            (o[:, 128:256], dv[:, 1, P * h:P * h + P], daT[:, h % 2, 256:384], False, True)])
                for i in range(4):
                    pe.wait_ge(ret_done, 2 + i)
                    one_tile(T("dV", i), lambda o: [(o[:, :], ones, dsq[:, 2 * i:2 * i + 2])])
                ada(2, 10, 12)
                waited = set()

                def normed(k):
                    if k // 2 not in waited:
                        pe.wait_ge(o_done, 2 + k // 2)
                        waited.add(k // 2)
                    return o1[:, k]

                for g in range(2):
                    project(f"out1.{g}", normed, S)
                ada_sums(2, "a")
                ada_sums(2, "b")
                ln_sums("ln1a", 3)

            def routing(l):
                m = moe[l]
                pe.wait_ge(u_act, 8 + 8 * l)
                pe.wait_ge(u_dve, 8 + 8 * l)
                pe.wait_ge(wroute_in, 32 * (l + 1))
                t = T(f"route{l}")
                b = open_tile(t)
                for tb in range(2):
                    for k in range(KT):
                        r = mm(b[:, 36 * tb:36 * tb + 36], u[:, 0, k, P * tb:P * tb + P],
                               wroute[:, 36 * k:36 * k + 36], k == 0, k == KT - 1)
                r.then_inc(filled[t % 8], 1)
                for i in range(4):
                    t = T(f"route{l}", 1 + i)
                    b = open_tile(t)
                    for j in range(4):
                        n = 4 * i + j
                        r = pe.transpose(b[:, P * j:P * j + P], x[:, n % KT, P * (n // KT):P * (n // KT) + P], ident)
                    r.then_inc(filled[t % 8], 1)
                pe.wait_ge(route_dve, 2 * l + 1)
                t = T(f"route{l}", 5)
                ch = route[:, R_CH:R_CH + 64]
                one_tile(t, lambda o: [
                    (o[:, 0:32], K("before"), ch[:, 0:32]),
                    (o[:, 32:64], K("before"), ch[:, 32:64], True, False),
                    (o[:, 32:64], ones, ch[:, 0:32], False, True),
                    (o[:, 64:96], ones, ch[:, 0:32], True, False),
                    (o[:, 64:96], ones, ch[:, 32:64], False, True)])
                pe.wait_ge(route_dve, 2 * l + 2)
                for i in range(2):
                    t = T(f"route{l}", 6 + i)
                    b = open_tile(t)
                    for j in range(4):
                        v, tb = 2 * i + j // 2, j % 2
                        at = R_BC + P * (4 * i + j)
                        r = mm(b[:, P * j:P * j + P], route[:, at:at + P], ident)
                    r.then_inc(filled[t % 8], 1)

            def experts(l):
                m = moe[l]
                last = T(f"route{l}", 7)
                for t in range(last - 7, last + 1):
                    is_moved(pe, t)
                pe.wait_ge(info_done, l + 1)
                n = pe.value_load(info[0:1, 0:1], min_val=0, max_val=MAX_GROUPS - 1) + 1
                with pe.Fori(0, n) as i:
                    pe.wait_ge(m["selected"], i + 1)
                    pe.wait_ge(m["summed"], 4 * i + 1)
                    for k in range(KT):
                        o = bank[k // 4][:, P * (k % 4):P * (k % 4) + P]
                        mm(o, xnat[:, 0, P * k:P * k + P], sel[:, 0], True, False)
                        r = mm(o, xnat[:, 1, P * k:P * k + P], sel[:, 1], False, True)
                        if k % 4 == 3:
                            r.then_inc(m["gathered"], 1)
                    pe.wait_ge(m["xg_by_act"], 4 * i + 4)
                    pe.wait_ge(m["xg_by_dve"], 4 * i + 4)
                    for ph in range(4):
                        o = bank[2 + ph // 2]
                        for j in range(GRP):
                            r_ = (lead0[l] + 4 * ph + j) % RING
                            pe.wait_ge(mloaded[l][r_], 16 * (2 * i + (1 if ph < 3 else 2)))
                        for k in range(4):
                            for j in range(GRP):
                                w = ring[:, (lead0[l] + 4 * ph + j) % RING, :].rearrange("p (k n) -> p k n", k=4)
                                r = mm(o[32 * j:32 * j + 32, :], xg[:, 4 * (ph % 2) + k, 32 * j:32 * j + 32], w[:, k],
                                       ph % 2 == 0 and k == 0, ph % 2 == 1 and k == 3)
                        r.then_inc(m["phase"], 1)
                    pe.wait_ge(m["hidden"], i + 1)
                    for f in range(4):
                        r = pe.transpose(bank[4][:, P * f:P * f + P], hid[:, P * f:P * f + P], ident)
                    r.then_inc(m["turned"], 1)
                    pe.wait_ge(m["turned_out"], i + 1)
                    for ph in (4, 5):
                        for j in range(GRP):
                            r_ = (lead0[l] + 4 * ph + j) % RING
                            pe.wait_ge(mloaded[l][r_], 16 * (2 * i + 2))
                        for k in range(2):
                            f = 2 * (ph - 4) + k
                            for c in range(2):
                                for j in range(GRP):
                                    w = ring[:, (lead0[l] + 4 * ph + j) % RING, :].rearrange("p (k n) -> p k n", k=2)
                                    r = mm(bank[5 + c][32 * j:32 * j + 32, :], hidT[:, f, 32 * j:32 * j + 32],
                                           w[:, k, 512 * c:512 * c + 512], f == 0, f == 3)
                        r.then_inc(m["phase"], 1)
                    pe.wait_ge(m["y_by_act"], i + 1)
                    pe.wait_ge(m["y_by_dve"], i + 1)
                    pe.wait_ge(m["spread_ready"], i + 1)
                    for c, b in enumerate((7, 4, 0, 1)):
                        for k in range(2):
                            n_ = 2 * c + k
                            r = mm(bank[b][:, S * k:S * k + S], ysb[:, P * n_:P * n_ + P], selT)
                        r.then_inc(m["scattered"], 1)
                pe.wait_ge(m["summed"], 4 * n + 1)

            def rms_sums(name, n_sq, streams):
                sqv = W(0, 2, KT, S)
                square_sums(T(name), n_sq, S * streams, lambda k: sqv[:, 0:streams, k])

            def u_in(base, streams):
                seen = set()

                def rhs(k):
                    if k not in seen:
                        pe.wait_ge(u_act, base + k + 1)
                        seen.add(k)
                    return both(u, k) if streams == 2 else u[:, 0, k]
                return rhs

            def head_sums(L, i):
                width = 512 if L == 2 or i >= 8 else S
                pe.wait_ge(nsq_done, NB[L] + i + 1)
                one_tile(NT(L, i), lambda o: [(o[:, 0:width], K("blk64"), nsq(i, width))])

            def rotate(i):
                pe.wait_ge(nrm_q, i + 1)
                src = wq[:, i, 0] if i < 8 else kraw[:, i - 8, 0]
                one_tile(RT(i), lambda o: [(o[:, 0:S], K("rot"), src)])

            def attention(L):
                units = UNITS[L]
                for n in range(len(units) + 3):
                    if n < len(units):
                        s, h = units[n]
                        for qb in range(2 if s == 0 else 1):
                            t = T(f"aS{L}.{n}", qb)
                            if L == 2:
                                kp = kpad[:, 2 * (h // 4) + h % 2]
                                if s == 0:
                                    one_tile(t, lambda o: [(o[:, :], wq[:, h // 2, 0, P * qb:P * qb + P], kp)])
                                else:
                                    one_tile(t, lambda o: [(o[:, S * b:S * b + S], wq[:, h // 2, 1, P * b:P * b + P],
                                                            kp[:, S:2 * S]) for b in range(2)])
                            else:
                                one_tile(t, lambda o: [(o[:, :], nq_pad[:, h, P * qb:P * qb + P],
                                                        nk[:, h // 2])])
                    if L == 2 and n < 24 and n % 2 == 0:
                        ada(3, n // 2, n // 2 + 1)
                    if 2 <= n < len(units) + 2:
                        v = n - 2
                        s, h = units[v]
                        for qb in range(2 if s == 0 else 1):
                            t = T(f"aT{L}.{v}", qb)
                            q = next(n_ for n_, e in enumerate(SEQ[L]) if e[0] == v and e[3] == qb)
                            z = zbuf[L][q % 6]
                            pe.wait_ge(soft_p, SB0[L] + q + 1)
                            o = open_tile(t)
                            for kb in range(4):
                                r = pe.transpose(o[:, P * kb:P * kb + P], z[:, P * kb:P * kb + P], ident)
                            r.then_inc(filled[t % 8], 1)
                    if n >= 4 and n % 2 == 0:
                        pair = (n - 4) // 2
                        s = units[2 * pair][0]
                        t = T(f"aO{L}.{pair}")
                        for v in (2 * pair, 2 * pair + 1):
                            is_moved(pe, T(f"aT{L}.{v}"))
                            if s == 0:
                                is_moved(pe, T(f"aT{L}.{v}", 1))
                        calls = []
                        o = B(t)
                        nkb = 4 if s == 0 else 2
                        for kb in range(nkb):
                            for j in range(2):
                                v = 2 * pair + j
                                h = units[v][1]
                                if L == 2:
                                    val = wv[:, kb + (0 if s == 0 else 2), 64 * (h // 4):64 * (h // 4) + 64]
                                else:
                                    val = nv[:, kb, 64 * h:64 * h + 64]
                                calls.append((o[64 * j:64 * j + 64, 0:S], val, pT[:, v % 4, kb], kb == 0, kb == nkb - 1))
                        one_tile(t, lambda o: calls)
                for pair in range(len(units) // 2):
                    is_moved(pe, T(f"aO{L}.{pair}"))

            def ffn(L):
                streams = 2 if L == 2 else 1
                rhs = u_in(U_N[L][1], streams)
                width = S * streams
                for g in range(11):
                    project(f"gu{L}.{g}", rhs, width)
                for i in range(8):
                    open_tile(T(f"down{L}", i))
                for g in (9, 10):
                    for i in range(4):
                        is_moved(pe, T(f"gu{L}.{g}", i))
                for i in range(FFT // 2):
                    w = slot(slot0[f"down{L}"] + i)
                    for k in range(2):
                        f = 2 * i + k
                        for c in range(8):
                            t = T(f"down{L}", c)
                            r = mm(B(t)[:, 0:width], w[:, k, P * c:P * c + P], hidden[:, f, 0:streams],
                                   f == 0, f == FFT - 1)
                            if f == FFT - 1:
                                r.then_inc(filled[t % 8], 1)
                            elif k == 1 and c == 7:
                                r.then_inc(down_used, 1)

            def second(L):
                streams = 2 if L == 2 else 1
                rms_sums(f"rms{L}a", RMS_N[L][0], 2)
                ru = u_in(U_N[L][0], 2)
                if L == 2:
                    for g in range(3):
                        w = panel_slots(f"in2.{g}")
                        for kind, i in panels2[g]:
                            if kind == "in":
                                c = P * (i % 4)
                                one_tile(tile2["in", i], lambda o: [
                                    (o[:, :], w(k)[:, c:c + P], ru(k), k == 0, k == KT - 1) for k in range(KT)])
                            elif kind == "v":
                                one_tile(tile2["v", i], lambda o: [
                                    (o[:, 0:S], u[:, i // 2, k, P * (i % 2):P * (i % 2) + P], w(k)[:, S:2 * S],
                                     k == 0, k == KT - 1) for k in range(KT)])
                            elif kind == "nrm":
                                head_sums(2, i)
                            else:
                                rotate(i)
                    pe.wait_ge(nrm_done, 10)
                    for kv in range(HKV):
                        for d in range(2):
                            lo = CONST["halves"][0] + 64 + 128 * (kv % 2) - 64 * d
                            one_tile(T("kpad", 2 * kv + d), lambda o: [
                                (o[:, :], const[:, lo:lo + P], kraw[:, kv // 2])])
                    for i in range(8):
                        is_moved(pe, T("kpad", i))
                    for i in range(4):
                        is_moved(pe, tile2["v", i])
                else:
                    for g in range(2):
                        project(f"in3.{g}", lambda k: ru(k)[:, 0], S)
                    for g in range(2, 6):
                        w = panel_slots(f"in3.{g}")
                        for i in range(4):
                            if g < 4:
                                one_tile(IT(g, i), lambda o: [
                                    (o[:, :], w(k)[:, P * i:P * i + P], ru(k), k == 0, k == KT - 1) for k in range(KT)])
                            else:
                                one_tile(IT(g, i), lambda o: [
                                    (o[:, :], u[:, i // 2, k, P * (i % 2):P * (i % 2) + P], w(k), k == 0, k == KT - 1)
                                    for k in range(KT)])
                            head_sums(3, 4 * (g - 2) + i)
                    pe.wait_ge(nrm_q, 26)
                    for g in (4, 5):
                        for i in range(4):
                            is_moved(pe, IT(g, i))
                attention(L)
                for g in range(2):
                    project(f"out{L}.{g}", (lambda k: both(u, k)) if L == 2 else (lambda k: u[:, 0, k]), S * streams)
                if L == 2:
                    ada_sums(3, "a")
                    ada_sums(3, "b")
                rms_sums(f"rms{L}b", RMS_N[L][1], streams)
                ffn(L)

            even()
            routing(0)
            experts(0)
            ln_sums("ln0b", 2)
            odd()
            routing(1)
            experts(1)
            ln_sums("ln1b", 4)
            second(2)
            second(3)

        @block.scalar
        def _(act):
            def f(o, i, func, **kw):
                return act.activation(o, i, func, **kw)

            cnt = {"cent": 0, "x": 0, "u": 0}

            def deviation(tile, o, width, n, eps):
                is_filled(act, tile)
                f(o, B(tile)[:, 0:width], ACT.Sqrt, scale=1.0 / n, bias=K(eps)).then_inc(moved[tile % 8], 1)

            def layer_norm(name, which, L):
                for k in range(KT):
                    cnt["cent"] += 1
                    act.wait_ge(cent_done, cnt["cent"])
                    f(X(S * k, S), x[:, k], ACT.Square).then_inc(sq_act, 1)
                deviation(T(name, 1), X(2048, S), S, D, "eps_ln")
                for k in range(KT):
                    cnt["cent"] += 1
                    act.wait_ge(cent_done, cnt["cent"])
                    f(x[:, k], x[:, k], ACT.Identity, bias=C(f"ln{which}_b", KT * L + k, 1)).then_inc(x_act, 1)
                cnt["x"] += KT

            def modulate(L, half):
                act.wait_ge(mod_done, 2 * L + 1 + half)
                if L or half:
                    act.wait_ge(x_act, cnt["x"])
                for k in range(4):
                    f(u[:, 0, k], x[:, k], ACT.Identity, scale=mod[:, L, 24 * half + 8 + k, 0:1],
                      bias=mod[:, L, 24 * half + k, 0:1]).then_inc(u_act, 1)
                cnt["u"] += 4

            def scale_residual():
                act.wait_ge(u_dve, cnt["u"])
                f(x, x, ACT.Copy, scale=ALPHA).then_inc(xs_done, 1)

            def copy_tile(t, o, width, func=ACT.Copy, **kw):
                is_filled(act, t)
                f(o, B(t)[:, 0:width], func, **kw).then_inc(moved[t % 8], 1)

            def pad_heads(t, o0, o1_):
                is_filled(act, t)
                f(o0, B(t)[:, 0:S], ACT.Identity, scale=K("halfcol")[:, 0:1])
                f(o1_, B(t)[:, 0:S], ACT.Identity, scale=K("halfcol")[:, 1:2]).then_inc(moved[t % 8], 1)

            def even():
                modulate(0, 0)
                for i in range(4):
                    pad_heads(T("even.0", i), sq_pad[:, 2 * i], sq_pad[:, 2 * i + 1])
                scale_residual()
                for i in range(4):
                    copy_tile(T("even.4", i), rk[:, i], S, scale=128 ** -0.5)
                for i in range(2):
                    copy_tile(T("even.5", i), rv[:, i], 512)
                for i in range(4):
                    copy_tile(T("even.6", i), rg[:, i], S, ACT.Silu)
                for b in range(2):
                    act.wait_ge(sb_d, b + 1)
                    f(sb_l, sb_l, ACT.Exp).then_inc(chain_a, 1)
                    act.wait_ge(chain_a, b + 1)
                    f(sb_l, sb_l, ACT.Ln, bias=K("one")).then_inc(sb_e, 1)
                    act.wait_ge(sb_a, b + 1)
                    f(sb_l, sb_z, ACT.Exp).then_inc(sb_w, 1)
                    for i in range(2):
                        copy_tile(T(f"sbO{b}", i), o1[:, 2 * b + i], S)
                for h in range(2):
                    deviation(T("retV", h), X(512 * h, 512), 512, P, "eps_ln")
                layer_norm("ln0a", 1, 0)

            def odd():
                modulate(1, 0)
                for g in range(2):
                    for i in range(4):
                        t = 4 * g + i
                        pad_heads(T(f"odd.{g}", i), dq_pad[:, 2 * t], dq_pad[:, 2 * t + 1])
                scale_residual()
                for i in range(2):
                    copy_tile(T("odd.4", i), dv[:, i, 0:512], 512)
                copy_tile(T("lam"), tiny[:, 2:4], 2, ACT.Exp)
                for n in range(DIFF_HEADS + 4):
                    if n < DIFF_HEADS:
                        act.wait_ge(soft_z, n + 1)
                        sm = tiny[:, 16 + 16 * (n % 2):32 + 16 * (n % 2)]
                        for m in range(2):
                            for qb, (lo, hi) in enumerate(((0, 128), (128, 384))):
                                c = 2 * m + qb
                                z = dz3[n % 3][:, m, lo:hi]
                                r = f(z, z, ACT.Exp, bias=sm[:, 4 + c:5 + c], accum_out=sm[:, 8 + c:9 + c])
                        r.then_inc(soft_e, 1)
                    if 2 <= n < DIFF_HEADS + 2:
                        h = n - 2
                        if h >= 2:
                            is_filled(act, T(f"dO{h - 2}"))
                        copy_tile(T(f"dT{h}"), daT[:, h % 2], 384)
                    if n >= 4:
                        copy_tile(T(f"dO{n - 4}"), o1[:, n - 4], S)
                for i in range(4):
                    deviation(T("dV", i), dr[:, 2 * i:2 * i + 2], 512, P, "eps_ln")
                layer_norm("ln1a", 1, 1)

            def experts(l):
                m = moe[l]
                modulate(l, 1)
                act.wait_ge(route_dve, 2 * l + 1)
                f(route[:, R_EXP:R_EXP + 10], route[:, R_EXP:R_EXP + 10], ACT.Exp).then_inc(route_act, 1)
                for i in range(2):
                    copy_tile(T(f"route{l}", 1 + i), xnat[:, 0, 512 * i:512 * i + 512], 512)
                is_filled(act, T(f"route{l}", 4))
                scale_residual()
                for i in range(2):
                    copy_tile(T(f"route{l}", 6 + i), drow[:, 2 * i:2 * i + 2], 512)
                act.wait_ge(info_done, l + 1)
                n = act.value_load(info[0:1, 0:1], min_val=0, max_val=MAX_GROUPS - 1) + 1
                with act.Fori(0, n) as i:
                    act.wait_ge(m["gathered"], 2 * i + 1)
                    for k in range(4):
                        f(xg[:, k], bank[0][:, P * k:P * k + P], ACT.Identity, scale=mod[:, l, 32 + k, 0:1],
                          bias=mod[:, l, 24 + k, 0:1]).then_inc(m["xg_by_act"], 1)
                    act.wait_ge(m["phase"], 6 * i + 2)
                    f(sil, bank[2][:, :], ACT.Silu).then_inc(m["silu"], 1)
                    act.wait_ge(m["turned"], i + 1)
                    f(hidT.rearrange("p a b -> p (a b)"), bank[4][:, :], ACT.Copy).then_inc(m["turned_out"], 1)
                    act.wait_ge(m["phase"], 6 * i + 6)
                    f(ysb[:, 0:512], bank[5][:, :], ACT.Copy).then_inc(m["y_by_act"], 1)
                layer_norm(f"ln{l}b", 2, l)

            def rms(L, half, streams, name):
                if half == 0 and L == 2:
                    act.wait_ge(second_in, 16)
                    act.wait_ge(x_act, 4 * KT)
                sqv = W(0, 2, KT, S)
                for k in range(KT):
                    if half == 1:
                        is_moved(act, T(f"out{L}.{k // 4}", k % 4))
                    elif L == 3:
                        is_moved(act, T("down2", k))
                    f(sqv[:, 0:streams, k], res[:, 0:streams, k], ACT.Square).then_inc(sq_act, 1)
                deviation(T(name), X(0, S * streams), S * streams, D, "eps_rms")
                act.wait_ge(mod_done, 2 * L + 1 + half)
                for k in range(KT):
                    cnt["cent"] += 1
                    act.wait_ge(cent_done, cnt["cent"])
                    for s in range(streams):
                        r = f(u[:, s, k], u[:, s, k], ACT.Identity, bias=mod[:, L, 24 * half + k, s:s + 1])
                    r.then_inc(u_act, 1)

            def head_norms(L):
                def square(i):
                    if L == 3 and i < 8:
                        src, width = nq_pad[:, 2 * i], S
                        is_moved(act, T(f"in3.{i // 4}", i % 4))
                    elif L == 3:
                        src, width = nk[:, i - 8], 512
                        is_moved(act, IT(i // 4, i % 4))
                    else:
                        src, width = (wq[:, i] if i < 8 else kraw[:, i - 8]), 512
                        is_moved(act, tile2["in", i])
                    if i >= 2:
                        is_filled(act, NT(L, i - 2))
                    f(nsq(i, width), src, ACT.Square).then_inc(nsq_done, 1)

                if L == 2:
                    for kind, i in steps2:
                        if kind == "in":
                            copy_tile(tile2["in", i], wq[:, i] if i < 8 else kraw[:, i - 8], 512)
                            square(i)
                        elif kind == "nrm":
                            if i >= 2:
                                act.wait_ge(nrm_q, i - 1)
                            deviation(NT(2, i), X(2048 + 512 * (i % 2), 512), 512, 64, "eps_rms")
                    return
                square(0)
                for i in range(16):
                    if i + 1 < 16:
                        square(i + 1)
                    width = S if i < 8 else 512
                    if 8 <= i < 12:
                        copy_tile(IT(4, i - 8), nv[:, i - 8, 0:512], 512)
                    if i >= 2:
                        act.wait_ge(nrm_q, NB[L] + i - 1)
                    deviation(NT(L, i), X(2048 + 512 * (i % 2), width), width, 64, "eps_rms")

            def attention(L):
                seqs = SEQ[L]

                def exps(q):
                    v, s, h, qb, tS, tT = seqs[q]
                    act.wait_ge(soft_z, SB0[L] + q + 1)
                    sm = tiny[:, 16 + 16 * (q % 4):32 + 16 * (q % 4)]
                    z = zbuf[L][q % 6]
                    if s == 0:
                        f(z[:, S:2 * S], B(tS)[:, S:2 * S], ACT.Exp, bias=sm[:, 4:5],
                          accum_out=sm[:, 6:7]).then_inc(moved[tS % 8], 1)
                        if L == 2:
                            f(sm[:, 8:9], C("sink", h, 1), ACT.Exp, bias=sm[:, 4:5])
                        f(z[:, 0:S], z[:, 0:S], ACT.Exp, bias=sm[:, 4:5], accum_out=sm[:, 7:8]).then_inc(soft_e, 1)
                    else:
                        for b in range(2):
                            r = f(z[:, S * b:S * b + S], B(tS)[:, S * b:S * b + S], ACT.Exp, bias=sm[:, 4 + b:5 + b],
                                  accum_out=sm[:, 6 + b:7 + b])
                        r.then_inc(moved[tS % 8], 1)
                        f(sm[:, 8:10], sm[:, 4:6], ACT.Exp, bias=C("sink", h, 1)).then_inc(soft_e, 1)

                def turned(q):
                    v, s, h, qb, tS, tT = seqs[q]
                    if v >= 4:
                        is_filled(act, T(f"aO{L}.{(v - 4) // 2}"))
                    if s == 0:
                        copy_tile(tT, pT[:, v % 4, :, P * qb:P * qb + P], 512)
                    else:
                        for b in range(2):
                            is_filled(act, tT)
                            r = f(pT[:, v % 4, 0:2, P * b:P * b + P], B(tT)[:, S * b:S * b + S], ACT.Copy)
                        r.then_inc(moved[tT % 8], 1)

                for n in range(len(UNITS[L]) + 2):
                    for q, e in enumerate(seqs):
                        if e[0] == n:
                            exps(q)
                    for q, e in enumerate(seqs):
                        if e[0] == n - 2:
                            turned(q)

            def second(L):
                rms(L, 0, 2, f"rms{L}a")
                if L == 2:
                    head_norms(2)
                    for i in range(0, 8, 2):
                        copy_tile(T("kpad", i), kpad[:, i], 512)
                else:
                    for i in range(8):
                        copy_tile(T(f"in3.{i // 4}", i % 4), nq_pad[:, 2 * i], S)
                    head_norms(3)
                attention(L)
                streams = 2 if L == 2 else 1
                rms(L, 1, streams, f"rms{L}b")
                for n in range(FFT):
                    copy_tile(T(f"gu{L}.{n // 4}", n % 4), hidden[:, n, 0:streams], S * streams, ACT.Silu)

            act.dma_start(cols[:, :], a["cols"]).then_inc(cols_in, 16)
            act.dma_start(const[:, :], a["const"]).then_inc(const_in, 16)
            act.dma_start(x, a["x"]).then_inc(first_in, 16)
            act.dma_start(first, a["first"]).then_inc(first_in, 16)
            act.wait_ge(cols_in, 16)
            f(cond[:, :], cols[:, 0:24], ACT.Silu).then_inc(cond_done, 1)
            act.wait_ge(const_in, 16)
            act.wait_ge(first_in, 32)
            even()
            experts(0)
            odd()
            experts(1)
            second(2)
            second(3)

        @block.vector
        def _(dve):
            cnt = {"chain": 0, "cent": 0, "x": 0, "u": 0, "xs": 0}

            def step(ins):
                cnt["chain"] += 1
                ins.then_inc(chain_v, 1)
                dve.wait_ge(chain_v, cnt["chain"])

            tt, ts, stt = dve.tensor_tensor, dve.tensor_scalar, dve.scalar_tensor_tensor

            def ada(L, g0, g1):
                for g in range(g0, g1):
                    t = T(f"ada{L}.{g}")
                    if L or g:
                        dve.wait_ge(chain_adac, 12 * L + g)
                    is_filled(dve, t)
                    dve.transpose(adaT[:, :], B(t)[:, :]).then_inc(moved[t % 8], 1)
                    is_moved(dve, t)
                    v = adaT[:, :].rearrange("p (a q c r) -> p q a c r", a=4, q=4, c=2)
                    for c in range(2):
                        r = dve.tensor_copy(adac[:, :, 4 * g:4 * g + 4, c], v[:, :, :, c, 0])
                    r.then_inc(chain_adac, 1)

            def ada_sums(L, part):
                t = T(f"adafin{L}{part}")
                a0, a1 = (0, 16) if part == "a" else (16, 48)
                is_filled(dve, t)
                bias = C("b_ada", 48 * L + a0, a1 - a0).unsqueeze(2).broadcast_to([P, a1 - a0, 2])
                tt(mod[:, L, a0:a1], B(t)[:, 0:2 * (a1 - a0)].rearrange("p (a c) -> p a c", c=2), bias,
                   ALU.add).then_inc(moved[t % 8], 1)
                is_moved(dve, t)
                if L < 2 and part == "b":
                    ts(mod[:, L, 16:24], mod[:, L, 16:24], 1.0, None, ALU.add)
                at, name = (8, "g_mix") if part == "a" else (32, "g_ffn")
                if L < 2:
                    n = 8 if part == "a" else 16
                    r = ts(mod[:, L, at:at + n], mod[:, L, at:at + n], 1.0, None, ALU.add)
                else:
                    g = C(name, KT * (L - 2), KT).unsqueeze(2).broadcast_to([P, KT, 2])
                    r = stt(mod[:, L, at:at + 8], mod[:, L, at:at + 8], 1.0, g, ALU.add, ALU.mult)
                r.then_inc(mod_done, 1)
                dve.wait_ge(mod_done, 2 * L + (1 if part == "a" else 2))

            def modulate(L, half):
                if L or half:
                    dve.wait_ge(x_act, cnt["x"])
                for k in range(4, 8):
                    ts(u[:, 0, k], x[:, k], mod[:, L, 24 * half + 8 + k, 0:1], mod[:, L, 24 * half + k, 0:1],
                       ALU.mult, ALU.add).then_inc(u_dve, 1)
                cnt["u"] += 4

            def copy_tile(t, o, width):
                is_filled(dve, t)
                dve.tensor_copy(o, B(t)[:, 0:width]).then_inc(moved[t % 8], 1)

            def layer_norm(name, which, L):
                t = T(name)
                dve.wait_ge(res_ready, res_n["dve"])
                is_filled(dve, t)
                for k in range(KT):
                    stt(x[:, k], B(t)[:, 0:S], -1.0 / D, x[:, k], ALU.mult, ALU.add).then_inc(cent_done, 1)
                cnt["cent"] += KT
                dve.wait_ge(cent_done, cnt["cent"])
                dve.tensor_copy(tiny[:, 90:91], tiny[:, 91:92]).then_inc(moved[t % 8], 1)
                invert(T(name, 1), X(2048, S))
                for k in range(KT):
                    stt(x[:, k], x[:, k], C(f"ln{which}_g", KT * L + k, 1), X(2048, S), ALU.mult,
                        ALU.mult).then_inc(cent_done, 1)
                cnt["cent"] += KT
                cnt["x"] += KT

            def invert(t, v):
                is_moved(dve, t)
                step(dve.reciprocal(v, v))

            res_n = {"dve": 0}

            def add_mixer(L):
                cnt["xs"] += 1
                dve.wait_ge(xs_done, cnt["xs"])
                for g in range(2):
                    for i in range(4):
                        t, k = T(f"out{L}.{g}", i), 4 * g + i
                        is_filled(dve, t)
                        stt(x[:, k], B(t)[:, 0:S], mod[:, L, 16 + k, 0:1], x[:, k], ALU.mult,
                            ALU.add).then_inc(moved[t % 8], 1)
                for i in range(4):
                    is_moved(dve, T(f"out{L}.1", i))
                    is_moved(dve, T(f"out{L}.0", i))
                dve.tensor_copy(tiny[:, 90:91], tiny[:, 91:92]).then_inc(res_ready, 1)
                res_n["dve"] += 1

            def even():
                dve.memset(tiny[:, :], 0.0).then_inc(chain_v, 1)
                cnt["chain"] += 1
                dve.wait_ge(chain_v, cnt["chain"])
                dve.wait_ge(cond_done, 1)
                dve.tensor_copy(condrep[:, :, :], cond[:, 0:8].unsqueeze(2).broadcast_to([P, KT, 32]))\
                   .then_inc(condrep_done, 1)
                ada(0, 0, 4)
                dve.wait_ge(cols_in, 16)
                ada_sums(0, "a")
                dve.wait_ge(const_in, 16)
                dve.wait_ge(first_in, 32)
                modulate(0, 0)
                ada(0, 4, 5)
                for i in range(4):
                    copy_tile(T("even.1", i), sk[:, i], S)
                ada(0, 5, 6)
                for i in range(2):
                    copy_tile(T("even.2", i), sv[:, i], 512)
                ada(0, 6, 7)
                for i in range(4):
                    copy_tile(T("even.3", i), rq[:, i], S)
                ada(0, 7, 12)
                ada_sums(0, "b")
                for b in range(2):
                    if b:
                        is_filled(dve, T("sbO0", 1))
                    for i in range(4):
                        t = T(f"sbS{b}", i)
                        is_filled(dve, t)
                        tt(sb_z[:, i], B(t)[:, 0:384], K("sbmask"), ALU.add).then_inc(moved[t % 8], 1)
                    for i in range(4):
                        is_moved(dve, T(f"sbS{b}", i))
                    step(ts(sb_t, sb_z, 0.0, None, ALU.max))
                    stt(sb_l, sb_t, -2.0, sb_z, ALU.mult, ALU.add).then_inc(sb_d, 1)
                    ada(1, 4 * b, 4 * b + 3)
                    dve.wait_ge(sb_e, b + 1)
                    tt(sb_l, sb_l, sb_t, ALU.add).then_inc(sb_sp, 1)
                    for i in range(4):
                        t = T(f"sbR{b}", i)
                        is_filled(dve, t)
                        tt(sb_z[:, i], sb_z[:, i], B(t)[:, 0:384], ALU.subtract).then_inc(moved[t % 8], 1)
                    for i in range(4):
                        is_moved(dve, T(f"sbR{b}", i))
                    dve.tensor_copy(tiny[:, 90:91], tiny[:, 91:92]).then_inc(sb_a, 1)
                    ada(1, 4 * b + 3, 4 * b + 4)
                for h in range(4):
                    t = T("retS", h)
                    is_filled(dve, t)
                    tt(ret_p[:, h], B(t)[:, 0:384], decay[:, h], ALU.mult).then_inc(moved[t % 8], 1)
                is_filled(dve, T("sbO1", 1))
                ada(1, 8, 9)
                for h in range(4):
                    copy_tile(T("retO", h), ret_o[:, h], S)
                for h in range(2):
                    t = T("retM", h)
                    is_filled(dve, t)
                    v = ret_o[:, 2 * h:2 * h + 2]
                    stt(v, B(t)[:, :].rearrange("p (a s) -> p a s", a=2), -1.0 / P, v, ALU.mult,
                        ALU.add).then_inc(moved[t % 8], 1)
                    is_moved(dve, t)
                    r = tt(ret_s[:, 2 * h:2 * h + 2], v, v, ALU.mult)
                r.then_inc(ret_done, 1)
                ada(1, 9, 10)
                for h in range(2):
                    invert(T("retV", h), X(512 * h, 512))
                step(tt(ret_o, ret_o, X(0, 4, S), ALU.mult))
                for h in range(4):
                    is_moved(dve, T("even.6", h))
                    r = stt(o1[:, 4 + h], ret_o[:, h], C("ret_g", h, 1), rg[:, h], ALU.mult, ALU.mult)
                r.then_inc(o_done, 1)
                ada(1, 10, 12)
                add_mixer(0)
                ada_sums(1, "a")
                ada_sums(1, "b")
                layer_norm("ln0a", 1, 0)

            def odd():
                dve.tensor_copy(condrep[:, :, 0:16], cond[:, 8:16].unsqueeze(2).broadcast_to([P, KT, 16]))
                dve.tensor_copy(condrep[:, :, 16:32], cond[:, 16:24].unsqueeze(2).broadcast_to([P, KT, 16]))\
                   .then_inc(condrep_done, 1)
                modulate(1, 0)
                tt(tiny[:, 0:2], C("lam", 0, 2), C("lam", 2, 2), ALU.mult).then_inc(lam_p, 1)
                ts(tiny[:, 6:7], C("subln"), 1.0 - LAMBDA_INIT, None, ALU.mult)
                for g in (2, 3):
                    for i in range(4):
                        copy_tile(T(f"odd.{g}", i), dk[:, 4 * (g - 2) + i], S)
                for i in range(2):
                    copy_tile(T("odd.5", i), dv[:, i, 512:1024], 512)
                is_moved(dve, T("lam"))
                step(tt(tiny[:, 4:5], tiny[:, 3:4], tiny[:, 2:3], ALU.subtract))
                step(ts(tiny[:, 5:6], tiny[:, 4:5], -LAMBDA_INIT, None, ALU.add))
                for n in range(DIFF_HEADS + 2):
                    if n < DIFF_HEADS:
                        sm = tiny[:, 16 + 16 * (n % 2):32 + 16 * (n % 2)]
                        for m in range(2):
                            t = T(f"dS{n}", m)
                            is_filled(dve, t)
                            stt(dz3[n % 3][:, m], dist, -(2.0 ** -(n + 1)), B(t)[:, 0:384], ALU.mult,
                                ALU.add).then_inc(moved[t % 8], 1)
                        is_moved(dve, T(f"dS{n}", 0))
                        is_moved(dve, T(f"dS{n}", 1))
                        mx = sm[:, 0:4].rearrange("p (m q) -> p m q", m=2)
                        dve.tensor_reduce(mx[:, :, 0], dz3[n % 3][:, :, 0:128], AX_X, ALU.max)
                        step(dve.tensor_reduce(mx[:, :, 1], dz3[n % 3][:, :, 128:384], AX_X, ALU.max))
                        ts(sm[:, 4:8], sm[:, 0:4], -1.0, None, ALU.mult).then_inc(soft_z, 1)
                    if 1 <= n <= DIFF_HEADS:
                        h = n - 1
                        sm = tiny[:, 16 + 16 * (h % 2):32 + 16 * (h % 2)]
                        dve.wait_ge(soft_e, n)
                        step(dve.reciprocal(sm[:, 12:16], sm[:, 8:12]))
                        step(ts(sm[:, 14:16], sm[:, 14:16], tiny[:, 5:6], None, ALU.mult))
                        for qb, (lo, hi) in enumerate(((0, 128), (128, 384))):
                            r = ts(dz3[h % 3][:, 1, lo:hi], dz3[h % 3][:, 1, lo:hi], sm[:, 14 + qb:15 + qb], None, ALU.mult)
                        step(r)
                        if h >= 2:
                            is_filled(dve, T(f"dT{h - 2}"))
                        for qb, (lo, hi) in enumerate(((0, 128), (128, 384))):
                            r = stt(da[:, h % 2, lo:hi], dz3[h % 3][:, 0, lo:hi], sm[:, 12 + qb:13 + qb],
                                    dz3[h % 3][:, 1, lo:hi], ALU.mult, ALU.add)
                        r.then_inc(soft_p, 1)
                    ada(2, n, n + 1)
                for i in range(4):
                    pair = o1[:, 2 * i:2 * i + 2]
                    is_moved(dve, T(f"dO{2 * i}"))
                    is_moved(dve, T(f"dO{2 * i + 1}"))
                    tt(dsq[:, 2 * i:2 * i + 2], pair, pair, ALU.mult).then_inc(ret_done, 1)
                for i in range(4):
                    pair = o1[:, 2 * i:2 * i + 2]
                    invert(T("dV", i), dr[:, 2 * i:2 * i + 2])
                    stt(pair, pair, tiny[:, 6:7], dr[:, 2 * i:2 * i + 2], ALU.mult, ALU.mult).then_inc(o_done, 1)
                ada(2, 10, 12)
                add_mixer(1)
                ada_sums(2, "a")
                ada_sums(2, "b")
                layer_norm("ln1a", 1, 1)

            def routing(l):
                at = {"n": R_SMALL}

                def new(*dims):
                    n = int(np.prod(dims))
                    v = route[:, at["n"]:at["n"] + n]
                    at["n"] += n
                    assert at["n"] <= 2048
                    if len(dims) == 1:
                        return v
                    names = "abcd"[:len(dims)]
                    return v.rearrange(f"p ({' '.join(names)}) -> p {' '.join(names)}", **dict(zip(names, dims)))

                def wide(v, n):
                    return v.unsqueeze(2).broadcast_to([P, 2, n])

                def first_of(v, top, n, out_index, eq):
                    step(tt(eq, v, wide(top, n), ALU.is_equal))
                    step(stt(eq, eq, -1000.0, iota_of(n), ALU.mult, ALU.add))
                    step(dve.tensor_reduce(out_index, eq, AX_X, ALU.min))
                    step(ts(out_index, out_index, 1000.0, None, ALU.add))

                def iota_of(n):
                    return K("iota")[:, 0:n].unsqueeze(1).broadcast_to([P, 2, n])

                t = T(f"route{l}")
                is_filled(dve, t)
                lg = new(2, 36)
                logits = B(t)[:, 0:72].rearrange("p (a b) -> p a b", a=2)
                bias = C("b_route", 36 * l, 36).unsqueeze(1).broadcast_to([P, 2, 36])
                tt(lg, logits, bias, ALU.add).then_inc(moved[t % 8], 1)
                is_moved(dve, t)
                gl = lg[:, :, 0:4]
                gmax, grp, eq4, g1h = new(2), new(2), new(2, 4), new(2, 4)
                step(dve.tensor_reduce(gmax, gl, AX_X, ALU.max))
                ex = route[:, R_EXP:R_EXP + 10].rearrange("p (a b) -> p a b", a=2)
                tt(ex[:, :, 0:4], gl, wide(gmax, 4), ALU.subtract)
                first_of(gl, gmax, 4, grp, eq4)
                step(tt(g1h, iota_of(4), wide(grp, 4), ALU.is_equal))
                pick, ing, eq8 = new(2, 4, 8), new(2, 8), new(2, 8)
                for tb in range(2):
                    r = tt(pick[:, tb], lg[:, tb, 4:36].rearrange("p (g e) -> p g e", g=4),
                           g1h[:, tb].unsqueeze(2).broadcast_to([P, 4, 8]), ALU.mult)
                step(r)
                for tb in range(2):
                    r = dve.tensor_reduce(ing[:, tb], pick[:, tb].rearrange("p g e -> p e g"), AX_X, ALU.add)
                step(r)
                top, idx, rest = new(2, 2), new(2, 2), new(2, 8)
                step(dve.tensor_reduce(top[:, 0], ing, AX_X, ALU.max))
                first_of(ing, top[:, 0], 8, idx[:, 0], eq8)
                step(tt(eq8, iota_of(8), wide(idx[:, 0], 8), ALU.is_equal))
                step(stt(rest, eq8, NEG, ing, ALU.mult, ALU.add))
                step(dve.tensor_reduce(top[:, 1], rest, AX_X, ALU.max))
                first_of(rest, top[:, 1], 8, idx[:, 1], eq8)
                tt(ex[:, :, 4], top[:, 1], top[:, 0], ALU.subtract)
                eid, hot, ch = new(2, 2), new(2, 2, 32), route[:, R_CH:R_CH + 64].rearrange("p (a b) -> p a b", a=2)
                for c in range(2):
                    r = stt(eid[:, c], grp, float(PER_GROUP), idx[:, c], ALU.mult, ALU.add)
                step(r)
                for c in range(2):
                    r = tt(hot[:, c], iota_of(32), wide(eid[:, c], 32), ALU.is_equal)
                step(r)
                tt(ch, hot[:, 0], hot[:, 1], ALU.add).then_inc(route_dve, 1)
                for i in range(2):
                    copy_tile(T(f"route{l}", 3 + i), xnat[:, 1, 512 * i:512 * i + 512], 512)
                dve.memset(acc, 0.0).then_inc(moe[l]["summed"], 1)
                dve.tensor_copy(slotcol, K("pid"))
                t = T(f"route{l}", 5)
                is_filled(dve, t)
                rank = new(96)
                dve.tensor_copy(rank, B(t)[:, 0:96]).then_inc(moved[t % 8], 1)
                is_moved(dve, t)
                over, nblk, end, zero32 = W(5120, 32, 8), new(32), new(32), new(32)
                dve.memset(zero32, 0.0)
                step(tt(over, rank[:, 64:96].unsqueeze(2).broadcast_to([P, 32, 8]),
                        K("thresh").unsqueeze(1).broadcast_to([P, 32, 8]), ALU.is_gt))
                step(dve.tensor_reduce(nblk, over, AX_X, ALU.add))
                step(tt(nblk, nblk, K("lead"), ALU.subtract))
                step(ts(nblk, nblk, 0.0, None, ALU.max))
                step(dve.tensor_tensor_scan(end, nblk, zero32, 0.0, ALU.add, ALU.add))
                start = new(32)
                step(tt(start, end, nblk, ALU.subtract))
                step(ts(end, end, float(GRP), None, ALU.add))
                base, lower = new(32), new(32)
                step(tt(base, start, K("lead"), ALU.subtract))
                step(ts(base, base, float(GRP), float(BLK), ALU.add, ALU.mult))
                step(stt(lower, K("iota")[:, 0:32], float(BLK), base, ALU.mult, ALU.subtract))
                step(tt(lower, lower, K("lead"), ALU.mult))
                slots, in_lead, hs = new(2, 32), W(6144, 2, 32), W(5632, 2, 2, 32)
                rank2 = rank[:, 0:64].rearrange("p (a b) -> p a b", a=2)
                step(ts(in_lead, rank2, float(BLK), None, ALU.is_lt))
                step(tt(in_lead, in_lead, lower.unsqueeze(1).broadcast_to([P, 2, 32]), ALU.mult))
                step(tt(slots, rank2, base.unsqueeze(1).broadcast_to([P, 2, 32]), ALU.add))
                step(tt(slots, slots, in_lead, ALU.add))
                for c in range(2):
                    r = tt(hs[:, c], hot[:, c], slots, ALU.mult)
                step(r)
                step(dve.tensor_reduce(dest, hs, AX_X, ALU.add))
                dve.wait_ge(route_act, l + 1)
                den, gate = new(2, 2), new(2, 2)
                step(dve.tensor_reduce(den[:, 0], ex[:, :, 0:4], AX_X, ALU.add))
                step(ts(den[:, 1], ex[:, :, 4], 1.0, None, ALU.add))
                step(tt(den[:, 0], den[:, 0], den[:, 1], ALU.mult))
                step(dve.reciprocal(gate[:, 0], den[:, 0]))
                step(tt(gate[:, 1], gate[:, 0], ex[:, :, 4], ALU.mult))
                bc = route[:, R_BC:R_BC + 1024].rearrange("p (a b) -> p a b", b=P)
                for c in range(2):
                    for tb in range(2):
                        ts(bc[:, 2 * c + tb], ones, dest[:, c, tb:tb + 1], None, ALU.mult)
                        r = ts(bc[:, 4 + 2 * c + tb], ones, gate[:, c, tb:tb + 1], None, ALU.mult)
                r.then_inc(route_dve, 1)
                tb_ = W(5120, MAX_BLOCKS, 32)
                fl = W(7168, 64)
                step(tt(tb_[0:1], end[0:1].unsqueeze(1).broadcast_to([1, MAX_BLOCKS, 32]),
                        K("iota")[0:1, 0:MAX_BLOCKS].unsqueeze(2).broadcast_to([1, MAX_BLOCKS, 32]), ALU.is_le))
                step(dve.tensor_reduce(fl[0:1, 1:1 + MAX_BLOCKS], tb_[0:1], AX_X, ALU.add))
                step(ts(fl[0:1, 1:1 + MAX_BLOCKS], fl[0:1, 1:1 + MAX_BLOCKS], float(N_EXPERTS - 1), 1.0, ALU.min, ALU.add))
                step(dve.tensor_copy(fl[0:1, 1:1 + GRP], K("iota")[0:1, 1:1 + GRP]))
                step(tt(tb_[0:1, 0, 0:MAX_GROUPS], end[0:1, 31:32].broadcast_to([1, MAX_GROUPS]), K("gthresh")[0:1],
                        ALU.is_gt))
                step(dve.tensor_reduce(fl[0:1, 0:1], tb_[0:1, 0, 0:MAX_GROUPS], AX_X, ALU.add))
                dve.tensor_copy(info[0:1, 0:INFO], fl[0:1, 0:INFO]).then_inc(info_done, 1)

            def experts(l):
                m = moe[l]
                modulate(l, 1)
                routing(l)

                def select():
                    for tb in range(2):
                        r = ts(sel[:, tb], K("iota"), dest[:, 0, tb:tb + 1], None, ALU.is_equal)
                    r.then_inc(m["step"], 1)

                def select2():
                    for tb in range(2):
                        r = stt(sel[:, tb], K("iota"), dest[:, 1, tb:tb + 1], sel[:, tb], ALU.is_equal, ALU.add)
                    r.then_inc(m["selected"], 1)

                select()
                dve.wait_ge(m["step"], 1)
                select2()
                for i in range(2):
                    is_moved(dve, T(f"route{l}", 6 + i))
                n = dve.value_load(info[0:1, 0:1], min_val=0, max_val=MAX_GROUPS - 1) + 1
                STEPS = 3
                with dve.Fori(0, n) as i:
                    stt(selT, drow[:, 0], slotcol, drow[:, 2], ALU.is_equal, ALU.mult)
                    stt(selT2, drow[:, 1], slotcol, drow[:, 3], ALU.is_equal, ALU.mult).then_inc(m["step"], 1)
                    dve.wait_ge(m["step"], STEPS * i + 2)
                    tt(selT, selT, selT2, ALU.add).then_inc(m["spread_ready"], 1)
                    dve.wait_ge(m["gathered"], 2 * i + 2)
                    for k in range(4, 8):
                        ts(xg[:, k], bank[1][:, P * (k - 4):P * (k - 4) + P], mod[:, l, 32 + k, 0:1],
                           mod[:, l, 24 + k, 0:1], ALU.mult, ALU.add).then_inc(m["xg_by_dve"], 1)
                    ts(slotcol, slotcol, float(P), None, ALU.add)
                    ts(dest, dest, -float(P), None, ALU.add).then_inc(m["step"], 1)
                    dve.wait_ge(m["step"], STEPS * i + 3)
                    select()
                    dve.wait_ge(m["step"], STEPS * i + 4)
                    select2()
                    dve.wait_ge(m["silu"], i + 1)
                    dve.wait_ge(m["phase"], 6 * i + 4)
                    tt(hid, sil, bank[3][:, :], ALU.mult).then_inc(m["hidden"], 1)
                    dve.wait_ge(m["phase"], 6 * i + 6)
                    dve.tensor_copy(ysb[:, 512:1024], bank[6][:, :]).then_inc(m["y_by_dve"], 1)
                    for c, b in enumerate((7, 4, 0, 1)):
                        dve.wait_ge(m["scattered"], 4 * i + c + 1)
                        v = acc[:, 2 * c:2 * c + 2]
                        tt(v, v, bank[b][:, :].rearrange("p (a s) -> p a s", a=2), ALU.add).then_inc(m["summed"], 1)
                cnt["xs"] += 1
                dve.wait_ge(m["summed"], 4 * n + 1)
                dve.wait_ge(xs_done, cnt["xs"])
                for k in range(KT):
                    r = stt(x[:, k], acc[:, k], mod[:, l, 40 + k, 0:1], x[:, k], ALU.mult, ALU.add)
                r.then_inc(res_ready, 1)
                res_n["dve"] += 1
                layer_norm(f"ln{l}b", 2, l)

            def rms(L, half, streams, name):
                if half == 1:
                    for k in range(KT):
                        is_moved(dve, T(f"out{L}.{k // 4}", k % 4))
                elif L == 2:
                    dve.wait_ge(second_in, 16)
                    dve.wait_ge(x_act, 4 * KT)
                else:
                    for k in range(KT):
                        is_moved(dve, T("down2", k))
                invert(T(name), X(0, S * streams))
                for k in range(KT):
                    for s in range(streams):
                        r = stt(u[:, s, k], res[:, s, k], mod[:, L, 24 * half + 8 + k, s:s + 1], X(S * s, S),
                                ALU.mult, ALU.mult)
                    r.then_inc(cent_done, 1)
                cnt["cent"] += KT

            def add_second(L, names, gate, streams):
                for k, t in enumerate(names):
                    is_filled(dve, t)
                    for s in range(streams):
                        r = stt(res[:, s, k], B(t)[:, S * s:S * s + S], mod[:, L, gate + k, s:s + 1], res[:, s, k],
                                ALU.mult, ALU.add)
                    r.then_inc(moved[t % 8], 1)

            def head_norms(L):
                def rotate(i):
                    t = RT(i)
                    is_filled(dve, t)
                    v = wq[:, i, 0] if i < 8 else kraw[:, i - 8, 0]
                    w = X(3072 + S * (i % 2), S)
                    tt(w, B(t)[:, 0:S], rope[:, 256:512], ALU.mult).then_inc(moved[t % 8], 1)
                    step(tt(v, v, rope[:, 0:256], ALU.mult))
                    tt(v, v, w, ALU.add).then_inc(nrm_done, 1)

                if L == 2:
                    dve.wait_ge(rope_in, 16)
                    for kind, i in steps2:
                        if kind == "nrm":
                            r = X(2048 + 512 * (i % 2), 512)
                            invert(NT(2, i), r)
                            v = (wq[:, i] if i < 8 else kraw[:, i - 8]).rearrange("p s t -> p (s t)")
                            g = tiny[:, 8:9] if i < 8 else C("swa_gk")
                            stt(v, v, g, r, ALU.mult, ALU.mult).then_inc(nrm_q, 1)
                        elif kind == "rot":
                            rotate(i)
                        elif kind == "v":
                            copy_tile(tile2["v", i], wv[:, i], S)
                    return
                for i in range(16):
                    if i < 8:
                        copy_tile(IT(2 + i // 4, i % 4), nk[:, i], 512)
                    if i >= 12:
                        copy_tile(IT(5, i - 12), nv[:, i - 12, 512:1024], 512)
                    width = S if i < 8 else 512
                    r = X(2048 + 512 * (i % 2), width)
                    invert(NT(L, i), r)
                    if i < 8:
                        v = nq_pad[:, 2 * i]
                        step(stt(v, v, C("na_gq"), r, ALU.mult, ALU.mult))
                        step(ts(nq_pad[:, 2 * i + 1], v, K("halfcol")[:, 1:2], None, ALU.mult))
                        ts(v, v, K("halfcol")[:, 0:1], None, ALU.mult).then_inc(nrm_q, 1)
                    else:
                        v = nk[:, i - 8].rearrange("p s t -> p (s t)")
                        stt(v, v, C("na_gk"), r, ALU.mult, ALU.mult).then_inc(nrm_q, 1)

            def attention(L):
                seqs = SEQ[L]

                def shift(q):
                    v, s, h, qb, tS, tT = seqs[q]
                    sm = tiny[:, 16 + 16 * (q % 4):32 + 16 * (q % 4)]
                    z = zbuf[L][q % 6]
                    if q >= 6:
                        is_filled(dve, seqs[q - 6][5])
                    is_filled(dve, tS)
                    if s == 0:
                        step(dve.tensor_reduce(sm[:, 0:1], B(tS)[:, S:2 * S], AX_X, ALU.max))
                        if L == 2:
                            step(tt(sm[:, 0:1], sm[:, 0:1], C("sink", h, 1), ALU.max))
                            bias = rope[:, 512 + S * qb:512 + S * qb + S]
                            src, dst = B(tS)[:, 0:S], z[:, 0:S]
                        else:
                            if qb == 0:
                                b = h % 4
                                dve.wait_ge(bias_in[b], 32 * (h // 4 + 1))
                                tb = btab[:, b]
                                step(tt(tb, tb, K("namask").unsqueeze(1).broadcast_to([P, 6, GRID_W]), ALU.add))
                            j = 2 - 2 * qb
                            bias = btab[:, h % 4, j:j + 4].rearrange("p j w -> p (j w)")
                            src, dst = B(tS)[:, 0:S], z[:, 0:S]
                        step(dve.tensor_tensor_reduce(out=dst, in0=src, in1=bias, scale=1.0, scalar=sm[:, 0:1],
                                                      op0=ALU.add, op1=ALU.max, accum_out=sm[:, 1:2]))
                        ts(sm[:, 4:5], sm[:, 1:2], -1.0, None, ALU.mult).then_inc(soft_z, 1)
                    else:
                        step(dve.tensor_reduce(sm[:, 0:2], B(tS)[:, :].rearrange("p (b k) -> p b k", b=2), AX_X, ALU.max))
                        ts(sm[:, 4:6], sm[:, 0:2], C("sink", h, 1), -1.0, ALU.max, ALU.mult).then_inc(soft_z, 1)

                def norm(q):
                    v, s, h, qb, tS, tT = seqs[q]
                    sm = tiny[:, 16 + 16 * (q % 4):32 + 16 * (q % 4)]
                    z = zbuf[L][q % 6]
                    dve.wait_ge(soft_e, SB0[L] + q + 1)
                    if s == 0:
                        n = 3 if L == 2 else 2
                        step(dve.tensor_reduce(sm[:, 10:11], sm[:, 6:6 + n], AX_X, ALU.add))
                        step(dve.reciprocal(sm[:, 11:12], sm[:, 10:11]))
                        ts(z, z, sm[:, 11:12], None, ALU.mult).then_inc(soft_p, 1)
                    else:
                        step(tt(sm[:, 10:12], sm[:, 6:8], sm[:, 8:10], ALU.add))
                        step(dve.reciprocal(sm[:, 12:14], sm[:, 10:12]))
                        for b in range(2):
                            r = ts(z[:, S * b:S * b + S], z[:, S * b:S * b + S], sm[:, 12 + b:13 + b], None, ALU.mult)
                        r.then_inc(soft_p, 1)

                for n in range(len(UNITS[L]) + 4):
                    for q, e in enumerate(seqs):
                        if e[0] == n:
                            shift(q)
                    for q, e in enumerate(seqs):
                        if e[0] == n - 1:
                            norm(q)
                    if L == 2 and n < 24 and n % 2 == 0:
                        ada(3, n // 2, n // 2 + 1)
                    if n >= 5 and n % 2 == 1:
                        pair = (n - 5) // 2
                        s, h = UNITS[L][2 * pair]
                        copy_tile(T(f"aO{L}.{pair}"), u[:, s, h // 2], S)

            def second(L):
                streams = 2 if L == 2 else 1
                if L == 2:
                    step(ts(tiny[:, 8:9], C("swa_gq"), 0.125, None, ALU.mult))
                rms(L, 0, 2, f"rms{L}a")
                if L == 2:
                    head_norms(2)
                    for i in range(1, 8, 2):
                        copy_tile(T("kpad", i), kpad[:, i], 512)
                    for i in range(0, 8, 2):
                        is_filled(dve, T("kpad", i))
                else:
                    head_norms(3)
                attention(L)
                add_second(L, [T(f"out{L}.{k // 4}", k % 4) for k in range(8)], 16, streams)
                if L == 2:
                    ada_sums(3, "a")
                    ada_sums(3, "b")
                rms(L, 1, streams, f"rms{L}b")
                for n in range(FFT):
                    t = T(f"gu{L}.{(n + FFT) // 4}", (n + FFT) % 4)
                    is_moved(dve, T(f"gu{L}.{n // 4}", n % 4))
                    is_filled(dve, t)
                    v = hidden[:, n, 0:streams]
                    tt(v, v, B(t)[:, 0:S * streams].rearrange("p (s t) -> p s t", s=streams), ALU.mult)\
                        .then_inc(moved[t % 8], 1)
                add_second(L, [T(f"down{L}", k) for k in range(8)], 40, streams)

            even()
            experts(0)
            odd()
            experts(1)
            second(2)
            second(3)

        @block.gpsimd
        def _(pool):
            def route_weights(l):
                if l:
                    is_filled(pool, T("route0"))
                v = wroute[:, :].rearrange("p (k n) -> p k n", n=36)
                pool.dma_start(v[:, :, 0:4], a["moe_w_group"][l].rearrange("(k p) n -> p k n", p=P)).then_inc(wroute_in, 16)
                pool.dma_start(v[:, :, 4:36], a["moe_w_router"][l].rearrange("(k p) n -> p k n", p=P))\
                    .then_inc(wroute_in, 16)

            route_weights(0)
            route_weights(1)
            pool.wait_ge(res_ready, 3)
            pool.dma_start(res[:, 1], a["ctx"]).then_inc(second_in, 16)
            pool.wait_ge(res_ready, 4)
            pool.dma_start(rope, a["rope"]).then_inc(rope_in, 16)
            is_filled(pool, IT(5, 3))
            rpb = a["na_rpb"]
            for h in range(HQ):
                if h >= 4:
                    pool.wait_ge(soft_z, SB0[3] + 2 * (h - 4) + 2)
                for b in range(2):
                    src = bass.AP(rpb.tensor, h * 465 + (5 - b) * 31 + 15, [[HQ * 465 - 1, 64], [31, 6], [1, 64]])
                    pool.dma_start(btab[64 * b:64 * b + 64, h % 4], src).then_inc(bias_in[h % 4], 16)


_INS = ["w_ada", "w_ada_2", "even_w_in", "even_w_out", "odd_w_in", "odd_w_out", "moe_w_group", "moe_w_router",
        "moe_w1", "moe_w3", "moe_w2", "w_gate_up_2", "w_down_2", "swa_w_qkv_2", "swa_w_o_2", "na_w_qkv_2", "na_w_o_2"]


def lay_out(inputs):
    g = {k: np.asarray(v) for k, v in inputs.items()}

    def col(v):
        v = v.reshape(-1, P)
        return np.ascontiguousarray(v.T)

    def rows(v):
        return np.broadcast_to(v.reshape(1, -1), (P, v.size))

    def tall(v):
        return np.concatenate([v.reshape(-1, 1), np.zeros((P - v.size, 1), v.dtype)])

    def twice(v):
        return np.concatenate([v.reshape(-1, 1)] * 2)

    parts = [col(g["c"]), col(g["c_2"]), col(g["c_ctx_2"]), col(g["ln1_g"]), col(g["ln1_b"]), col(g["ln2_g"]),
             col(g["ln2_b"]), col(g["b_ada"]), col(g["b_ada_2"]), col(g["ret_gn_g"]), col(g["diff_subln_g"]),
             col(g["g_mix_2"]), col(g["g_ffn_2"]), twice(g["swa_g_q_2"]), twice(g["swa_g_k_2"]),
             twice(g["na_g_q_2"]), twice(g["na_g_k_2"]), rows(g["swa_sink_2"]),
             tall(g["lambda_q1"]), tall(g["lambda_q2"]), tall(g["lambda_k1"]), tall(g["lambda_k2"])]
    for l in range(2):
        parts += [rows(g["moe_b_group"][l]), rows(g["moe_b_router"][l])]
    const, first, rope = shape_constants()
    arrays = {"cols": np.ascontiguousarray(np.concatenate(parts, 1)), "const": const, "first": first, "rope": rope}
    for name, key in (("x", "x"), ("ctx", "ctx_2")):
        arrays[name] = np.ascontiguousarray(g[key][0].T.reshape(KT, P, S).transpose(1, 0, 2))
    for name in _INS:
        arrays[name] = np.ascontiguousarray(g[name])
    arrays["na_rpb"] = np.ascontiguousarray(np.broadcast_to(g["na_rpb_2"].reshape(1, -1), (GRID_W, HQ * 465)))
    return arrays


def kernel(**inputs):
    import concourse.bacc as bacc
    from concourse.bass_utils import run_bass_kernel_spmd

    nc = bacc.Bacc("TRN2", target_bir_lowering=False, num_devices=1, dynamic_dma_scratch_size=8192)
    arrays = {f"in_{k}": v for k, v in lay_out(inputs).items()}
    aps = {k[3:]: nc.dram_tensor(k, v.shape, mybir.dt.from_np(v.dtype), kind="ExternalInput").ap()
           for k, v in arrays.items()}
    out = nc.dram_tensor("out_x", (P, KT, S), F32, kind="ExternalOutput").ap()
    build(nc, aps, out)
    r = run_bass_kernel_spmd(nc, [arrays], core_ids=[0])
    got = r.results[0]["out_x"]
    return np.ascontiguousarray(got.transpose(1, 0, 2).reshape(D, S).T)[None]
```
